# Optimizing a Trainium2 kernel written in Bass

```python
import math
import jax, jax.numpy as jnp
from jax import lax
import numpy as np

D_MODEL = 1024
BATCH = 1
SEQ = 256
DEPTH = 1

N_META = 16
DN_HEADS = 4
DN_HEAD_DIM = 128
DN_WIDTH = DN_HEADS * DN_HEAD_DIM
DN_CONV = 4
DN_CHUNK = 64
SB_HEADS = 8
SB_HEAD_DIM = 64
SB_WIDTH = SB_HEADS * SB_HEAD_DIM
SB_BLOCK = 128
N_BRANCH = 2
IN_COLS = 4 * DN_WIDTH + 2 * DN_HEADS + 3 * SB_WIDTH + N_BRANCH * D_MODEL
SPLIT_POINTS = [3 * DN_WIDTH, 4 * DN_WIDTH, 4 * DN_WIDTH + DN_HEADS, 4 * DN_WIDTH + 2 * DN_HEADS,
                4 * DN_WIDTH + 2 * DN_HEADS + 3 * SB_WIDTH]
COL_DN_V0 = 2 * DN_WIDTH
COL_SB_V0 = 4 * DN_WIDTH + 2 * DN_HEADS + 2 * SB_WIDTH
N_GROUPS = 4
EXPERTS_PER_GROUP = 8
TOP_K_IN_GROUP = 2
EXPERT_FF = 256
DEEPNORM_ALPHA = (2.0 * DEPTH) ** 0.25
DEEPNORM_BETA = (8.0 * DEPTH) ** -0.25
LN_EPS = 1e-5
RMS_EPS = 1e-6


def layer_norm(x, g, b):
    xf = x.astype(jnp.float32)
    mu = jnp.mean(xf, -1, keepdims=True)
    var = jnp.mean(jnp.square(xf - mu), -1, keepdims=True)
    return ((xf - mu) * lax.rsqrt(var + LN_EPS) * g.astype(jnp.float32) + b.astype(jnp.float32)).astype(x.dtype)

def rms_norm(x, g):
    xf = x.astype(jnp.float32)
    return xf * lax.rsqrt(jnp.mean(xf * xf, -1, keepdims=True) + RMS_EPS) * g.astype(jnp.float32)

def l2_normalize(x):
    xf = x.astype(jnp.float32)
    return xf * lax.rsqrt(jnp.sum(xf * xf, -1, keepdims=True) + RMS_EPS)

def split_heads(t, n):
    b, l, _ = t.shape
    return t.reshape(b, l, n, -1).transpose(0, 2, 1, 3)

def merge_heads(t):
    b, h, l, d = t.shape
    return t.transpose(0, 2, 1, 3).reshape(b, l, h * d)

def causal_depthwise_conv(x, w):
    c = x.shape[-1]
    return lax.conv_general_dilated(x, w[:, None, :], window_strides=(1,), padding=[(w.shape[0] - 1, 0)],
                                    dimension_numbers=("NWC", "WIO", "NWC"), feature_group_count=c)

def gated_delta_rule_chunked(q, k, v, beta, g):
    b, h, l, dk = q.shape
    dv = v.shape[-1]
    c = DN_CHUNK
    n = l // c
    q = q.reshape(b, h, n, c, dk)
    k = k.reshape(b, h, n, c, dk)
    v = v.reshape(b, h, n, c, dv)
    beta = beta.reshape(b, h, n, c)
    decay = jnp.cumsum(g.reshape(b, h, n, c), axis=-1)
    idx = jnp.arange(c)
    causal = idx[:, None] >= idx[None, :]
    strict = idx[:, None] > idx[None, :]
    diff = decay[..., :, None] - decay[..., None, :]
    lmask = jnp.where(causal, jnp.exp(jnp.where(causal, diff, 0.0)), 0.0)
    k_beta = k * beta[..., None]
    v_beta = v * beta[..., None]
    a = jnp.where(strict, jnp.einsum("bhnid,bhnjd->bhnij", k_beta, k) * lmask, 0.0)
    m = a + jnp.eye(c, dtype=a.dtype)
    u = lax.linalg.triangular_solve(m, v_beta, left_side=True, lower=True, unit_diagonal=True)
    w = lax.linalg.triangular_solve(m, k_beta * jnp.exp(decay)[..., None], left_side=True, lower=True,
                                    unit_diagonal=True)
    qk = jnp.where(causal, jnp.einsum("bhnid,bhnjd->bhnij", q, k) * lmask, 0.0)
    q_dec = q * jnp.exp(decay)[..., None]
    k_dec = k * jnp.exp(decay[..., -1:] - decay)[..., None]
    chunk_decay = jnp.exp(decay[..., -1])
    xs = tuple(jnp.moveaxis(t, 2, 0) for t in (q_dec, k_dec, u, w, qk, chunk_decay))

    def step(state, inp):
        qd, kd, uc, wc, qkc, cd = inp
        v_new = uc - jnp.einsum("bhcd,bhde->bhce", wc, state)
        o = jnp.einsum("bhcd,bhde->bhce", qd, state) + jnp.einsum("bhij,bhje->bhie", qkc, v_new)
        state = state * cd[..., None, None] + jnp.einsum("bhcd,bhce->bhde", kd, v_new)
        return state, o

    s0 = jnp.zeros((b, h, dk, dv), jnp.float32)
    _, o = lax.scan(step, s0, xs)
    return jnp.moveaxis(o, 0, 2).reshape(b, h, l, dv)

def stick_breaking_attention(q, k, v):
    l = q.shape[2]
    scale = q.shape[-1] ** -0.5
    bounds = [0] + list(range(N_META, l, SB_BLOCK)) + [l]
    outs = []
    for s0, s1 in zip(bounds[:-1], bounds[1:]):
        z = jnp.einsum("bhqd,bhkd->bhqk", q[:, :, s0:s1], k[:, :, :s1]).astype(jnp.float32) * scale
        mask = jnp.arange(s1)[None, :] < jnp.arange(s0, s1)[:, None]
        log_keep = jnp.where(mask, jax.nn.log_sigmoid(-z), 0.0)
        later = lax.cumsum(log_keep, axis=3, reverse=True) - log_keep
        weights = jnp.where(mask, jnp.exp(jax.nn.log_sigmoid(z) + later), 0.0)
        outs.append(jnp.einsum("bhqk,bhkd->bhqd", weights.astype(v.dtype), v[:, :, :s1]))
    return jnp.concatenate(outs, axis=2)

def hybrid_mixer(x, w_in, b_gate, dn_conv_w, dn_a_log, dn_dt_bias, dn_norm_g, w_branch_dn, w_branch_sb, w_out):
    b, l, d = x.shape
    proj = x @ w_in
    dn_qkv, dn_z, dn_b, dn_a, sb_qkv, gates = jnp.split(proj, SPLIT_POINTS, axis=-1)
    dn_qkv = jax.nn.silu(causal_depthwise_conv(dn_qkv, dn_conv_w))
    q, k, v = jnp.split(dn_qkv, 3, axis=-1)
    q = l2_normalize(split_heads(q, DN_HEADS)) * (DN_HEAD_DIM ** -0.5)
    k = l2_normalize(split_heads(k, DN_HEADS))
    v = split_heads(v, DN_HEADS).astype(jnp.float32)
    beta = jax.nn.sigmoid(dn_b.astype(jnp.float32)).transpose(0, 2, 1)
    g = (-jnp.exp(dn_a_log.astype(jnp.float32))
         * jax.nn.softplus(dn_a.astype(jnp.float32) + dn_dt_bias.astype(jnp.float32))).transpose(0, 2, 1)
    pad = (DN_CHUNK - N_META % DN_CHUNK) % DN_CHUNK
    front = lambda t: jnp.pad(t, [(0, 0), (0, 0), (pad, 0)] + [(0, 0)] * (t.ndim - 3))
    o_dn = gated_delta_rule_chunked(front(q), front(k), front(v), front(beta), front(g))[:, :, pad:]
    o_dn = merge_heads(rms_norm(o_dn, dn_norm_g)) * jax.nn.silu(dn_z.astype(jnp.float32))
    sq, sk, sv = (split_heads(t, SB_HEADS) for t in jnp.split(sb_qkv, 3, axis=-1))
    o_sb = merge_heads(stick_breaking_attention(sq, sk, sv))
    gate = jax.nn.sigmoid(gates.reshape(b, l, N_BRANCH, d) + b_gate)
    merged = (gate[:, :, 0] * (o_dn.astype(x.dtype) @ w_branch_dn)
              + gate[:, :, 1] * (o_sb.astype(x.dtype) @ w_branch_sb))
    return merged @ w_out

def hierarchical_moe(h, router_group_w, router_group_b, router_expert_w, router_expert_b,
                     expert_w_gate, expert_w_up, expert_w_down):
    b, l, d = h.shape
    t = h.reshape(b * l, d)
    group_probs = jax.nn.softmax((t @ router_group_w).astype(jnp.float32) + router_group_b, axis=-1)
    g_idx = jnp.argmax(group_probs, axis=-1)
    g_prob = jnp.max(group_probs, axis=-1)
    exp_logits = jnp.einsum("td,gde->tge", t, router_expert_w).astype(jnp.float32) + router_expert_b
    sel_logits = jnp.take_along_axis(exp_logits, g_idx[:, None, None], axis=1)[:, 0]
    top_logit, top_idx = lax.top_k(sel_logits, TOP_K_IN_GROUP)
    top_w = jax.nn.softmax(top_logit, axis=-1) * g_prob[:, None]
    combine_e = jnp.sum(jax.nn.one_hot(top_idx, EXPERTS_PER_GROUP) * top_w[..., None], axis=1)
    combine = jax.nn.one_hot(g_idx, N_GROUPS)[:, :, None] * combine_e[:, None, :]
    y = jnp.zeros_like(t)
    for gi in range(N_GROUPS):
        hid = (jax.nn.silu(jnp.einsum("td,edf->tef", t, expert_w_gate[gi]))
               * jnp.einsum("td,edf->tef", t, expert_w_up[gi]))
        hid = hid * combine[:, gi, :, None].astype(hid.dtype)
        y = y + jnp.einsum("tef,efd->td", hid, expert_w_down[gi])
    return y.reshape(b, l, d)

def first_inputs(seed: int = 0) -> dict:
    key = jax.random.key(seed)
    ks = jax.random.split(key, 24)
    f32 = jnp.float32
    nrm = lambda k, shape, scale: jax.random.normal(k, shape, f32) * scale
    col_scale = np.ones((IN_COLS,), np.float32)
    col_scale[COL_DN_V0:COL_DN_V0 + DN_WIDTH] = DEEPNORM_BETA
    col_scale[COL_SB_V0:COL_SB_V0 + SB_WIDTH] = DEEPNORM_BETA
    dt = jnp.exp(jax.random.uniform(ks[6], (DEPTH, DN_HEADS), f32, math.log(1e-3), math.log(1e-1)))
    return {
        "x": nrm(ks[0], (BATCH, SEQ, D_MODEL), 1.0),
        "meta_tokens": nrm(ks[1], (N_META, D_MODEL), 1.0),
        "ln_emb_g": 1.0 + nrm(ks[2], (D_MODEL,), 0.05),
        "ln_emb_b": nrm(ks[3], (D_MODEL,), 0.02),
        "w_in": nrm(ks[4], (DEPTH, D_MODEL, IN_COLS), D_MODEL ** -0.5) * jnp.asarray(col_scale),
        "b_gate": nrm(ks[5], (DEPTH, N_BRANCH, D_MODEL), 0.02),
        "dn_conv_w": nrm(ks[7], (DEPTH, DN_CONV, 3 * DN_WIDTH), DN_CONV ** -0.5),
        "dn_a_log": jnp.log(jax.random.uniform(ks[8], (DEPTH, DN_HEADS), f32, 1.0, 16.0)),
        "dn_dt_bias": jnp.log(jnp.expm1(dt)),
        "dn_norm_g": 1.0 + nrm(ks[9], (DEPTH, DN_HEAD_DIM), 0.05),
        "w_branch_dn": nrm(ks[10], (DEPTH, DN_WIDTH, D_MODEL), DEEPNORM_BETA * DN_WIDTH ** -0.5),
        "w_branch_sb": nrm(ks[11], (DEPTH, SB_WIDTH, D_MODEL), DEEPNORM_BETA * SB_WIDTH ** -0.5),
        "w_out": nrm(ks[12], (DEPTH, D_MODEL, D_MODEL), DEEPNORM_BETA * D_MODEL ** -0.5),
        "ln1_g": 1.0 + nrm(ks[13], (DEPTH, D_MODEL), 0.05),
        "ln1_b": nrm(ks[14], (DEPTH, D_MODEL), 0.02),
        "router_group_w": nrm(ks[15], (DEPTH, D_MODEL, N_GROUPS), D_MODEL ** -0.5),
        "router_group_b": nrm(ks[16], (DEPTH, N_GROUPS), 0.01),
        "router_expert_w": nrm(ks[17], (DEPTH, N_GROUPS, D_MODEL, EXPERTS_PER_GROUP), D_MODEL ** -0.5),
        "router_expert_b": nrm(ks[18], (DEPTH, N_GROUPS, EXPERTS_PER_GROUP), 0.01),
        "expert_w_gate": nrm(ks[19], (DEPTH, N_GROUPS, EXPERTS_PER_GROUP, D_MODEL, EXPERT_FF), D_MODEL ** -0.5),
        "expert_w_up": nrm(ks[20], (DEPTH, N_GROUPS, EXPERTS_PER_GROUP, D_MODEL, EXPERT_FF),
                           DEEPNORM_BETA * D_MODEL ** -0.5),
        "expert_w_down": nrm(ks[21], (DEPTH, N_GROUPS, EXPERTS_PER_GROUP, EXPERT_FF, D_MODEL),
                             DEEPNORM_BETA * EXPERT_FF ** -0.5),
        "ln2_g": 1.0 + nrm(ks[22], (DEPTH, D_MODEL), 0.05),
        "ln2_b": nrm(ks[23], (DEPTH, D_MODEL), 0.02),
    }

def first_block(x, meta_tokens, ln_emb_g, ln_emb_b, w_in, b_gate, dn_conv_w, dn_a_log, dn_dt_bias, dn_norm_g,
              w_branch_dn, w_branch_sb, w_out, ln1_g, ln1_b, router_group_w, router_group_b, router_expert_w,
              router_expert_b, expert_w_gate, expert_w_up, expert_w_down, ln2_g, ln2_b):
    b = x.shape[0]
    meta = jnp.broadcast_to(meta_tokens[None].astype(x.dtype), (b, N_META, x.shape[-1]))
    h = layer_norm(jnp.concatenate([meta, x], axis=1), ln_emb_g, ln_emb_b)
    for i in range(DEPTH):
        mix = hybrid_mixer(h, w_in[i], b_gate[i], dn_conv_w[i], dn_a_log[i], dn_dt_bias[i], dn_norm_g[i],
                           w_branch_dn[i], w_branch_sb[i], w_out[i])
        h = layer_norm(DEEPNORM_ALPHA * h + mix, ln1_g[i], ln1_b[i])
        ffn = hierarchical_moe(h, router_group_w[i], router_group_b[i], router_expert_w[i], router_expert_b[i],
                               expert_w_gate[i], expert_w_up[i], expert_w_down[i])
        h = layer_norm(DEEPNORM_ALPHA * h + ffn, ln2_g[i], ln2_b[i])
    return h[:, N_META:]


DEPTH_2 = 2

N_MIXERS = 3
N_HEADS = 8
HEAD_DIM = D_MODEL // N_HEADS
ROT_DIM = HEAD_DIM // 4
ROPE_THETA = 500000.0
MOBA_BLOCK = 256
MOBA_TOPK = 3
Q_CHUNK = 16
POOL_WINDOWS = (2, 4, 8, 16)
N_POOL_GROUPS = len(POOL_WINDOWS)
POOL_GROUP_DIM = D_MODEL // N_POOL_GROUPS
CONV_WIDTH = 3
D_FF = 4 * D_MODEL
NORM_EPS = 1e-6
NEG_INF = -1e30


def rms_norm_2(x, g):
    xf = x.astype(jnp.float32)
    y = xf * lax.rsqrt(jnp.mean(xf * xf, axis=-1, keepdims=True) + NORM_EPS)
    return (y * g.astype(jnp.float32)).astype(x.dtype)

def rope_tables(positions):
    inv_freq = ROPE_THETA ** (-jnp.arange(0, ROT_DIM, 2, dtype=jnp.float32) / ROT_DIM)
    ang = positions.astype(jnp.float32)[..., None] * inv_freq
    return jnp.cos(ang)[:, None], jnp.sin(ang)[:, None]

def apply_partial_rope(t, cos, sin):
    half = ROT_DIM // 2
    rot = t[..., :ROT_DIM].astype(jnp.float32)
    x1, x2 = rot[..., :half], rot[..., half:]
    rotated = jnp.concatenate([x1 * cos - x2 * sin, x2 * cos + x1 * sin], axis=-1)
    return jnp.concatenate([rotated.astype(t.dtype), t[..., ROT_DIM:]], axis=-1)

def moba_attention(xn, w_qkv, w_o, cos, sin):
    b, s, _ = xn.shape
    qkv = (xn @ w_qkv).reshape(b, s, 3, N_HEADS, HEAD_DIM)
    q, k, v = [jnp.transpose(qkv[:, :, i], (0, 2, 1, 3)) for i in range(3)]
    q = apply_partial_rope(q, cos, sin)
    k = apply_partial_rope(k, cos, sin)

    n_blocks = -(-s // MOBA_BLOCK)
    top_k = min(MOBA_TOPK, n_blocks)
    pad = n_blocks * MOBA_BLOCK - s
    kp = jnp.pad(k, ((0, 0), (0, 0), (0, pad), (0, 0)))
    vp = jnp.pad(v, ((0, 0), (0, 0), (0, pad), (0, 0)))
    kb = kp.reshape(b, N_HEADS, n_blocks, MOBA_BLOCK, HEAD_DIM)
    vb = vp.reshape(b, N_HEADS, n_blocks, MOBA_BLOCK, HEAD_DIM)
    k_mean = jnp.mean(kb.astype(jnp.float32), axis=3)

    scale = 1.0 / math.sqrt(HEAD_DIM)
    bi = jnp.arange(b)[:, None, None, None]
    hi = jnp.arange(N_HEADS)[None, :, None, None]
    blk_ids = jnp.arange(n_blocks)

    def chunk(c):
        start = c * Q_CHUNK
        qc = lax.dynamic_slice_in_dim(q, start, Q_CHUNK, axis=2)
        qpos = start + jnp.arange(Q_CHUNK)
        qblk = start // MOBA_BLOCK
        gate = jnp.einsum('bhqd,bhnd->bhqn', qc.astype(jnp.float32), k_mean)
        gate = jnp.where(blk_ids < qblk, gate, NEG_INF)
        _, sel = lax.top_k(gate, top_k)
        sel_valid = sel < qblk
        k_sel = kb[bi, hi, sel]
        v_sel = vb[bi, hi, sel]
        s_sel = jnp.einsum('bhqd,bhqnkd->bhqnk', qc, k_sel).astype(jnp.float32) * scale
        s_sel = jnp.where(sel_valid[..., None], s_sel, NEG_INF)
        s_sel = s_sel.reshape(b, N_HEADS, Q_CHUNK, top_k * MOBA_BLOCK)
        k_own = lax.dynamic_slice_in_dim(kp, qblk * MOBA_BLOCK, MOBA_BLOCK, axis=2)
        v_own = lax.dynamic_slice_in_dim(vp, qblk * MOBA_BLOCK, MOBA_BLOCK, axis=2)
        s_own = jnp.einsum('bhqd,bhkd->bhqk', qc, k_own).astype(jnp.float32) * scale
        kpos = qblk * MOBA_BLOCK + jnp.arange(MOBA_BLOCK)
        s_own = jnp.where(kpos[None, :] <= qpos[:, None], s_own, NEG_INF)
        p = jax.nn.softmax(jnp.concatenate([s_sel, s_own], axis=-1), axis=-1)
        p_sel = p[..., :top_k * MOBA_BLOCK].reshape(
            b, N_HEADS, Q_CHUNK, top_k, MOBA_BLOCK).astype(v.dtype)
        p_own = p[..., top_k * MOBA_BLOCK:].astype(v.dtype)
        return (jnp.einsum('bhqnk,bhqnkd->bhqd', p_sel, v_sel)
                + jnp.einsum('bhqk,bhkd->bhqd', p_own, v_own))

    outs = lax.map(chunk, jnp.arange(s // Q_CHUNK))
    out = jnp.transpose(outs, (1, 0, 3, 2, 4)).reshape(b, s, D_MODEL)
    return out @ w_o

def pool_mixer(xn, w_groups, ls_scale):
    b, s, _ = xn.shape
    xf = xn.astype(jnp.float32).reshape(b, s, N_POOL_GROUPS, POOL_GROUP_DIM)
    cs = jnp.concatenate([jnp.zeros((b, 1, N_POOL_GROUPS, POOL_GROUP_DIM), jnp.float32),
                          jnp.cumsum(xf, axis=1)], axis=1)
    t = jnp.arange(s)
    pooled = []
    for g, w in enumerate(POOL_WINDOWS):
        c = cs[:, :, g]
        lower = jnp.pad(c[:, :s - w + 1], ((0, 0), (w - 1, 0), (0, 0)))
        count = jnp.minimum(t + 1, w).astype(jnp.float32)[None, :, None]
        pooled.append((c[:, 1:] - lower) / count)
    pooled = jnp.stack(pooled, axis=2) - xf
    y = jnp.einsum('bsgc,gcd->bsgd', pooled.astype(xn.dtype), w_groups)
    return y.reshape(b, s, D_MODEL) * ls_scale

def short_conv_mixer(xn, w_in, conv_w, w_out):
    u = xn @ w_in
    gate_b, gate_c, h = jnp.split(u, 3, axis=-1)
    z = gate_c * h
    zc = lax.conv_general_dilated(
        z, conv_w[:, None, :].astype(z.dtype), window_strides=(1,),
        padding=[(CONV_WIDTH - 1, 0)], dimension_numbers=('NWC', 'WIO', 'NWC'),
        feature_group_count=D_MODEL)
    return (gate_b * zc) @ w_out

def squared_relu_mlp(x, w_up, w_down):
    h = jax.nn.relu(x @ w_up)
    return (h * h) @ w_down

def second_inputs(seed: int = 0) -> dict:
    key = jax.random.key(seed)
    ks = jax.random.split(key, 16)
    n_attn = len(range(0, DEPTH_2, N_MIXERS))
    n_pool = len(range(1, DEPTH_2, N_MIXERS))
    n_conv = len(range(2, DEPTH_2, N_MIXERS))
    f32 = jnp.float32

    def nrm(k, shape, fan_in):
        return jax.random.normal(k, shape, f32) * (fan_in ** -0.5)

    x = jax.random.normal(ks[0], (BATCH, SEQ, D_MODEL), f32)
    positions = jnp.broadcast_to(jnp.arange(SEQ, dtype=jnp.int32), (BATCH, SEQ))
    norm_mix = 1.0 + 0.02 * jax.random.normal(ks[1], (DEPTH_2, D_MODEL), f32)
    norm_mlp = 1.0 + 0.02 * jax.random.normal(ks[2], (DEPTH_2, D_MODEL), f32)
    attn_w_qkv = nrm(ks[3], (n_attn, D_MODEL, 3 * D_MODEL), D_MODEL)
    attn_w_o = nrm(ks[4], (n_attn, D_MODEL, D_MODEL), D_MODEL)
    pool_w = nrm(ks[5], (n_pool, N_POOL_GROUPS, POOL_GROUP_DIM, POOL_GROUP_DIM), POOL_GROUP_DIM)
    pool_scale = 1.0 + 0.1 * jax.random.normal(ks[6], (n_pool, D_MODEL), f32)
    conv_w_in = nrm(ks[7], (n_conv, D_MODEL, 3 * D_MODEL), D_MODEL)
    conv_w = nrm(ks[8], (n_conv, CONV_WIDTH, D_MODEL), CONV_WIDTH)
    conv_w_out = nrm(ks[9], (n_conv, D_MODEL, D_MODEL), D_MODEL)
    mlp_w_up = nrm(ks[10], (DEPTH_2, D_MODEL, D_FF), D_MODEL)
    mlp_w_down = nrm(ks[11], (DEPTH_2, D_FF, D_MODEL), D_FF)
    norm_final = 1.0 + 0.02 * jax.random.normal(ks[12], (D_MODEL,), f32)
    return {"x": x, "positions": positions, "norm_mix": norm_mix, "norm_mlp": norm_mlp,
            "attn_w_qkv": attn_w_qkv, "attn_w_o": attn_w_o,
            "pool_w": pool_w, "pool_scale": pool_scale,
            "conv_w_in": conv_w_in, "conv_w": conv_w, "conv_w_out": conv_w_out,
            "mlp_w_up": mlp_w_up, "mlp_w_down": mlp_w_down, "norm_final": norm_final}

def second_block(x, positions, norm_mix, norm_mlp, attn_w_qkv, attn_w_o, pool_w, pool_scale,
              conv_w_in, conv_w, conv_w_out, mlp_w_up, mlp_w_down, norm_final):
    cos, sin = rope_tables(positions)
    i_attn = i_pool = i_conv = 0
    for i in range(DEPTH_2):
        xn = rms_norm_2(x, norm_mix[i])
        kind = i % N_MIXERS
        if kind == 0:
            y = moba_attention(xn, attn_w_qkv[i_attn], attn_w_o[i_attn], cos, sin)
            i_attn += 1
        elif kind == 1:
            y = pool_mixer(xn, pool_w[i_pool], pool_scale[i_pool])
            i_pool += 1
        else:
            y = short_conv_mixer(xn, conv_w_in[i_conv], conv_w[i_conv], conv_w_out[i_conv])
            i_conv += 1
        x = x + y
        x = x + squared_relu_mlp(rms_norm_2(x, norm_mlp[i]), mlp_w_up[i], mlp_w_down[i])
    return rms_norm_2(x, norm_final)


def setup_inputs(seed=0):
    out = dict(first_inputs(seed))
    for name, value in second_inputs(seed + 1).items():
        if name != "x":
            out[name + "_2"] = value
    return out


def reference(
    x, meta_tokens, ln_emb_g, ln_emb_b, w_in, b_gate, dn_conv_w, dn_a_log, dn_dt_bias,
    dn_norm_g, w_branch_dn, w_branch_sb, w_out, ln1_g, ln1_b, router_group_w, router_group_b,
    router_expert_w, router_expert_b, expert_w_gate, expert_w_up, expert_w_down, ln2_g, ln2_b,
    positions_2, norm_mix_2, norm_mlp_2, attn_w_qkv_2, attn_w_o_2, pool_w_2, pool_scale_2,
    conv_w_in_2, conv_w_2, conv_w_out_2, mlp_w_up_2, mlp_w_down_2, norm_final_2,
):
    x = first_block(
        x, meta_tokens, ln_emb_g, ln_emb_b, w_in, b_gate, dn_conv_w, dn_a_log, dn_dt_bias,
        dn_norm_g, w_branch_dn, w_branch_sb, w_out, ln1_g, ln1_b, router_group_w,
        router_group_b, router_expert_w, router_expert_b, expert_w_gate, expert_w_up,
        expert_w_down, ln2_g, ln2_b,
    )
    return second_block(
        x, positions_2, norm_mix_2, norm_mlp_2, attn_w_qkv_2, attn_w_o_2, pool_w_2,
        pool_scale_2, conv_w_in_2, conv_w_2, conv_w_out_2, mlp_w_up_2, mlp_w_down_2,
        norm_final_2,
    )


_drawn_inputs = setup_inputs


def setup_inputs(seed=0):
    import zlib

    import numpy as np

    out = dict(_drawn_inputs(seed))
    spreads = {}
    factors = {'b_gate': 8.0,
     'dn_norm_g': 7.009,
     'router_group_b': 8.0,
     'router_expert_b': 8.0,
     'norm_mix_2': 4.647,
     'norm_final_2': 22.976,
     'norm_mlp_2': 7.479,
     'pool_scale_2': 8.0}
    for name, (base, spread) in spreads.items():
        noise = np.random.default_rng([zlib.crc32(name.encode()), seed]).standard_normal(out[name].shape)
        drawn = base * np.exp(spread * noise) if base else spread * noise
        out[name] = __import__('jax').numpy.asarray(drawn.astype(out[name].dtype))
    for name, factor in factors.items():
        out[name] = (out[name] * factor).astype(out[name].dtype)
    return out
```

```python
import math

import numpy as np

import concourse.bass as bass
from concourse import mybir

F32 = mybir.dt.float32
I32 = mybir.dt.int32
ALU = mybir.AluOpType
ACT = mybir.ActivationFunctionType
AX = mybir.AxisListType

P = 128
D = 1024
KD = D // P
SEQ = 256
NT = SEQ // P
META = 16
L = META + SEQ
DN_H = 4
DN_W = DN_H * 128
SB_H = 8
SB_D = 64
CONV = 4
COL_Z = 3 * DN_W
COL_BA = COL_Z + DN_W
COL_SB = COL_BA + 2 * DN_H
COL_G = COL_SB + 3 * SB_H * SB_D
NG = 4
NE = 8
FF = 256
ALPHA = 2.0 ** 0.25
LN_EPS = 1e-5
RMS_EPS = 1e-6
AT_H = 8
AT_D = 128
ROT = AT_D // 4
HALF = ROT // 2
THETA = 500000.0
WINDOWS = (2, 4, 8, 16)
NEG = -1e30
NM = NT * DN_H + 1
LEVELS = 7
SLOTS = 4
ROUND = 12582912.0
TWO_PI = (6.28125, round((2 * math.pi - 6.28125) * 2 ** 20) / 2 ** 20)
TWO_PI += (2 * math.pi - sum(TWO_PI),)
UNIT = 4096

SQUARES = ["ident", "upper", "strict", "ones", "lower", "mupper", "mones"] + [f"level{i}" for i in range(LEVELS)] + ["neg", "iota", "rep"]
SMALL = {"hmask": DN_H, "idx4": NG, "desc4": NG, "desc8": NE, "freq": HALF, "eps5": 1, "eps6": 1, "one": 1, "zero": 1}


def const_layout():
    at, out = 0, {}
    for n in SQUARES:
        out[n] = (at, P)
        at += P
    for n, w in SMALL.items():
        out[n] = (at, w)
        at += w
    return out, at


def shape_constants():
    lay, width = const_layout()
    c = np.zeros((P, width), np.float32)
    r, q = np.arange(P)[:, None], np.arange(P)[None, :]
    same = (r // 32 == q // 32) & (r % 32 < META) & (q % 32 < META)
    put = {
        "ident": r == q, "upper": r <= q, "strict": r < q, "ones": r >= 0, "lower": r >= q,
        "mupper": same & (r <= q), "mones": r // 32 == q // 32,
        "neg": np.where(q <= r, 0.0, NEG), "iota": q + 0 * r,
        "rep": (q % 32 == r) & (r < META),
        "hmask": (r // 32 == np.arange(DN_H)[None, :]) & (r % 32 < META),
        "idx4": np.arange(NG)[None, :] + 0 * r, "desc4": NG - np.arange(NG)[None, :] + 0 * r,
        "desc8": NE - np.arange(NE)[None, :] + 0 * r,
        "freq": (np.float32(THETA) ** (-np.arange(0, ROT, 2, dtype=np.float32) / np.float32(ROT)))[None, :] + 0 * r,
        "eps5": LN_EPS + 0 * r, "eps6": RMS_EPS + 0 * r, "one": 1 + 0 * r, "zero": 0 * r,
    }
    for i in range(LEVELS):
        s = 1 << i
        put[f"level{i}"] = ((r // s) % 2 == 1) & (q // s == r // s - 1)
    for n, v in put.items():
        a, w = lay[n]
        c[:, a:a + w] = v
    bands = np.zeros((P, 4, 3, P), np.float32)
    s = np.arange(SEQ)[:, None]
    t = np.arange(SEQ)[None, :]
    for g, w in enumerate(WINDOWS):
        full = np.where((s <= t) & (s > t - w), np.float32(1) / np.minimum(t + 1, w).astype(np.float32), 0) - (s == t)
        bands[:, g, 0], bands[:, g, 1], bands[:, g, 2] = full[:P, :P], full[P:, P:], full[:P, P:]
    return c, bands.astype(np.float32)


def build(nc, t):
    lay, const_w = const_layout()
    mm, tr = nc.tensor.matmul, nc.tensor.transpose
    act = nc.scalar.activation
    tt, ts, stt = nc.vector.tensor_tensor, nc.vector.tensor_scalar, nc.vector.scalar_tensor_tensor

    def sb(name, shape, dt=F32):
        return nc.alloc_sbuf_tensor(name, shape, dt)

    named = {}

    def S(name):
        if name not in named:
            named[name] = nc.alloc_semaphore(name)
        return named[name]

    class Line:
        def __init__(self, eng, name):
            self.eng, self.sem, self.n = eng, S(name), 0

        def __call__(self, ins):
            self.n += 1
            ins.then_inc(self.sem, 1)
            self.eng.wait_ge(self.sem, self.n)

    B = [nc.alloc_psum_tensor(f"bank{i}", [P, 512], F32)[:, :] for i in range(8)]
    ring = sb("ring", [P, SLOTS, UNIT])
    cst = sb("cst", [P, const_w])
    params = sb("params", [P, 4, D])
    X0 = sb("X0", [P, NT, D])
    X1 = sb("X1", [P, 2 * NT, D])
    xmeta = sb("xmeta", [META, D])
    xT = sb("xT", [P, KD, L])
    stats = sb("stats", [P, 3, 2, 6])
    mv = sb("mv", [P, 3, 2])
    small = sb("small", [P, 512])
    arena = sb("arena", [P, 19456])
    taken = {"arena": 0, "small": 0}

    def reg(cols):
        a = taken["arena"]
        taken["arena"] += cols
        assert taken["arena"] <= 19456, taken
        return arena[:, a:a + cols]

    def sm(cols):
        a = taken["small"]
        taken["small"] += cols
        assert taken["small"] <= 512
        return small[:, a:a + cols]

    def C(name, rows=P, cols=None):
        a, w = lay[name]
        return cst[0:rows, a:a + (cols or w)]

    def cube(ap, c):
        return ap.rearrange("p (c i) -> p c i", c=c)

    conv_out = cube(reg(12 * L), 12)
    sbT = cube(reg(8 * L), 8)
    sbv = cube(reg(3 * 512), 3)
    zs = cube(reg(NT * 512), NT)
    phase = taken["arena"]
    raw = cube(reg(12 * (L + 3)), 12)
    sq = cube(reg(8 * L), 8)
    taken["arena"] = phase
    AT, XI, XIT, TM, LM, LB, kdec, vb = [cube(reg(NM * P), NM) for _ in range(8)]
    QKT = cube(reg(8 * P), 8)
    kTm, vTm = reg(P), reg(P)
    gB, bB = AT, XI
    vnew, state = AT[:, 0:4, :], XI[:, 0:4, :]
    rhs, odec = TM[:, 0:4, :], (TM[:, 4:8, :], LB[:, 0:4, :])
    junk = LB[:, 4:8, :]
    used_up = conv_out.rearrange("p c t -> p (c t)")
    odT, osT, osb = [cube(used_up[:, a:a + 1024], 4) for a in (8 * L, 4 * L, 0)]
    osb = cube(used_up[:, 0:1024], NT)
    taken["arena"] = phase
    Z = reg(5120)
    SP = reg(5120)
    Z0, Z1, ZM = cube(Z[:, 0:2048], 8), cube(Z[:, 2048:3072], 8), cube(Z[0:META, 3072:5120], 8)
    SP0, SP1, SPM = cube(SP[:, 0:2048], 8), cube(SP[:, 2048:3072], 8), cube(SP[0:META, 3072:5120], 8)

    wr, rbias = cube(arena[:, 18496:18496 + KD * 36], KD), arena[:, 18784:18820]
    taken["arena"] = 0
    xs = cube(reg(KD * P), KD)
    sel, selT = cube(reg(NT * P), NT), reg(NT * P)
    sg, hid, hT = cube(reg(2 * FF), 2), cube(reg(2 * FF), 2), cube(reg(2 * FF), 2)
    ysb = reg(D)
    comb = reg(NE)
    lg = cube(reg(2 * 36), 2)
    gl, exl = lg[:, :, 0:NG], lg[:, :, NG:36].rearrange("p t (g e) -> p t g e", g=NG)
    two = lambda: reg(2)
    mx, gs, gp, top1, top2, w1, w2, rank, gid, over, pos = [two() for _ in range(11)]
    gd, oh, g4 = [cube(reg(2 * NG), 2) for _ in range(3)]
    sl, sl2, oh1, oh2, e8, cmb = [cube(reg(2 * NE), 2) for _ in range(6)]
    picked = reg(2 * 32).rearrange("p (t g e) -> p t g e", t=2, g=NG)
    rk, ct = reg(3 * NG), reg(NG)
    ovf = reg(2)
    ovi = sb("ovi", [P, 2], I32)

    taken["arena"] = 0
    qk = cube(reg(NT * 2 * D), NT)
    vv = cube(reg(NT * D), NT)
    qkT = cube(reg(16 * SEQ), 16)
    sc_ = cube(reg(AT_H * 3 * P), AT_H)
    pT = cube(reg(AT_H * 3 * P), AT_H)
    rope_t = [pT[:, 0:4, 0:256].rearrange("p (a h) d -> p a (h d)", a=4)[:, a, 0:256].rearrange("p (h d) -> p h d", h=16) for a in range(4)]
    bands = reg(12 * P).rearrange("p (g b t) -> p g b t", g=4, b=3)
    causal = reg(3 * P)
    cosine, sine, ang, turn = [cube(reg(2 * HALF), 2) for _ in range(4)]
    posf = reg(2)
    posi = sb("posi", [P, 2], I32)
    mxs, sums = cube(arena[:, 18820:18836], 2), cube(arena[:, 18836:18852], 2)
    taken["arena"] = 0
    hid2 = reg(2 * 4 * SEQ).rearrange("p (a c t) -> p a c t", a=2, c=4)

    gates = X1[:, :, :].rearrange("p (t b) d -> p t b d", t=NT)
    wba = cube(sm(KD * 8), KD)
    cw = sm(12 * CONV).rearrange("p (j c) -> p j c", j=CONV)
    cwr = sb("cwr", [48, P])
    dng = sb("dng", [P, P])
    alog, dtb = sm(DN_H), sm(DN_H)
    ba = cube(sm(24), 3)
    be, ge, gt, gu = cube(sm(12), 3), cube(sm(12), 3), cube(sm(12), 3), cube(sm(12), 3)
    G, BE, DEC, ED, KF, CD, NBE, DL = [sm(NM) for _ in range(8)]
    lnv, rst = sm(4), sm(4)
    ssq, rsd = sm(8), sm(8)
    ident = C("ident")
    warm = sm(1)

    def rows(w, k0, nk, c0, nc_):
        return w[k0 * P:(k0 + nk) * P, c0:c0 + nc_].rearrange("(k p) n -> p k n", p=P)

    def wide(w, c0, n=512, nk=KD, k0=0):
        h = nk // 2
        return [(i * h * n, h, rows(w, k0 + i * h, h, c0, n)) for i in range(2)]

    units, freed = [], []

    def unit(loads, name, count):
        units.append(loads)
        freed.append((name, count))

    w_in = t["w_in"][0]
    for i, (col, count) in enumerate([(0, 4), (512, 8), (1024, 12), (COL_SB, 16), (COL_SB + 512, 20), (COL_SB + 1024, 23),
                                      (COL_Z, 25)] + [(COL_G + 512 * i, 27 + 2 * i) for i in range(4)]):
        unit(wide(w_in, col), "proj", count)
    unit(wide(t["w_branch_dn"][0], 0, D, 4), "branch", 4)
    unit(wide(t["w_branch_sb"][0], 0, D, 4), "branch", 8)
    unit(wide(t["w_out"][0], 0), "mixed", 2)
    unit(wide(t["w_out"][0], 512), "mixed", 4)
    U_MOE = len(units)
    wg, wu, wd = t["expert_w_gate"][0], t["expert_w_up"][0], t["expert_w_down"][0]
    MOE = ["gu0", "gu1", "gu2", "d0", "gu3", "gu4", "d2", "gu5", "gu6", "d4", "gu7", "d6"]
    NU = len(MOE)

    def expert_loads(g, j):
        e, s_ = int(MOE[j][-1]), (U_MOE + j) % SLOTS
        if MOE[j][0] == "g":
            place = ring[:, s_, :].rearrange("p (k n) -> p k n", k=KD)
            return [(place[:, :, i * FF:(i + 1) * FF], w[bass.ds(g, 1), e].rearrange("a (k p) n -> p (a k) n", p=P)) for i, w in enumerate((wg, wu))]
        place = ring[:, s_, :].rearrange("p (e k n) -> p e k n", e=2, k=2)
        return [(place[:, i], wd[bass.ds(g, 1), e + i].rearrange("a (k p) n -> p (a k) n", p=P)) for i in range(2)]

    def expert_freed(j):
        e = int(MOE[j][-1])
        return ("gu", e + 1) if MOE[j][0] == "g" else ("down", e + 2)

    def expert_landed(eng, s_, name, over_=False):
        j = MOE.index(name)
        u = U_MOE + j
        if over_:
            eng.wait_ge(S(f"over_landed{u % SLOTS}"), 32 * (j // SLOTS + 1))
        else:
            eng.wait_ge(S(f"landed{u % SLOTS}"), s_ * (32 * NU // SLOTS) + 32 * (u // SLOTS + 1))

    for g in range(NG):
        for j in range(NU):
            unit(None, expert_freed(j)[0], NE * g + expert_freed(j)[1])
    U_TWO = len(units)
    for i in range(6):
        unit(wide(t["attn_w_qkv_2"][0], 512 * i), "qkv", 2 * i + 2)
    for i in range(2):
        unit(wide(t["attn_w_o_2"][0], 512 * i), "att_o", 2 * i + 2)
    MLP_ORDER = ["up0", "up1", "down0"] + [f"{n}{2 * j + a}" for j in range(3) for n, a in (("up", 2), ("down", 1), ("up", 3), ("down", 2))] + ["down7"]
    mlp_base = []

    def mlp_units(m):
        mlp_base.append(len(units))
        for name in MLP_ORDER:
            j = int(name[-1])
            if name.startswith("up"):
                unit(wide(t["mlp_w_up_2"][m], 512 * j), "up", 16 * m + 2 * j + 2)
            else:
                unit(wide(t["mlp_w_down_2"][m], 0, D, 4, 4 * j), "mlp_down", 8 * m + j + 1)

    mlp_units(0)
    U_POOL = len(units)
    pool_w = t["pool_w_2"][0].rearrange("g k n -> (g k) n")
    unit(wide(pool_w, 0, FF), "pooled", 4)
    mlp_units(1)

    def slot(u):
        return ring[:, u % SLOTS, :]

    def slab(u, k, n=512):
        return slot(u)[:, k * n:(k + 1) * n]

    def landed(eng, u):
        eng.wait_ge(S(f"landed{u % SLOTS}"), 32 * (u // SLOTS + 1))

    N_DN = 12
    N_FM = 20
    GATE0 = 25
    xblk = lambda i: (META + i * P, P)
    block_cm = nc.Block()
    block = block_cm.__enter__()
    M4, M8 = slice(0, 4), slice(4, 8)
    PARTS = [slice(0, 4), slice(4, 8), slice(8, 9)]
    flat = lambda a: a.rearrange("p c i -> p (c i)")

    def masks(name, n):
        return C(name).unsqueeze(1).broadcast_to([P, n, P])

    @block.sync
    def _(sp):
        def load(u):
            if u >= SLOTS:
                sp.wait_ge(S(freed[u - SLOTS][0]), freed[u - SLOTS][1])
            for a, k, src in units[u]:
                n = src.shape[2]
                sp.dma_start(slot(u)[:, a:a + k * n].rearrange("p (k n) -> p k n", k=k), src).then_inc(S(f"landed{u % SLOTS}"), 16)

        sp.dma_start(xmeta[:, :], t["meta_tokens"]).then_inc(S("meta_in"), 16)
        for i in range(NT):
            sp.dma_start(X0[:, i, :], t["x"][0, i * P:(i + 1) * P, :]).then_inc(S(f"x{i}_in"), 16)
        sp.dma_start(cst[:, :], t["consts"]).then_inc(S("cst_in"), 16)
        sp.dma_start(cwr[:, :], t["dn_conv_w"][0].rearrange("j (c p) -> (j c) p", p=P)).then_inc(S("cw_in"), 16)
        for u in range(2):
            load(u)
        sp.dma_start(wba, w_in[:, COL_BA:COL_BA + 8].rearrange("(k p) n -> p k n", p=P)).then_inc(S("wba_in"), 16)
        for u in range(2, U_MOE):
            load(u)
        def load_expert(g, j, over_=False):
            s_ = (U_MOE + j) % SLOTS
            for place, src in expert_loads(g, j):
                sp.dma_start(place, src).then_inc(S(f"over_landed{s_}" if over_ else f"landed{s_}"), 16)

        def wait_freed(g, j):
            name, count = expert_freed((j - SLOTS) % NU)
            sp.wait_ge(S(name), (g if j >= SLOTS else g - 1) * NE + count)

        for j in range(SLOTS):
            sp.wait_ge(S(freed[U_MOE + j - SLOTS][0]), freed[U_MOE + j - SLOTS][1])
            load_expert(0, j)
        with sp.Fori(0, NG - 1) as g:
            for j in range(SLOTS, NU):
                wait_freed(g, j)
                load_expert(g, j)
            for j in range(SLOTS):
                name, count = expert_freed(j + NU - SLOTS)
                sp.wait_ge(S(name), g * NE + count)
                load_expert(g + 1, j)
        for j in range(SLOTS, NU):
            wait_freed(NG - 1, j)
            load_expert(NG - 1, j)
        sp.wait_ge(S("over_made"), 1)
        flag = sp.value_load(ovi[0:1, 0:1], min_val=0, max_val=1)
        group_ = sp.value_load(ovi[0:1, 1:2], min_val=0, max_val=NG - 1)
        with sp.If(flag):
            for j in range(NU):
                wait_freed(NG, j)
                load_expert(group_, j, True)
            sp.wait_ge(S("down"), NE * (NG + 1))
        for u in range(U_TWO, len(units)):
            load(u)
        for i in range(NT):
            sp.wait_ge(S("xn_made"), 9 + i)
            sp.dma_start(t["out"][0, i * P:(i + 1) * P, :], X1[:, i, :]).then_inc(S("stored"), 16)
        sp.wait_ge(S("stored"), 16 * NT)

    @block.gpsimd
    def _(pool):
        def bcast(dst, src, name):
            pool.dma_start(dst, src.partition_broadcast(P)).then_inc(S(name), 16)

        bcast(params[:, 0, :], t["ln_emb_g"], "emb_in")
        bcast(params[:, 1, :], t["ln_emb_b"], "emb_in")
        nc.gpsimd.memset(raw[:, :, 0:3], 0.0).then_inc(S("raw_pad"), 1)
        bcast(alog, t["dn_a_log"][0], "dn_small_in")
        bcast(dtb, t["dn_dt_bias"][0], "dn_small_in")
        bcast(dng[:, :], t["dn_norm_g"][0], "dn_small_in")
        bcast(params[:, 2:4, :], t["b_gate"][0], "b_gate_in")
        pool.dma_start(wr[:, :, 0:NG], t["router_group_w"][0].rearrange("(k p) n -> p k n", p=P)).then_inc(S("router_in"), 16)
        for g in range(NG):
            pool.dma_start(wr[:, :, NG + NE * g:NG + NE * (g + 1)], t["router_expert_w"][0, g].rearrange("(k p) n -> p k n", p=P)).then_inc(S("router_in"), 16)
        bcast(rbias[:, 0:NG], t["router_group_b"][0], "router_in")
        bcast(rbias[:, NG:36], t["router_expert_b"][0].rearrange("g e -> (g e)"), "router_in")
        for c in range(8):
            pool.wait_ge(S("silu"), c + 1)
            nc.gpsimd.tensor_tensor(sq[:, c, :], conv_out[:, c, :], conv_out[:, c, :], ALU.mult).then_inc(S("squares"), 1)
        line = Line(pool, "pool_line")
        pool.wait_ge(S("silu"), N_DN)
        pool.wait_ge(S("normed"), 8)
        line(nc.gpsimd.memset(kTm, 0.0))
        line(nc.gpsimd.memset(vTm, 0.0))
        for h in range(DN_H):
            nc.gpsimd.tensor_copy(kTm[:, 32 * h:32 * h + META], conv_out[:, 4 + h, 0:META])
            last = nc.gpsimd.tensor_copy(vTm[:, 32 * h:32 * h + META], conv_out[:, 8 + h, 0:META])
        last.then_inc(S("meta_stack"), 1)
        pool.wait_ge(S("row_psum"), 6)
        for c in range(NM):
            nc.gpsimd.tensor_copy(XI[:, c, :], ident)
            last = nc.gpsimd.tensor_copy(XIT[:, c, :], ident)
        last.then_inc(S("inverse_start"), 1)
        for what, name in ((SP, "sp_made"), (Z, "w_made")):
            pool.wait_ge(S(name), 1 if what is SP else 2)
            a0 = cube(what[:, 0:2048], 8)[:, :, 0:P]
            a1 = cube(what[:, 2048:3072], 8)
            nc.gpsimd.tensor_tensor(a0, a0, masks("strict", 8), ALU.mult).then_inc(S("masked"), 1)
            nc.gpsimd.tensor_tensor(a1, a1, masks("strict", 8), ALU.mult).then_inc(S("masked"), 1)
        pool.wait_ge(S("embedded"), 3)
        bcast(params[:, 0, :], t["ln1_g"][0], "ln1_in")
        bcast(params[:, 1, :], t["ln1_b"][0], "ln1_in")
        pool.wait_ge(S("gate_out"), 8)
        bcast(params[:, 2, :], t["ln2_g"][0], "ln2_in")
        bcast(params[:, 3, :], t["ln2_b"][0], "ln2_in")
        for i in range(NT):
            pool.dma_start(posi[:, i:i + 1], t["positions_2"][0, i * P:(i + 1) * P].rearrange("(p a) -> p a", a=1)).then_inc(S("pos_in"), 16)
        pool.wait_ge(S("h1_made"), 2)
        pool.dma_start(bands, t["bands"]).then_inc(S("bands_in"), 16)
        bcast(params[:, 0, :], t["norm_mix_2"][0], "rms0_in")
        bcast(params[:, 1, :], t["norm_mlp_2"][0], "rms1_in")
        nc.gpsimd.tensor_copy(causal[:, 0:P], C("neg"))
        nc.gpsimd.memset(causal[:, P:2 * P], 0.0)
        nc.gpsimd.tensor_copy(causal[:, 2 * P:3 * P], C("neg")).then_inc(S("causal_made"), 1)
        pool.wait_ge(S("h2_made"), 2)
        bcast(params[:, 2, :], t["norm_mix_2"][1], "rms2_in")
        bcast(params[:, 3, :], t["norm_mlp_2"][1], "rms3_in")
        pool.wait_ge(S("xn_made"), 2)
        bcast(params[:, 0, :], t["pool_scale_2"][0], "scale_in")
        pool.wait_ge(S("xn_made"), 4)
        bcast(params[:, 1, :], t["norm_final_2"], "rms4_in")

    @block.tensor
    def _(pe):
        def transposes(call, tiles, made=None):
            if made:
                name, count = made if isinstance(made, tuple) else (made, 2)
                pe.wait_ge(S(name), count)
            for k in range(KD):
                if k >= 2 or call > 0:
                    pe.wait_ge(S("xT_act" if k % 2 == 0 else "xT_dve"), (KD // 2) * call + k // 2)
                for src, r, col in tiles:
                    last = tr(B[6 + k % 2][:, col:col + r], src[:, k * P:(k + 1) * P], ident[0:r, 0:r])
                last.then_inc(S("xT_psum"), 1)

        def xT_ready(call):
            pe.wait_ge(S("xT_act"), (KD // 2) * (call + 1))
            pe.wait_ge(S("xT_dve"), (KD // 2) * (call + 1))

        pe.wait_ge(S("cst_in"), 16)
        pe.wait_ge(S("embedded"), 3)
        transposes(0, [(xmeta[:, :], META, 0), (X0[:, 0, :], P, META), (X0[:, 1, :], P, META + P)])
        pe.wait_ge(S("cw_in"), 16)
        tr(B[5][:, 0:48], cwr[:, :], ident[0:48, 0:48]).then_inc(S("ba_psum"), 1)
        xT_ready(0)
        group = [0]

        def bank_free(n):
            if 4 <= n < GATE0 + 4:
                pe.wait_ge(S("proj_out"), n - 3)
            elif n >= GATE0 + 4:
                pe.wait_ge(S("gate_out"), n - 3 - GATE0)

        def features(u):
            landed(pe, u)
            for c in range(4):
                n = group[0]
                bank_free(n)
                for k in range(KD):
                    last = mm(B[n % 4][:, 0:L], slab(u, k)[:, c * P:(c + 1) * P], xT[:, k, :], start=(k == 0), stop=(k == KD - 1))
                last.then_inc(S("proj"), 1)
                group[0] += 1

        def tokens(u, tiles):
            landed(pe, u)
            for a, r in tiles:
                n = group[0]
                bank_free(n)
                for k in range(KD):
                    last = mm(B[n % 4][0:r, :], xT[:, k, a:a + r], slab(u, k), start=(k == 0), stop=(k == KD - 1))
                last.then_inc(S("proj"), 1)
                group[0] += 1

        for u in range(3):
            features(u)
        pe.wait_ge(S("wba_in"), 16)
        for i, (a, r) in enumerate([xblk(0), xblk(1), (0, META)]):
            for k in range(KD):
                last = mm(B[4][0:r, 8 * i:8 * i + 8], xT[:, k, a:a + r], wba[:, k, :], start=(k == 0), stop=(k == KD - 1))
        last.then_inc(S("ba_psum"), 1)
        pe.wait_ge(S("ba_meta"), 1)
        mm(B[4][:, 32:40], C("rep", META), ba[0:META, 2, :], start=True, stop=True).then_inc(S("ba_psum"), 1)
        for u in (3, 4):
            features(u)
        for c in range(8):
            pe.wait_ge(S("squares"), c + 1)
            pe.wait_ge(S("proj_out"), N_FM if c < 4 else N_FM)
            if c >= 4:
                pe.wait_ge(S("ssq_ln"), c - 3)
            mm(B[c % 4][:, 0:L], C("ones"), sq[:, c, :], start=True, stop=True).then_inc(S("ssq_psum"), 1)
        pe.wait_ge(S("g_made"), 1)
        pe.wait_ge(S("cw_out"), 1)
        mm(B[5][:, 0:8], C("upper"), G[:, 0:8], start=True, stop=True)
        mm(B[5][:, 8:9], C("mupper"), G[:, 8:9], start=True, stop=True)
        mm(B[5][:, 16:24], C("ones"), G[:, 0:8], start=True, stop=True)
        mm(B[5][:, 24:25], C("mones"), G[:, 8:9], start=True, stop=True).then_inc(S("dec_psum"), 1)
        pe.wait_ge(S("rows_made"), 1)
        pe.wait_ge(S("ba_out"), 2)
        for i, part in enumerate(PARTS):
            rhs_ = C("upper") if i < 2 else C("mupper")
            dst = B[4] if i == 0 else B[6] if i == 1 else B[7]
            for j, c in enumerate(range(part.start, part.stop)):
                last = mm(dst[:, j * P:(j + 1) * P], gB[:, c, :], rhs_, start=True, stop=True)
            last.then_inc(S("row_psum"), 1)
        for i, part in enumerate(PARTS):
            dst = (B[4], B[6], B[7])[i]
            pe.wait_ge(S("decay_rows"), i + 1)
            for j, c in enumerate(range(part.start, part.stop)):
                last = mm(dst[:, j * P:(j + 1) * P], bB[:, c, :], ident, start=True, stop=True)
            last.then_inc(S("row_psum"), 1)
        pe.wait_ge(S("ssq_ln"), 8)
        tokens(5, [xblk(0), xblk(1), (0, META)])
        tokens(6, [xblk(0), xblk(1)])
        pe.wait_ge(S("normed"), 8)
        pe.wait_ge(S("proj_out"), 25)
        for i in range(NT):
            for h in range(DN_H):
                a = META + i * P
                last = tr(B[i][:, h * P:(h + 1) * P], conv_out[:, 4 + h, a:a + P], ident)
            last.then_inc(S("chunk_psum"), 1)
        for i in range(NT):
            for h in range(DN_H):
                a = META + i * P
                last = tr(B[2 + i][:, h * P:(h + 1) * P], conv_out[:, 8 + h, a:a + P], ident)
            last.then_inc(S("chunk_psum"), 1)
        pe.wait_ge(S("meta_stack"), 1)
        tr(B[5][:, 0:P], kTm, ident)
        tr(B[5][:, P:2 * P], vTm, ident).then_inc(S("chunk_psum"), 1)
        pe.wait_ge(S("lb_made"), 3)
        for i in range(NT):
            for h in range(DN_H):
                k_ = conv_out[:, 4 + h, META + i * P:META + (i + 1) * P]
                last = mm((B[4], B[6])[i][:, h * P:(h + 1) * P], k_, k_, start=True, stop=True)
            last.then_inc(S("chunk_psum"), 1)
        mm(B[7][:, 0:P], kTm, kTm, start=True, stop=True).then_inc(S("chunk_psum"), 1)
        for i in range(NT):
            pe.wait_ge(S("chunk_dve"), i + 1)
            for h in range(DN_H):
                a = META + i * P
                last = mm(B[i][:, h * P:(h + 1) * P], conv_out[:, 4 + h, a:a + P], conv_out[:, h, a:a + P], start=True, stop=True)
            last.then_inc(S("chunk_psum"), 1)
        pe.wait_ge(S("chunk_dve"), 8)
        pe.wait_ge(S("chunk_act"), 2)
        for u in range(7, 11):
            tokens(u, [xblk(0), xblk(1)])
        pe.wait_ge(S("chunk_dve"), 6)
        pe.wait_ge(S("chunk_dve"), 3)
        pe.wait_ge(S("chunk_act"), 3)
        pe.wait_ge(S("inverse_start"), 1)
        pe.wait_ge(S("gate_out"), 8)
        for lv in range(LEVELS):
            for i, part in enumerate(PARTS):
                if lv:
                    pe.wait_ge(S("inv_step"), 3 * (lv - 1) + i + 1)
                for j, c in enumerate(range(part.start, part.stop)):
                    last = mm(B[i if i < 2 else 6][:, j * P:(j + 1) * P], AT[:, c, :], XI[:, c, :], start=True, stop=True)
                last.then_inc(S("inv_ax"), 1)
            for i, part in enumerate(PARTS):
                pe.wait_ge(S("inv_masked"), 3 * lv + i + 1)
                for j, c in enumerate(range(part.start, part.stop)):
                    mm((B[2], B[3], B[6][:, P:2 * P])[i][:, j * P:(j + 1) * P], XIT[:, c, :], TM[:, c, :], start=True, stop=True)
                for j, c in enumerate(range(part.start, part.stop)):
                    last = mm((B[4], B[5], B[6][:, 2 * P:3 * P])[i][:, j * P:(j + 1) * P], TM[:, c, :], XIT[:, c, :], start=True, stop=True)
                last.then_inc(S("inv_xax"), 1)
        pe.wait_ge(S("inv_step"), 3 * LEVELS)
        mm(B[0][:, 0:P], XIT[:, 8, :], vb[:, 8, :], start=True, stop=True).then_inc(S("step_psum"), 1)
        pe.wait_ge(S("v_out"), 1)
        for h in range(DN_H):
            last = mm(B[1 + h][:, 0:P], kdec[32 * h:32 * h + 32, 8, :], vnew[32 * h:32 * h + 32, 0, :], start=True, stop=True)
        last.then_inc(S("step_psum"), 1)
        for i in range(NT):
            a = META + i * P
            pe.wait_ge(S("state_first") if i == 0 else S("state_out"), 1)
            for h in range(DN_H):
                last = mm(B[0][:, h * P:(h + 1) * P], conv_out[:, 4 + h, a:a + P], state[:, h, :], start=True, stop=True)
            last.then_inc(S("step_psum"), 1)
            for h in range(DN_H):
                last = mm(B[5][:, h * P:(h + 1) * P], conv_out[:, h, a:a + P], state[:, h, :], start=True, stop=True)
            last.then_inc(S("step_psum"), 1)
            pe.wait_ge(S("rhs_made"), i + 1)
            for h in range(DN_H):
                last = mm(B[1][:, h * P:(h + 1) * P], XIT[:, 4 * i + h, :], rhs[:, h, :], start=True, stop=True)
            last.then_inc(S("step_psum"), 1)
            pe.wait_ge(S("v_out"), i + 2)
            if i < NT - 1:
                for h in range(DN_H):
                    last = mm(B[2][:, h * P:(h + 1) * P], kdec[:, 4 * i + h, :], vnew[:, h, :], start=True, stop=True)
                last.then_inc(S("step_psum"), 1)
            if i:
                pe.wait_ge(S("o_made"), i)
            for h in range(DN_H):
                last = mm(B[7][:, h * P:(h + 1) * P], QKT[:, 4 * i + h, :], vnew[:, h, :], start=True, stop=True)
            last.then_inc(S("step_psum"), 1)
        for i in range(NT):
            pe.wait_ge(S("o_normed"), i + 1)
            for k in range(4):
                last = tr(B[3][:, k * P:(k + 1) * P] if i == 0 else B[4][:, k * P:(k + 1) * P], zs[:, i, k * P:(k + 1) * P], ident)
            last.then_inc(S("mix_psum"), 1)
        def head_qk(h):
            c, r = h // 2, 64 * (h % 2)
            return sbT[r:r + 64, c, META:L], sbT[r:r + 64, 4 + c, :]

        pe.wait_ge(S("od_out"), 2)
        pe.wait_ge(S("o_made"), 2)
        for g in range(4):
            for j in range(2):
                h = 2 * (2 * (g % 2) + j) + g // 2
                q_, k_ = head_qk(h)
                last = mm(B[g][:, j * SEQ:(j + 1) * SEQ], k_[:, META:META + P], q_, start=True, stop=True)
            last.then_inc(S("z_psum"), 1)
        for g in range(2):
            for j in range(4):
                q_, k_ = head_qk(2 * j + g)
                last = mm(B[4 + g][:, j * P:(j + 1) * P], k_[:, META + P:L], q_[:, P:SEQ], start=True, stop=True)
            last.then_inc(S("z_psum"), 1)
        for g in range(4):
            bk = B[(6, 0, 7, 1)[g]]
            if g == 1:
                pe.wait_ge(S("z_out"), 1)
            if g == 3:
                pe.wait_ge(S("z_out"), 2)
            for j in range(2):
                h = 2 * (2 * (g % 2) + j) + g // 2
                q_, k_ = head_qk(h)
                last = mm(bk[0:META, j * SEQ:(j + 1) * SEQ], k_[:, 0:META], q_, start=True, stop=True)
            last.then_inc(S("z_psum"), 1)
        pe.wait_ge(S("sp_made"), 1)
        pe.wait_ge(S("masked"), 2)
        pe.wait_ge(S("zm_out"), 4)
        for g in range(4):
            hs = slice(2 * g, 2 * g + 2)
            pair = cube(B[g], 2)
            mm(B[g], C("lower"), SP0[:, hs, :], start=True, stop=False)
            mm(pair[:, :, P:SEQ], C("ones"), SP1[:, hs, :], start=False, stop=True).then_inc(S("later_psum"), 1)
        for g in range(2):
            mm(B[4 + g], C("lower"), SP1[:, 4 * g:4 * g + 4, :], start=True, stop=True).then_inc(S("later_psum"), 1)
        for g in range(4):
            bk = B[(6, 7, 0, 1)[g]]
            if g >= 2:
                pe.wait_ge(S("later_out"), g - 1)
            hs = slice(2 * g, 2 * g + 2)
            mm(bk[0:META, :], C("lower", META, META), SPM[:, hs, :], start=True, stop=False)
            mm(bk[0:META, :], C("ones", P, META), SP0[:, hs, :], start=False, stop=False)
            mm(cube(bk[0:META, :], 2)[:, :, P:SEQ], C("ones", P, META), SP1[:, hs, :], start=False, stop=True).then_inc(S("later_psum"), 1)
        pe.wait_ge(S("masked"), 4)
        pe.wait_ge(S("w_made"), 3)
        for i in range(NT):
            for h in range(SB_H):
                hh = 4 * (h % 2) + h // 2
                vcol = slice(h * SB_D, (h + 1) * SB_D)
                o = B[2 + i][:, vcol]
                qs = slice(i * P, (i + 1) * P)
                mm(o, ZM[:, hh, qs], sbv[0:META, 2, vcol], start=True, stop=False)
                last = mm(o, Z0[:, hh, qs], sbv[:, 0, vcol], start=False, stop=(i == 0))
                if i:
                    last = mm(o, Z1[:, hh, :], sbv[:, 1, vcol], start=False, stop=True)
            last.then_inc(S("mix_psum"), 1)
        for i in range(NT):
            pe.wait_ge(S("sb_out"), i + 1)
            for k in range(4):
                last = tr(B[4 + i][:, k * P:(k + 1) * P], osb[:, i, k * P:(k + 1) * P], ident)
            last.then_inc(S("mix_psum"), 1)
        n = 0
        for u, src, ready in ((11, odT, "od_out"), (12, osT, "os_out")):
            landed(pe, u)
            pe.wait_ge(S(ready), 2)
            for i in range(NT):
                for half in range(2):
                    bk = B[(0, 1, 2, 3)[n % 4]]
                    if n >= 4:
                        pe.wait_ge(S("branch_out"), n - 3)
                    for k in range(4):
                        last = mm(bk, src[:, k, i * P:(i + 1) * P], slab(u, k, D)[:, half * 512:(half + 1) * 512], start=(k == 0), stop=(k == 3))
                    last.then_inc(S("branch"), 1)
                    n += 1
        pe.wait_ge(S("merged"), 2)
        transposes(1, [(gates[:, 0, 0, :], P, 0), (gates[:, 1, 0, :], P, P)])
        xT_ready(1)
        pe.wait_ge(S("branch_out"), 8)
        n = 0
        for half in range(2):
            landed(pe, 13 + half)
            for i in range(NT):
                for k in range(KD):
                    last = mm(B[n], xT[:, k, i * P:(i + 1) * P], slab(13 + half, k), start=(k == 0), stop=(k == KD - 1))
                last.then_inc(S("mixed"), 1)
                n += 1
        transposes(2, [(X1[:, 0, :], P, 0), (X1[:, 1, :], P, P)], "h1_made")
        xT_ready(2)
        pe.wait_ge(S("router_in"), 16 * (NG + 3))
        for i in range(NT):
            for k in range(KD):
                last = mm(B[0][:, 64 * i:64 * i + 36], xT[:, k, i * P:(i + 1) * P], wr[:, k, :], start=(k == 0), stop=(k == KD - 1))
        last.then_inc(S("router_psum"), 1)
        pe.wait_ge(S("router_dve"), 2)
        mm(B[1][:, 0:NG], C("strict"), oh[:, 0, :], start=True, stop=True)
        mm(B[1][:, NG:2 * NG], C("strict"), oh[:, 1, :], start=True, stop=False)
        mm(B[1][:, NG:2 * NG], C("ones"), oh[:, 0, :], start=False, stop=True)
        mm(B[1][:, 2 * NG:3 * NG], C("ones"), oh[:, 0, :], start=True, stop=False)
        mm(B[1][:, 2 * NG:3 * NG], C("ones"), oh[:, 1, :], start=False, stop=True).then_inc(S("router_psum"), 1)

        def gather(s_):
            pe.wait_ge(S("sel_made"), s_ + 1)
            if not isinstance(s_, int):
                pe.wait_ge(S("selT_out"), s_)
            for k in range(KD):
                for i in range(NT):
                    last = mm(B[5 + k // 4][:, (k % 4) * P:(k % 4 + 1) * P], X1[:, i, k * P:(k + 1) * P], sel[:, i, :], start=(i == 0), stop=(i == NT - 1))
            last.then_inc(S("gather_psum"), 1)
            for i in range(NT):
                mm(B[7][:, 0:NE], sel[:, i, :], cmb[:, i, :], start=(i == 0), stop=(i == NT - 1))
            for i in range(NT):
                last = tr(B[7][:, (i + 1) * P:(i + 2) * P], sel[:, i, :], ident)
            last.then_inc(S("sel_psum"), 1)

        def experts(s_, over_=False):
            pe.wait_ge(S("xs_out"), s_ + 1)
            for e in range(NE + 2):
                if e < NE:
                    expert_landed(pe, s_, f"gu{e}", over_)
                    pe.wait_ge(S("scat_out" if e < 2 else "hid"), s_ * 4 + 1 if e < 2 else s_ * NE + (e - 1))
                    w_ = ring[:, (U_MOE + MOE.index(f"gu{e}")) % SLOTS, :]
                    for k in range(KD):
                        last = mm(B[e % 2], xs[:, k, :], w_[:, k * 512:(k + 1) * 512], start=(k == 0), stop=(k == KD - 1))
                    last.then_inc(S("gu"), 1)
                if e >= 2:
                    d = e - 2
                    name = f"d{d - d % 2}"
                    if d % 2 == 0:
                        expert_landed(pe, s_, name, over_)
                    pe.wait_ge(S("hT_out"), s_ * NE + (d + 1))
                    w_ = ring[:, (U_MOE + MOE.index(name)) % SLOTS, :]
                    for half in range(2):
                        for k in range(2):
                            a = (d % 2) * 2048 + k * D + half * 512
                            last = mm(B[2 + half], hT[:, d % 2, k * P:(k + 1) * P], w_[:, a:a + 512], start=(d == 0 and k == 0), stop=(d == NE - 1 and k == 1))
                    last.then_inc(S("down"), 1)
                if 1 <= e <= NE:
                    h = e - 1
                    pe.wait_ge(S("hid"), s_ * NE + (h + 1))
                    for k in range(2):
                        last = tr(B[4][:, k * P:(k + 1) * P], hid[:, h % 2, k * P:(k + 1) * P], ident)
                    last.then_inc(S("hT_psum"), 1)
                if e == NE - 1 and not over_:
                    gather(s_ + 1)
            pe.wait_ge(S("y_dve"), s_ + 1)
            pe.wait_ge(S("y_act"), s_ + 1)
            pe.wait_ge(S("selT_out"), s_ + 1)
            for q in range(4):
                if q >= 2:
                    pe.wait_ge(S("scat_out"), s_ * 4 + q)
                mm(B[q % 2], selT[:, (q // 2) * P:(q // 2 + 1) * P], ysb[:, (q % 2) * 512:(q % 2 + 1) * 512], start=True, stop=True).then_inc(S("scat"), 1)

        gather(0)
        with pe.Fori(0, NG) as s_:
            experts(s_)
        pe.wait_ge(S("over_made"), 1)
        flag = pe.value_load(ovi[0:1, 0:1], min_val=0, max_val=1)
        with pe.If(flag):
            experts(NG, True)
        def attention():
            transposes(3, [(X1[:, 0, :], P, 0), (X1[:, 1, :], P, P)], "xn_made")
            xT_ready(3)
            for n in range(12):
                u, i = U_TWO + n // 2, n % 2
                if i == 0:
                    landed(pe, u)
                if n >= 4:
                    pe.wait_ge(S("qkv_out"), n - 3)
                for k in range(KD):
                    last = mm(B[n % 4], xT[:, k, i * P:(i + 1) * P], slab(u, k), start=(k == 0), stop=(k == KD - 1))
                last.then_inc(S("qkv"), 1)
            for g in range(8):
                if g == 0:
                    pe.wait_ge(S("rope_made"), 2)
                if g >= 4:
                    pe.wait_ge(S("qkT_act" if g % 2 == 0 else "qkT_dve"), g // 2 - 1)
                for j in range(2):
                    for i in range(NT):
                        last = tr(B[4 + g % 4][:, (2 * j + i) * P:(2 * j + i + 1) * P], qk[:, i, (2 * g + j) * P:(2 * g + j + 1) * P], ident)
                last.then_inc(S("att_psum"), 1)
            pe.wait_ge(S("qkT_act"), 4)
            pe.wait_ge(S("qkT_dve"), 4)
            for h in range(AT_H):
                pe.wait_ge(S("qkv_out"), 12)
                if h >= 4:
                    pe.wait_ge(S("scores_out"), h - 3)
                mm(B[h % 4][:, 0:P], qkT[:, h, 0:P], qkT[:, 8 + h, 0:P], start=True, stop=True)
                mm(B[h % 4][:, P:3 * P], qkT[:, h, P:SEQ], qkT[:, 8 + h, :], start=True, stop=True).then_inc(S("att_psum"), 1)
            for h in range(AT_H):
                pe.wait_ge(S("p_made"), h + 1)
                if h >= 4:
                    pe.wait_ge(S("pT_out"), h - 3)
                for j in range(3):
                    last = tr(B[4 + h % 4][:, j * P:(j + 1) * P], sc_[:, h, j * P:(j + 1) * P], ident)
                last.then_inc(S("att_psum"), 1)
            pe.wait_ge(S("scores_out"), 8)
            for h in range(AT_H):
                pe.wait_ge(S("pT_out"), h + 1)
                o, v = slice((h % 4) * P, (h % 4 + 1) * P), slice(h * P, (h + 1) * P)
                mm(B[h // 4][:, o], pT[:, h, 0:P], vv[:, 0, v], start=True, stop=True)
                mm(B[2 + h // 4][:, o], pT[:, h, P:2 * P], vv[:, 0, v], start=True, stop=False)
                mm(B[2 + h // 4][:, o], pT[:, h, 2 * P:3 * P], vv[:, 1, v], start=False, stop=True).then_inc(S("att_psum"), 1)
            transposes(4, [(qk[:, 0, :], P, 0), (qk[:, 1, :], P, P)], "att_made")
            xT_ready(4)
            for n in range(4):
                half, i = n // 2, n % 2
                u = U_TWO + 6 + half
                if i == 0:
                    landed(pe, u)
                for k in range(KD):
                    last = mm(B[n], xT[:, k, i * P:(i + 1) * P], slab(u, k), start=(k == 0), stop=(k == KD - 1))
                last.then_inc(S("att_o"), 1)

        def mlp(m, call):
            base = mlp_base[m]
            transposes(call, [(X1[:, 0, :], P, 0), (X1[:, 1, :], P, P)], ("xn_made", 4 if m == 0 else 8))
            xT_ready(call)

            def ready(q, jj):
                u = base + q
                pe.wait_ge(S(f"landed{u % SLOTS}"), jj * 32 + 32 * (u // SLOTS + 1))
                return slot(u)

            def up(q, j, jj=0, wait=True):
                w_ = ready(q, jj)
                for pr in range(2):
                    if wait:
                        pe.wait_ge(S("relu"), jj * 4 + (16 * m + 2 * j + pr - 3))
                    for cc in range(2):
                        c = 2 * pr + cc
                        for k in range(KD):
                            last = mm(B[4 + (2 * j + pr) % 4][:, cc * SEQ:(cc + 1) * SEQ], w_[:, k * 512 + c * P:k * 512 + (c + 1) * P], xT[:, k, 0:SEQ],
                                      start=(k == 0), stop=(k == KD - 1))
                    last.then_inc(S("up"), 1)

            def down(q, j, jj=0, first=False, final=False):
                w_ = ready(q, jj)
                pe.wait_ge(S("squared"), jj * 4 + (16 * m + 2 * j + 2))
                for n in range(4):
                    i, half = n // 2, n % 2
                    for c in range(4):
                        last = mm(B[n], hid2[:, j % 2, c, i * P:(i + 1) * P], w_[:, c * D + half * 512:c * D + (half + 1) * 512],
                                  start=(first and c == 0), stop=(final and c == 3))
                last.then_inc(S("mlp_down"), 1)

            up(0, 0, wait=False)
            up(1, 1, wait=False)
            down(2, 0, first=True)
            with pe.Fori(0, 3) as jj:
                up(3, 2, jj)
                down(4, 1, jj)
                up(5, 3, jj)
                down(6, 2, jj)
            down(15, 7, final=True)

        attention()
        pe.wait_ge(S("res"), 2)
        mlp(0, 5)
        pe.wait_ge(S("bands_in"), 16)
        pe.wait_ge(S("xn_made"), 6)
        for c in range(KD):
            g = c // 2
            pe.wait_ge(S("xT_act" if c % 2 == 0 else "xT_dve"), 24 + c // 2)
            if c < 2:
                pe.wait_ge(S("relu"), 16)
            cols = slice(c * P, (c + 1) * P)
            mm(B[6 + c % 2][:, 0:P], X1[:, 0, cols], bands[:, g, 0, :], start=True, stop=True)
            mm(B[6 + c % 2][:, P:SEQ], X1[:, 0, cols], bands[:, g, 2, :], start=True, stop=False)
            mm(B[6 + c % 2][:, P:SEQ], X1[:, 1, cols], bands[:, g, 1, :], start=False, stop=True).then_inc(S("xT_psum"), 1)
        xT_ready(6)
        landed(pe, U_POOL)
        for n in range(4):
            i = n // 2
            for g in (2 * (n % 2), 2 * (n % 2) + 1):
                for k in range(2):
                    last = mm(B[n][:, (g % 2) * FF:(g % 2 + 1) * FF], xT[:, 2 * g + k, i * P:(i + 1) * P], slab(U_POOL, 2 * g + k, FF), start=(k == 0), stop=(k == 1))
            last.then_inc(S("pooled"), 1)
        pe.wait_ge(S("res"), 6)
        mlp(1, 7)

    @block.scalar
    def _(sc):
        line = Line(sc, "act_line")

        def xT_copies(call, width):
            for k in range(0, KD, 2):
                sc.wait_ge(S("xT_psum"), KD * call + k + 1)
                act(xT[:, k, 0:width], B[6][:, 0:width], ACT.Copy).then_inc(S("xT_act"), 1)

        def root(n, cols, out, scale, eps):
            line(act(lnv[:, 0:n], cols, ACT.Ln, scale=scale, bias=eps))
            return act(out, lnv[:, 0:n], ACT.Exp, scale=-0.5)

        sc.wait_ge(S("cst_in"), 16)
        for i in range(3):
            r = META if i == 0 else P
            sc.wait_ge(S("var"), i + 1)
            line(act(lnv[0:r, i:i + 1], mv[0:r, i, 1:2], ACT.Ln, bias=C("eps5", r)))
            act(rst[0:r, i:i + 1], lnv[0:r, i:i + 1], ACT.Exp, scale=-0.5).then_inc(S("rstd"), 1)
        xT_copies(0, L)
        sc.wait_ge(S("raw_pad"), 1)
        for c in range(N_DN):
            sc.wait_ge(S("proj"), c + 1)
            act(raw[:, c, 3:3 + L], B[c % 4][:, 0:L], ACT.Copy).then_inc(S("proj_out"), 1)
            if c >= 2:
                sc.wait_ge(S("conv"), c - 1)
                act(conv_out[:, c - 2, :], conv_out[:, c - 2, :], ACT.Silu).then_inc(S("silu"), 1)
        for c in (N_DN - 2, N_DN - 1):
            sc.wait_ge(S("conv"), c + 1)
            act(conv_out[:, c, :], conv_out[:, c, :], ACT.Silu).then_inc(S("silu"), 1)
        sc.wait_ge(S("ba_out"), 2)
        act(be, ba[:, :, 0:DN_H], ACT.Exp, scale=-1.0).then_inc(S("be_exp"), 1)
        sc.wait_ge(S("ga_abs"), 1)
        line(act(gt, gt, ACT.Exp, scale=-1.0))
        act(gt, gt, ACT.Ln, bias=C("one")).then_inc(S("ga_ln"), 1)
        sc.wait_ge(S("dn_small_in"), 48)
        act(alog, alog, ACT.Exp).then_inc(S("ga_ln"), 1)
        for c in range(8):
            sc.wait_ge(S("proj"), N_DN + c + 1)
            act(sbT[:, c, :], B[(N_DN + c) % 4][:, 0:L], ACT.Copy, scale=(SB_D ** -0.5 if c < 4 else 1.0)).then_inc(S("proj_out"), 1)
        for c in range(8):
            sc.wait_ge(S("ssq_psum"), c + 1)
            act(sq[:, c, :], B[c % 4][:, 0:L], ACT.Ln, bias=C("eps6")).then_inc(S("ssq_ln"), 1)
            sc.wait_ge(S("ssq_ln"), c + 1)
            act(sq[:, c, :], sq[:, c, :], ACT.Exp, scale=-0.5).then_inc(S("rnorm"), 1)
        sc.wait_ge(S("dec_out"), 1)
        act(ED, DEC, ACT.Exp)
        act(KF, KF, ACT.Exp)
        act(CD, DL, ACT.Exp).then_inc(S("dec_exp"), 1)
        for i, part in enumerate(PARTS):
            sc.wait_ge(S("decay_rows"), i + 1)
            act(LM[:, part, :], LM[:, part, :], ACT.Exp).then_inc(S("lm_exp"), 1)
        for n, (dst, r, f) in enumerate([(sbv[:, 0, :], P, ACT.Copy), (sbv[:, 1, :], P, ACT.Copy), (sbv[0:META, 2, :], META, ACT.Copy),
                                         (zs[:, 0, :], P, ACT.Silu), (zs[:, 1, :], P, ACT.Silu)]):
            sc.wait_ge(S("proj"), N_FM + n + 1)
            act(dst, B[(N_FM + n) % 4][0:r, :], f).then_inc(S("proj_out"), 1)
        for i in range(NT):
            sc.wait_ge(S("chunk_psum"), i + 3)
            for h in range(DN_H):
                c = 4 * i + h
                last = act(vb[:, c, :], B[2 + i][:, h * P:(h + 1) * P], ACT.Copy, scale=BE[:, c:c + 1])
            last.then_inc(S("chunk_act"), 1)
        sc.wait_ge(S("chunk_dve"), 3)
        act(vb[:, 8, :], B[5][:, P:2 * P], ACT.Copy, scale=BE[:, 8:9]).then_inc(S("chunk_act"), 1)
        for n in range(8):
            u, i = n // 2, n % 2
            g_ = gates[:, i, u // 2, (u % 2) * 512:(u % 2 + 1) * 512]
            sc.wait_ge(S("gate_out"), n + 1)
            act(g_, g_, ACT.Sigmoid).then_inc(S("gate_sig"), 1)
        sc.wait_ge(S("step_psum"), 1)
        act(vnew[:, 0, :], B[0][:, 0:P], ACT.Copy).then_inc(S("v_out"), 1)
        sc.wait_ge(S("step_psum"), 2)
        for h in range(DN_H):
            last = act(state[:, h, :], B[1 + h][:, 0:P], ACT.Copy)
        last.then_inc(S("state_first"), 1)
        for i in range(NT):
            sc.wait_ge(S("step_psum"), 5 * i + 4)
            for h in range(DN_H):
                c = 4 * i + h
                last = act(odec[i][:, h, :], B[5][:, h * P:(h + 1) * P], ACT.Copy, scale=ED[:, c:c + 1])
            last.then_inc(S("o_decayed"), 1)
            sc.wait_ge(S("step_psum"), 5 * i + 5)
            act(flat(vnew), B[1], ACT.Copy).then_inc(S("v_out"), 1)
        for i in range(NT):
            sc.wait_ge(S("o_made"), i + 1)
            for h in range(DN_H):
                line(act(junk[:, h, :], odec[i][:, h, :], ACT.Square, accum_out=ssq[:, 4 * i + h:4 * i + h + 1]))
            root(4, ssq[:, 4 * i:4 * i + 4], rsd[:, 4 * i:4 * i + 4], 1.0 / 128, C("eps6")).then_inc(S("o_rstd"), 1)
        for i in range(NT):
            sc.wait_ge(S("mix_psum"), i + 1)
            act(odT[:, :, i * P:(i + 1) * P], cube(B[3 + i], 4), ACT.Copy).then_inc(S("od_out"), 1)
        for g in range(4):
            sc.wait_ge(S("z_psum"), g + 7)
            act(ZM[:, 2 * g:2 * g + 2, :], cube(B[(6, 0, 7, 1)[g]][0:META, :], 2), ACT.Copy).then_inc(S("zm_out"), 1)
        sc.wait_ge(S("z_out"), 4)
        sc.wait_ge(S("z_out"), 6)
        sc.wait_ge(S("zm_out"), 4)
        for f, kw in ((ACT.Abs, {}), (ACT.Exp, {"scale": -1.0}), (ACT.Ln, {"bias": None})):
            src, srm = (Z[:, 0:3072], Z[0:META, 3072:5120]) if f is ACT.Abs else (SP[:, 0:3072], SP[0:META, 3072:5120])
            kb = {"bias": C("one")} if "bias" in kw else kw
            km = {"bias": C("one", META)} if "bias" in kw else kw
            line(act(SP[:, 0:3072], src, f, **kb))
            if f is ACT.Ln:
                act(SP[0:META, 3072:5120], srm, f, **km).then_inc(S("sp_ln"), 1)
            else:
                line(act(SP[0:META, 3072:5120], srm, f, **km))
        sc.wait_ge(S("later_out"), 4)
        act(Z[:, 0:2048], Z[:, 0:2048], ACT.Exp).then_inc(S("w_made"), 1)
        sc.wait_ge(S("later_out"), 6)
        act(Z[:, 2048:3072], Z[:, 2048:3072], ACT.Exp).then_inc(S("w_made"), 1)
        sc.wait_ge(S("later_out"), 10)
        act(Z[0:META, 3072:5120], Z[0:META, 3072:5120], ACT.Exp).then_inc(S("w_made"), 1)
        for i in range(NT):
            sc.wait_ge(S("mix_psum"), i + 5)
            act(osT[:, :, i * P:(i + 1) * P], cube(B[4 + i], 4), ACT.Copy).then_inc(S("os_out"), 1)
        xT_copies(1, SEQ)
        def deviation(i, n):
            sc.wait_ge(S("var"), n)
            line(act(lnv[:, i:i + 1], mv[:, i, 1:2], ACT.Ln, bias=C("eps5")))
            act(rst[:, i:i + 1], lnv[:, i:i + 1], ACT.Exp, scale=-0.5).then_inc(S("rstd"), 1)

        deviation(1, 4)
        deviation(2, 5)
        xT_copies(2, SEQ)
        sc.wait_ge(S("router_dve"), 1)
        act(gd, gd, ACT.Exp).then_inc(S("router_act"), 1)
        sc.wait_ge(S("router_dve"), 3)
        act(w2, w2, ACT.Exp).then_inc(S("router_act"), 1)

        def gathered(s_):
            sc.wait_ge(S("gather_psum"), s_ + 1)
            act(flat(xs[:, 0:4, :]), B[5], ACT.Copy)
            act(flat(xs[:, 4:8, :]), B[6], ACT.Copy).then_inc(S("xs_out"), 1)

        def experts(s_, over_=False):
            for e in range(NE + 1):
                if e < NE:
                    sc.wait_ge(S("gu"), s_ * NE + (e + 1))
                    if e >= 2:
                        sc.wait_ge(S("hid"), s_ * NE + (e - 1))
                    act(sg[:, e % 2, :], B[e % 2][:, 0:FF], ACT.Silu).then_inc(S("sg_made"), 1)
                if e == NE and not over_:
                    gathered(s_ + 1)
                if e >= 1:
                    h = e - 1
                    sc.wait_ge(S("hT_psum"), s_ * NE + (h + 1))
                    if h >= 2:
                        sc.wait_ge(S("down"), s_ * NE + (h - 1))
                    act(hT[:, h % 2, :], B[4][:, 0:FF], ACT.Copy).then_inc(S("hT_out"), 1)
            sc.wait_ge(S("down"), s_ * NE + NE)
            act(ysb[:, 512:1024], B[3], ACT.Copy).then_inc(S("y_act"), 1)

        gathered(0)
        with sc.Fori(0, NG) as s_:
            experts(s_)
        sc.wait_ge(S("over_made"), 1)
        flag = sc.value_load(ovi[0:1, 0:1], min_val=0, max_val=1)
        with sc.If(flag):
            experts(NG, True)
        deviation(1, 6)
        deviation(2, 7)
        def mean_square(r, ready, count):
            for i in range(NT):
                sc.wait_ge(S(ready), count + i + 1)
                line(act(X1[:, i, :], X0[:, i, :], ACT.Square, accum_out=ssq[:, i:i + 1]))
                root(1, ssq[:, i:i + 1], rsd[:, i:i + 1], 1.0 / D, C("eps6")).then_inc(S("rms"), 1)

        sc.wait_ge(S("turned"), 1)
        act(sine, sine, ACT.Sin)
        act(cosine, cosine, ACT.Sin).then_inc(S("sines"), 1)
        mean_square(0, "h2_made", 0)
        xT_copies(3, SEQ)
        for n in range(12):
            u, i = n // 2, n % 2
            sc.wait_ge(S("qkv"), n + 1)
            dst = qk[:, i, u * 512:(u + 1) * 512] if u < 4 else vv[:, i, (u - 4) * 512:(u - 3) * 512]
            act(dst, B[n % 4], ACT.Copy).then_inc(S("qkv_out"), 1)
        for g in range(0, 8, 2):
            sc.wait_ge(S("att_psum"), g + 1)
            act(flat(qkT[:, 2 * g:2 * g + 2, :]), B[4 + g % 4], ACT.Copy).then_inc(S("qkT_act"), 1)
        for h in range(AT_H):
            sc.wait_ge(S("max_made"), h // 4 + 1)
            act(sc_[:, h, 0:P], sc_[:, h, 0:P], ACT.Exp, bias=mxs[:, 0, h:h + 1], accum_out=sums[:, 0, h:h + 1])
            act(sc_[:, h, P:3 * P], sc_[:, h, P:3 * P], ACT.Exp, bias=mxs[:, 1, h:h + 1], accum_out=sums[:, 1, h:h + 1]).then_inc(S("p_made"), 1)
        xT_copies(4, SEQ)

        def mlp(m, call):
            xT_copies(call, SEQ)

            def relu(j, jj=0, wait=True):
                for pr in range(2):
                    n = 16 * m + 2 * j + pr
                    sc.wait_ge(S("up"), jj * 4 + (n + 1))
                    if wait and pr == 0:
                        sc.wait_ge(S("mlp_down"), jj * 2 + (8 * m + j - 1))
                    act(hid2[:, j % 2, 2 * pr:2 * pr + 2, :].rearrange("p c t -> p (c t)"), B[4 + (2 * j + pr) % 4], ACT.Relu).then_inc(S("relu"), 1)

            relu(0, wait=False)
            relu(1, wait=False)
            with sc.Fori(0, 3) as jj:
                relu(2, jj)
                relu(3, jj)

        mean_square(1, "res", 0)
        mlp(0, 5)
        mean_square(2, "res", 2)
        for k in range(0, KD, 2):
            sc.wait_ge(S("xT_psum"), KD * 6 + k + 1)
            act(xT[:, k, 0:SEQ], B[6][:, 0:SEQ], ACT.Copy).then_inc(S("xT_act"), 1)
        mean_square(3, "res", 4)
        mlp(1, 7)
        mean_square(4, "res", 6)

    @block.vector
    def _(dve):
        line = Line(dve, "dve_line")

        def xT_copies(call, width):
            for k in range(1, KD, 2):
                dve.wait_ge(S("xT_psum"), KD * call + k + 1)
                nc.vector.tensor_copy(xT[:, k, 0:width], B[7][:, 0:width]).then_inc(S("xT_dve"), 1)

        def moments(i, x, r):
            for j in range(2):
                line(nc.vector.bn_stats(stats[0:r, i, j, :], x[:, j * 512:(j + 1) * 512]))
            nc.vector.bn_aggr(mv[0:r, i, :], stats[0:r, i, :, :].rearrange("p a b -> p (a b)")).then_inc(S("var"), 1)

        def normalize(x, out, i, r, g, b):
            line(ts(out, x, mv[0:r, i, 0:1], rst[0:r, i:i + 1], ALU.subtract, ALU.mult))
            line(tt(out, out, params[0:r, g, :], ALU.mult))
            return tt(out, out, params[0:r, b, :], ALU.add)

        tiles = [(xmeta[:, :], META, "meta_in"), (X0[:, 0, :], P, "x0_in"), (X0[:, 1, :], P, "x1_in")]
        for i, (x, r, sem) in enumerate(tiles):
            dve.wait_ge(S(sem), 16)
            moments(i, x, r)
        dve.wait_ge(S("emb_in"), 32)
        for i, (x, r, sem) in enumerate(tiles):
            dve.wait_ge(S("rstd"), i + 1)
            normalize(x, x, i, r, 0, 1).then_inc(S("embedded"), 1)
        xT_copies(0, L)
        dve.wait_ge(S("ba_psum"), 1)
        nc.vector.tensor_copy(cw.rearrange("p j c -> p (j c)"), B[5][:, 0:48]).then_inc(S("cw_out"), 1)
        dve.wait_ge(S("cw_out"), 1)
        for c in range(N_DN):
            dve.wait_ge(S("proj_out"), c + 1)
            line(ts(conv_out[:, c, :], raw[:, c, 0:L], cw[:, 0, c:c + 1], None, ALU.mult))
            for j in range(1, CONV):
                ins = stt(conv_out[:, c, :], raw[:, c, j:j + L], cw[:, j, c:c + 1], conv_out[:, c, :], ALU.mult, ALU.add)
                if j < CONV - 1:
                    line(ins)
            ins.then_inc(S("conv"), 1)
        dve.wait_ge(S("ba_psum"), 2)
        nc.vector.tensor_copy(ba[:, 0:2, :], cube(B[4][:, 0:16], 2)).then_inc(S("ba_out"), 1)
        nc.vector.tensor_copy(ba[0:META, 2, :], B[4][0:META, 16:24]).then_inc(S("ba_meta"), 1)
        dve.wait_ge(S("ba_psum"), 3)
        nc.vector.tensor_copy(ba[:, 2, :], B[4][:, 32:40]).then_inc(S("ba_out"), 1)
        dve.wait_ge(S("ba_out"), 2)
        dve.wait_ge(S("dn_small_in"), 48)
        line(tt(gu, ba[:, :, DN_H:2 * DN_H], dtb.unsqueeze(1).broadcast_to([P, 3, DN_H]), ALU.add))
        stt(gt, gu, -1.0, gu, ALU.mult, ALU.max).then_inc(S("ga_abs"), 1)
        dve.wait_ge(S("be_exp"), 1)
        line(ts(be, be, 1.0, None, ALU.add))
        line(nc.vector.reciprocal(be, be))
        dve.wait_ge(S("ga_ln"), 2)
        line(stt(gu, gu, 0.0, gt, ALU.max, ALU.add))
        line(stt(ge, gu, -1.0, alog.unsqueeze(1).broadcast_to([P, 3, DN_H]), ALU.mult, ALU.mult))
        for src, dst in ((ge, G), (be, BE)):
            nc.vector.tensor_copy(dst[:, 0:8], src[:, 0:2, :].rearrange("p t h -> p (t h)"))
            line(tt(gt[:, 0, :], src[:, 2, :], C("hmask"), ALU.mult))
            line(nc.vector.reduce_sum(dst[:, 8:9], gt[:, 0, :], AX.X))
        dve.nop().then_inc(S("g_made"), 1)
        for dst, src in ((gB, G), (bB, BE)):
            for c in range(NM):
                last = ts(dst[:, c, :], C("ones"), src[:, c:c + 1], None, ALU.mult)
        last.then_inc(S("rows_made"), 1)
        for c in range(8):
            dve.wait_ge(S("rnorm"), c + 1)
            stt(conv_out[:, c, :], conv_out[:, c, :], (128 ** -0.5 if c < 4 else 1.0), sq[:, c, :], ALU.mult, ALU.mult).then_inc(S("normed"), 1)
        dve.wait_ge(S("dec_psum"), 1)
        nc.vector.tensor_copy(DEC, B[5][:, 0:NM])
        line(nc.vector.tensor_copy(DL, B[5][:, 16:16 + NM]))
        tt(KF, DL, DEC, ALU.subtract).then_inc(S("dec_out"), 1)
        rowbank = (B[4], B[6], B[7])
        for i, part in enumerate(PARTS):
            dve.wait_ge(S("row_psum"), i + 1)
            for j, c in enumerate(range(part.start, part.stop)):
                last = ts(LM[:, c, :], rowbank[i][:, j * P:(j + 1) * P], DEC[:, c:c + 1], 0.0, ALU.subtract, ALU.min)
            last.then_inc(S("decay_rows"), 1)
        dve.wait_ge(S("dec_exp"), 1)
        stt(NBE, BE, -1.0, ED, ALU.mult, ALU.mult).then_inc(S("nbe_made"), 1)
        for i, part in enumerate(PARTS):
            n = part.stop - part.start
            dve.wait_ge(S("lm_exp"), i + 1)
            line(tt(LM[:, part, :], LM[:, part, :], masks("upper" if i < 2 else "mupper", n), ALU.mult))
            dve.wait_ge(S("row_psum"), i + 4)
            tt(flat(LB[:, part, :]), flat(LM[:, part, :]), rowbank[i][:, 0:n * P], ALU.mult).then_inc(S("lb_made"), 1)
        for i in range(NT):
            dve.wait_ge(S("chunk_psum"), i + 1)
            for h in range(DN_H):
                c = 4 * i + h
                last = ts(kdec[:, c, :], B[i][:, h * P:(h + 1) * P], KF[:, c:c + 1], None, ALU.mult)
            last.then_inc(S("chunk_dve"), 1)
        dve.wait_ge(S("chunk_psum"), 5)
        ts(kdec[:, 8, :], B[5][:, 0:P], KF[:, 8:9], None, ALU.mult).then_inc(S("chunk_dve"), 1)
        dve.wait_ge(S("lb_made"), 3)
        for i, part in enumerate(PARTS):
            dve.wait_ge(S("chunk_psum"), i + 6)
            n = part.stop - part.start
            tt(flat(AT[:, part, :]), rowbank[i][:, 0:n * P], flat(LB[:, part, :]), ALU.mult).then_inc(S("chunk_dve"), 1)
        for i in range(NT):
            dve.wait_ge(S("chunk_psum"), i + 9)
            tt(flat(QKT[:, PARTS[i], :]), B[i], flat(LM[:, PARTS[i], :]), ALU.mult).then_inc(S("chunk_dve"), 1)
        dve.wait_ge(S("proj_out"), 25)
        dve.wait_ge(S("dn_small_in"), 48)
        for i in range(NT):
            last = tt(cube(zs[:, i, :], 4), cube(zs[:, i, :], 4), dng[:, :].unsqueeze(1).broadcast_to([P, 4, P]), ALU.mult)
        last.then_inc(S("z_scaled"), 1)
        dve.wait_ge(S("b_gate_in"), 16)
        for n in range(8):
            u, i = n // 2, n % 2
            cols = slice((u % 2) * 512, (u % 2 + 1) * 512)
            dve.wait_ge(S("proj"), GATE0 + n + 1)
            tt(gates[:, i, u // 2, cols], B[(GATE0 + n) % 4], params[:, 2 + u // 2, cols], ALU.add).then_inc(S("gate_out"), 1)
        dve.wait_ge(S("inverse_start"), 1)
        for lv in range(LEVELS):
            for i, part in enumerate(PARTS):
                n = part.stop - part.start
                dve.wait_ge(S("inv_ax"), 3 * lv + i + 1)
                tt(TM[:, part, :], cube(B[i if i < 2 else 6][:, 0:n * P], n), masks(f"level{lv}", n), ALU.mult).then_inc(S("inv_masked"), 1)
            for i, part in enumerate(PARTS):
                n = part.stop - part.start
                dve.wait_ge(S("inv_xax"), 3 * lv + i + 1)
                if lv:
                    dve.wait_ge(S("inv_step"), 3 * (lv - 1) + i + 1)
                tt(flat(XI[:, part, :]), flat(XI[:, part, :]), (B[2], B[3], B[6][:, P:2 * P])[i][:, 0:n * P], ALU.subtract)
                tt(flat(XIT[:, part, :]), flat(XIT[:, part, :]), (B[4], B[5], B[6][:, 2 * P:3 * P])[i][:, 0:n * P], ALU.subtract).then_inc(S("inv_step"), 1)
        dve.wait_ge(S("nbe_made"), 1)
        dve.wait_ge(S("chunk_act"), 2)
        dve.wait_ge(S("state_first"), 1)
        for i in range(NT):
            dve.wait_ge(S("step_psum"), 5 * i + 3)
            for h in range(DN_H):
                c = 4 * i + h
                last = stt(rhs[:, h, :], B[0][:, h * P:(h + 1) * P], NBE[:, c:c + 1], vb[:, c, :], ALU.mult, ALU.add)
            last.then_inc(S("rhs_made"), 1)
            if i < NT - 1:
                dve.wait_ge(S("step_psum"), 5 * i + 6)
                for h in range(DN_H):
                    c = 4 * i + h
                    last = stt(state[:, h, :], state[:, h, :], CD[:, c:c + 1], B[2][:, h * P:(h + 1) * P], ALU.mult, ALU.add)
                last.then_inc(S("state_out"), 1)
            dve.wait_ge(S("step_psum"), 4 * i + 7)
            dve.wait_ge(S("o_decayed"), i + 1)
            tt(flat(odec[i]), flat(odec[i]), B[7], ALU.add).then_inc(S("o_made"), 1)
        dve.wait_ge(S("z_scaled"), 1)
        for i in range(NT):
            dve.wait_ge(S("o_rstd"), i + 1)
            for h in range(DN_H):
                zh = zs[:, i, h * P:(h + 1) * P]
                last = stt(zh, odec[i][:, h, :], rsd[:, 4 * i + h:4 * i + h + 1], zh, ALU.mult, ALU.mult)
            last.then_inc(S("o_normed"), 1)
        for g in range(4):
            hs = slice(2 * g, 2 * g + 2)
            dve.wait_ge(S("z_psum"), g + 1)
            nc.vector.tensor_copy(Z0[:, hs, P:SEQ], cube(B[g], 2)[:, :, P:SEQ])
            tt(Z0[:, hs, 0:P], cube(B[g], 2)[:, :, 0:P], masks("strict", 2), ALU.mult).then_inc(S("z_out"), 1)
        for g in range(2):
            dve.wait_ge(S("z_psum"), g + 5)
            tt(Z1[:, 4 * g:4 * g + 4, :], cube(B[4 + g], 4), masks("strict", 4), ALU.mult).then_inc(S("z_out"), 1)
        dve.wait_ge(S("sp_ln"), 1)
        dve.wait_ge(S("z_out"), 6)
        stt(SP[0:META, 3072:5120], Z[0:META, 3072:5120], 0.0, SP[0:META, 3072:5120], ALU.max, ALU.add)
        stt(SP[:, 0:3072], Z[:, 0:3072], 0.0, SP[:, 0:3072], ALU.max, ALU.add).then_inc(S("sp_made"), 1)
        for g in range(4):
            hs = slice(2 * g, 2 * g + 2)
            dve.wait_ge(S("later_psum"), g + 1)
            tt(Z0[:, hs, :], Z0[:, hs, :], cube(B[g], 2), ALU.subtract).then_inc(S("later_out"), 1)
        for g in range(2):
            dve.wait_ge(S("later_psum"), g + 5)
            hs = slice(4 * g, 4 * g + 4)
            tt(Z1[:, hs, :], Z1[:, hs, :], cube(B[4 + g], 4), ALU.subtract).then_inc(S("later_out"), 1)
        for g in range(4):
            hs = slice(2 * g, 2 * g + 2)
            dve.wait_ge(S("later_psum"), g + 7)
            tt(ZM[:, hs, :], ZM[:, hs, :], cube(B[(6, 7, 0, 1)[g]][0:META, :], 2), ALU.subtract).then_inc(S("later_out"), 1)
        for i in range(NT):
            dve.wait_ge(S("mix_psum"), i + 3)
            nc.vector.tensor_copy(osb[:, i, :], B[2 + i]).then_inc(S("sb_out"), 1)
        dve.wait_ge(S("gate_sig"), 8)
        for n in range(8):
            br, i, half = n // 4, (n // 2) % 2, n % 2
            g_ = gates[:, i, br, half * 512:(half + 1) * 512]
            dve.wait_ge(S("branch"), n + 1)
            tt(g_, g_, B[n % 4], ALU.mult).then_inc(S("branch_out"), 1)
        for i in range(NT):
            dve.wait_ge(S("branch_out"), 6 + 2 * i)
            tt(gates[:, i, 0, :], gates[:, i, 0, :], gates[:, i, 1, :], ALU.add).then_inc(S("merged"), 1)
        xT_copies(1, SEQ)
        for n in range(4):
            half, i = n // 2, n % 2
            x = X0[:, i, half * 512:(half + 1) * 512]
            dve.wait_ge(S("mixed"), n + 1)
            stt(x, x, ALPHA, B[n], ALU.mult, ALU.add).then_inc(S("mixed_out"), 1)
        b3 = lambda a, n: a.unsqueeze(2).broadcast_to([P, 2, n])
        b2 = lambda name, n: C(name).unsqueeze(1).broadcast_to([P, 2, n])
        red = nc.vector.tensor_reduce
        n_rstd = [3]

        def norm_pair(src, dst, g, b, ready, out_sem):
            for i in range(NT):
                moments(1 + i, src[:, i, :], P)
            dve.wait_ge(S(ready), 32)
            for i in range(NT):
                n_rstd[0] += 1
                dve.wait_ge(S("rstd"), n_rstd[0])
                normalize(src[:, i, :], dst[:, i, :], 1 + i, P, g, b).then_inc(S(out_sem), 1)

        dve.wait_ge(S("mixed_out"), 4)
        norm_pair(X0, X1, 0, 1, "ln1_in", "h1_made")
        xT_copies(2, SEQ)
        dve.wait_ge(S("h1_made"), 2)
        for i in range(NT):
            ts(X0[:, i, :], X1[:, i, :], ALPHA, None, ALU.mult)
        dve.wait_ge(S("router_in"), 16 * (NG + 3))
        dve.wait_ge(S("router_psum"), 1)
        line(tt(lg, B[0][:, 0:128].rearrange("p (t n) -> p t n", t=2)[:, :, 0:36], rbias.unsqueeze(1).broadcast_to([P, 2, 36]), ALU.add))
        line(red(mx, gl, AX.X, ALU.max))
        line(tt(gd, gl, b3(mx, NG), ALU.subtract))
        line(ts(g4, gd, 0.0, None, ALU.is_equal))
        dve.nop().then_inc(S("router_dve"), 1)
        line(tt(g4, g4, b2("desc4", NG), ALU.mult))
        line(red(gs, g4, AX.X, ALU.max))
        tt(oh, g4, b3(gs, NG), ALU.is_equal).then_inc(S("router_dve"), 1)
        dve.wait_ge(S("router_dve"), 2)
        line(tt(g4, oh, b2("idx4", NG), ALU.mult))
        line(red(gid, g4, AX.X, ALU.add))
        dve.wait_ge(S("router_act"), 1)
        line(red(gs, gd, AX.X, ALU.add))
        line(nc.vector.reciprocal(gp, gs))
        for i in range(NT):
            last = tt(picked[:, i], exl[:, i], oh[:, i, :].unsqueeze(2).broadcast_to([P, NG, NE]), ALU.mult)
        line(last)
        line(red(sl, picked.rearrange("p t g e -> p t e g"), AX.X, ALU.add))

        def largest(vals, top, one_hot):
            line(red(top, vals, AX.X, ALU.max))
            line(tt(e8, vals, b3(top, NE), ALU.is_equal))
            line(tt(e8, e8, b2("desc8", NE), ALU.mult))
            line(red(gs, e8, AX.X, ALU.max))
            line(tt(one_hot, e8, b3(gs, NE), ALU.is_equal))

        largest(sl, top1, oh1)
        line(stt(sl2, oh1, NEG, sl, ALU.mult, ALU.add))
        largest(sl2, top2, oh2)
        tt(w2, top2, top1, ALU.subtract).then_inc(S("router_dve"), 1)
        dve.wait_ge(S("router_act"), 2)
        line(ts(w1, w2, 1.0, None, ALU.add))
        line(nc.vector.reciprocal(w1, w1))
        line(tt(w1, w1, gp, ALU.mult))
        line(tt(w2, w2, w1, ALU.mult))
        line(tt(oh1, oh1, b3(w1, NE), ALU.mult))
        line(tt(oh2, oh2, b3(w2, NE), ALU.mult))
        line(tt(cmb, oh1, oh2, ALU.add))
        dve.wait_ge(S("router_psum"), 2)
        nc.vector.tensor_copy(rk, B[1][:, 0:3 * NG]).then_inc(S("scat_out"), 1)
        dve.wait_ge(S("scat_out"), 1)
        line(tt(g4, oh, cube(rk[:, 0:2 * NG], 2), ALU.mult))
        line(red(rank, g4, AX.X, ALU.add))
        line(ts(over, rank, float(P), None, ALU.is_ge))
        line(stt(pos, gid, float(P), rank, ALU.mult, ALU.add))
        line(ts(gid, gid, -float(P), 3.0 * P, ALU.mult, ALU.add))
        line(tt(gid, gid, over, ALU.mult))
        line(tt(pos, pos, gid, ALU.add))
        line(ts(ct, rk[:, 2 * NG:3 * NG], float(P), None, ALU.is_gt))
        line(red(ovf[:, 0:1], ct, AX.X, ALU.add))
        line(tt(ct, ct, C("idx4"), ALU.mult))
        line(red(ovf[:, 1:2], ct, AX.X, ALU.add))
        nc.vector.tensor_copy(ovi[:, :], ovf).then_inc(S("over_made"), 1)

        def select(s_):
            for i in range(NT):
                last = ts(sel[:, i, :], C("iota"), pos[:, i:i + 1], None, ALU.is_equal)
            last.then_inc(S("sel_made"), 1)
            dve.wait_ge(S("sel_made"), s_ + 1)
            ts(pos, pos, -float(P), None, ALU.add).then_inc(S("pos_made"), 1)

        def weights(s_):
            dve.wait_ge(S("sel_psum"), s_ + 1)
            nc.vector.tensor_copy(comb, B[7][:, 0:NE]).then_inc(S("comb_out"), 1)

        def selection(s_):
            nc.vector.tensor_copy(selT, B[7][:, P:3 * P]).then_inc(S("selT_out"), 1)

        def experts(s_, over_=False):
            dve.wait_ge(S("comb_out"), s_ + 1)
            for e in range(NE):
                dve.wait_ge(S("sg_made"), s_ * NE + (e + 1))
                if e >= 2:
                    dve.wait_ge(S("hT_psum"), s_ * NE + (e - 1))
                stt(hid[:, e % 2, :], sg[:, e % 2, :], comb[:, e:e + 1], B[e % 2][:, FF:2 * FF], ALU.mult, ALU.mult).then_inc(S("hid"), 1)
                if e == 4 and not over_:
                    dve.wait_ge(S("sel_psum"), s_ + 1)
                    dve.wait_ge(S("pos_made"), s_ + 1)
                    select(s_ + 1)
            if not over_:
                dve.wait_ge(S("hid"), s_ * NE + NE)
                weights(s_ + 1)
            dve.wait_ge(S("down"), s_ * NE + NE)
            nc.vector.tensor_copy(ysb[:, 0:512], B[2]).then_inc(S("y_dve"), 1)
            for q in range(4):
                x_ = X0[:, q // 2, (q % 2) * 512:(q % 2 + 1) * 512]
                dve.wait_ge(S("scat"), s_ * 4 + (q + 1))
                tt(x_, x_, B[q % 2], ALU.add).then_inc(S("scat_out"), 1)
            if not over_:
                selection(s_ + 1)

        select(0)
        weights(0)
        selection(0)
        with dve.Fori(0, NG) as s_:
            experts(s_)
        dve.wait_ge(S("over_made"), 1)
        flag = dve.value_load(ovi[0:1, 0:1], min_val=0, max_val=1)
        with dve.If(flag):
            experts(NG, True)
            dve.wait_ge(S("scat_out"), 4 * (NG + 1) + 1)
        dve.wait_ge(S("scat_out"), 4 * NG + 1)
        norm_pair(X0, X0, 2, 3, "ln2_in", "h2_made")
        def rms_norm(r, param):
            for i in range(NT):
                dve.wait_ge(S("rms"), 2 * r + i + 1)
                if i == 0:
                    dve.wait_ge(S(f"rms{r}_in"), 16)
                stt(X1[:, i, :], X0[:, i, :], rsd[:, i:i + 1], params[:, param, :], ALU.mult, ALU.mult).then_inc(S("xn_made"), 1)

        dve.wait_ge(S("pos_in"), 32)
        line(nc.vector.tensor_copy(posf, posi[:, :]))
        for i in range(NT):
            last = ts(ang[:, i, :], C("freq"), posf[:, i:i + 1], None, ALU.mult)
        line(last)
        for out, quarter in ((sine, 0.0), (cosine, 0.25)):
            line(ts(turn, ang, 1.0 / (2 * math.pi), quarter, ALU.mult, ALU.add))
            line(ts(turn, turn, ROUND, -ROUND, ALU.add, ALU.add))
            line(stt(out, turn, -TWO_PI[0], ang, ALU.mult, ALU.add))
            line(stt(out, turn, -TWO_PI[1], out, ALU.mult, ALU.add))
            line(stt(out, turn, -TWO_PI[2], out, ALU.mult, ALU.add))
            if quarter:
                line(ts(out, out, math.pi / 2, None, ALU.add))
            line(ts(out, out, 3.1415925, -3.1415925, ALU.min, ALU.max))
        dve.nop().then_inc(S("turned"), 1)
        rms_norm(0, 0)
        xT_copies(3, SEQ)
        dve.wait_ge(S("sines"), 1)
        for i in range(NT):
            dve.wait_ge(S("qkv_out"), 7 + i)
            heads = qk[:, i, :].rearrange("p (h d) -> p h d", d=AT_D)
            x1, x2 = heads[:, :, 0:HALF], heads[:, :, HALF:ROT]
            cb, sb_ = [a[:, i, :].unsqueeze(1).broadcast_to([P, 16, HALF]) for a in (cosine, sine)]
            a, b, c, d = rope_t
            for o_, p_, q_ in ((a, x1, cb), (b, x2, sb_), (c, x2, cb), (d, x1, sb_)):
                last = tt(o_, p_, q_, ALU.mult)
            line(last)
            line(tt(x1, a, b, ALU.subtract))
            tt(x2, c, d, ALU.add).then_inc(S("rope_made"), 1)
            dve.wait_ge(S("rope_made"), i + 1)
        for g in range(1, 8, 2):
            dve.wait_ge(S("att_psum"), g + 1)
            nc.vector.tensor_copy(flat(qkT[:, 2 * g:2 * g + 2, :]), B[4 + g % 4]).then_inc(S("qkT_dve"), 1)
        dve.wait_ge(S("causal_made"), 1)
        for h in range(AT_H):
            dve.wait_ge(S("att_psum"), h + 9)
            stt(sc_[:, h, :], B[h % 4][:, 0:3 * P], AT_D ** -0.5, causal, ALU.mult, ALU.add).then_inc(S("scores_out"), 1)
            if h % 4 == 3:
                hs = slice(h - 3, h + 1)
                dve.wait_ge(S("scores_out"), h + 1)
                red(mxs[:, 0, hs], sc_[:, hs, 0:P], AX.X, ALU.max)
                line(red(mxs[:, 1, hs], sc_[:, hs, P:3 * P], AX.X, ALU.max))
                ts(mxs[:, :, hs], mxs[:, :, hs], -1.0, None, ALU.mult).then_inc(S("max_made"), 1)
        for h in range(AT_H):
            dve.wait_ge(S("att_psum"), h + 17)
            nc.vector.tensor_copy(pT[:, h, :], B[4 + h % 4][:, 0:3 * P]).then_inc(S("pT_out"), 1)
        dve.wait_ge(S("p_made"), 8)
        line(nc.vector.reciprocal(sums, sums))
        for i in range(NT):
            for hh in range(2):
                dve.wait_ge(S("att_psum"), 24 + (4 if hh == 0 and i == 0 else 8))
                rec = sums[:, i, 4 * hh:4 * hh + 4].unsqueeze(2).broadcast_to([P, 4, P])
                last = tt(cube(qk[:, i, hh * 512:(hh + 1) * 512], 4), cube(B[2 * i + hh], 4), rec, ALU.mult)
            last.then_inc(S("att_made"), 1)
        xT_copies(4, SEQ)
        for n in range(4):
            half, i = n // 2, n % 2
            x = X0[:, i, half * 512:(half + 1) * 512]
            dve.wait_ge(S("att_o"), n + 1)
            ins = tt(x, x, B[n], ALU.add)
            if half:
                ins.then_inc(S("res"), 1)

        def mlp(m, call):
            xT_copies(call, SEQ)

            def square(j, jj=0):
                for pr in range(2):
                    h_ = hid2[:, j % 2, 2 * pr:2 * pr + 2, :]
                    dve.wait_ge(S("relu"), jj * 4 + (16 * m + 2 * j + pr + 1))
                    tt(h_, h_, h_, ALU.mult).then_inc(S("squared"), 1)

            square(0)
            square(1)
            with dve.Fori(0, 3) as jj:
                square(2, jj)
                square(3, jj)
            dve.wait_ge(S("mlp_down"), 8 * (m + 1))
            for n in range(4):
                x = X0[:, n // 2, (n % 2) * 512:(n % 2 + 1) * 512]
                ins = tt(x, x, B[n], ALU.add)
                if n % 2:
                    ins.then_inc(S("res"), 1)

        rms_norm(1, 1)
        mlp(0, 5)
        rms_norm(2, 2)
        xT_copies(6, SEQ)
        dve.wait_ge(S("scale_in"), 16)
        for n in range(4):
            i, cols = n // 2, slice((n % 2) * 512, (n % 2 + 1) * 512)
            dve.wait_ge(S("pooled"), n + 1)
            line(tt(X1[:, i, cols], B[n], params[:, 0, cols], ALU.mult))
            ins = tt(X0[:, i, cols], X0[:, i, cols], X1[:, i, cols], ALU.add)
            if n % 2:
                ins.then_inc(S("res"), 1)
        rms_norm(3, 3)
        mlp(1, 7)
        rms_norm(4, 1)

    block_cm.__exit__(None, None, None)


_INS = ['x', 'meta_tokens', 'ln_emb_g', 'ln_emb_b', 'w_in', 'b_gate', 'dn_conv_w', 'dn_a_log', 'dn_dt_bias', 'dn_norm_g',
        'w_branch_dn', 'w_branch_sb', 'w_out', 'ln1_g', 'ln1_b', 'router_group_w', 'router_group_b', 'router_expert_w',
        'router_expert_b', 'expert_w_gate', 'expert_w_up', 'expert_w_down', 'ln2_g', 'ln2_b', 'positions_2', 'norm_mix_2',
        'norm_mlp_2', 'attn_w_qkv_2', 'attn_w_o_2', 'pool_w_2', 'pool_scale_2', 'mlp_w_up_2', 'mlp_w_down_2', 'norm_final_2']


def kernel(**inputs):
    import concourse.bacc as bacc
    from concourse.bass_utils import run_bass_kernel_spmd

    nc = bacc.Bacc("TRN2", target_bir_lowering=False, num_devices=1)
    arrays, args = {}, {}
    consts, bands = shape_constants()
    for name, a in [(n, inputs[n]) for n in _INS] + [("consts", consts), ("bands", bands)]:
        a = np.ascontiguousarray(a)
        arrays[f"in_{name}"] = a
        args[name] = nc.dram_tensor(f"in_{name}", a.shape, mybir.dt.from_np(a.dtype), kind="ExternalInput").ap()
    args["out"] = nc.dram_tensor("out_y", (1, SEQ, D), F32, kind="ExternalOutput").ap()
    build(nc, args)
    result = run_bass_kernel_spmd(nc, [arrays], core_ids=[0])
    return result.results[0]["out_y"]
```

```python
import math

import numpy as np

import concourse.bass as bass
from concourse import mybir

F32 = mybir.dt.float32
F32R = mybir.dt.float32r
I32 = mybir.dt.int32
ALU = mybir.AluOpType
ACT = mybir.ActivationFunctionType
AX = mybir.AxisListType

P = 128
D = 1024
KD = D // P
SEQ = 256
NT = SEQ // P
META = 16
L = META + SEQ
DN_H = 4
DN_W = DN_H * 128
SB_H = 8
SB_D = 64
CONV = 4
COL_Z = 3 * DN_W
COL_BA = COL_Z + DN_W
COL_SB = COL_BA + 2 * DN_H
COL_G = COL_SB + 3 * SB_H * SB_D
NG = 4
NE = 8
FF = 256
ALPHA = 2.0 ** 0.25
LN_EPS = 1e-5
RMS_EPS = 1e-6
AT_H = 8
AT_D = 128
ROT = AT_D // 4
HALF = ROT // 2
THETA = 500000.0
WINDOWS = (2, 4, 8, 16)
NEG = -1e30
NM = NT * DN_H + 1
LEVELS = 7
SLOTS = 4
ROUND = 12582912.0
TWO_PI = (6.28125, round((2 * math.pi - 6.28125) * 2 ** 20) / 2 ** 20)
TWO_PI += (2 * math.pi - sum(TWO_PI),)
UNIT = 4096

SQUARES = ["ident", "upper", "strict", "ones", "lower", "mupper", "mones"] + [f"level{i}" for i in range(LEVELS)] + ["neg", "iota", "rep"]
SMALL = {"hmask": DN_H, "idx4": NG, "desc4": NG, "desc8": NE, "freq": HALF, "eps5": 1, "eps6": 1, "one": 1, "zero": 1}


def const_layout():
    at, out = 0, {}
    for n in SQUARES:
        out[n] = (at, P)
        at += P
    for n, w in SMALL.items():
        out[n] = (at, w)
        at += w
    return out, at


def shape_constants():
    lay, width = const_layout()
    c = np.zeros((P, width), np.float32)
    r, q = np.arange(P)[:, None], np.arange(P)[None, :]
    same = (r // 32 == q // 32) & (r % 32 < META) & (q % 32 < META)
    put = {
        "ident": r == q, "upper": r <= q, "strict": r < q, "ones": r >= 0, "lower": r >= q,
        "mupper": same & (r <= q), "mones": r // 32 == q // 32,
        "neg": np.where(q <= r, 0.0, NEG), "iota": q + 0 * r,
        "rep": (q % 32 == r) & (r < META),
        "hmask": (r // 32 == np.arange(DN_H)[None, :]) & (r % 32 < META),
        "idx4": np.arange(NG)[None, :] + 0 * r, "desc4": NG - np.arange(NG)[None, :] + 0 * r,
        "desc8": NE - np.arange(NE)[None, :] + 0 * r,
        "freq": (np.float32(THETA) ** (-np.arange(0, ROT, 2, dtype=np.float32) / np.float32(ROT)))[None, :] + 0 * r,
        "eps5": LN_EPS + 0 * r, "eps6": RMS_EPS + 0 * r, "one": 1 + 0 * r, "zero": 0 * r,
    }
    for i in range(LEVELS):
        s = 1 << i
        put[f"level{i}"] = ((r // s) % 2 == 1) & (q // s == r // s - 1)
    for n, v in put.items():
        a, w = lay[n]
        c[:, a:a + w] = v
    bands = np.zeros((P, 4, 3, P), np.float32)
    s = np.arange(SEQ)[:, None]
    t = np.arange(SEQ)[None, :]
    for g, w in enumerate(WINDOWS):
        full = np.where((s <= t) & (s > t - w), np.float32(1) / np.minimum(t + 1, w).astype(np.float32), 0) - (s == t)
        bands[:, g, 0], bands[:, g, 1], bands[:, g, 2] = full[:P, :P], full[P:, P:], full[:P, P:]
    return c, bands.astype(np.float32)


def build(nc, t):
    lay, const_w = const_layout()
    mm, tr = nc.tensor.matmul, nc.tensor.transpose
    act = nc.scalar.activation
    tt, ts, stt = nc.vector.tensor_tensor, nc.vector.tensor_scalar, nc.vector.scalar_tensor_tensor

    placed = {}

    def sb(name, shape, dt=F32):
        placed[name] = -(-nc.sbuf_base // 32) * 32
        return nc.alloc_sbuf_tensor(name, shape, dt)

    def parts(name, of, col, cols):
        return nc.alloc_sbuf_tensor_at(name, [P, cols], F32R, offset=placed[of] + 4 * col)[:, :]

    def f32(ap):
        return ap.bitcast(F32)

    named = {}

    def S(name):
        if name not in named:
            named[name] = nc.alloc_semaphore(name)
        return named[name]

    class Line:
        def __init__(self, eng, name):
            self.eng, self.sem, self.n = eng, S(name), 0

        def __call__(self, ins):
            self.n += 1
            ins.then_inc(self.sem, 1)
            self.eng.wait_ge(self.sem, self.n)

    B = [nc.alloc_psum_tensor(f"bank{i}", [P, 512], F32)[:, :] for i in range(8)]
    ring = sb("ring", [P, SLOTS, UNIT])
    cst = sb("cst", [P, const_w])
    params = sb("params", [P, 4, D])
    X0 = sb("X0", [P, NT, D])
    X1 = sb("X1", [P, 2 * NT, D])
    xmeta = sb("xmeta", [META, D])
    xT = sb("xT", [P, KD, L])
    stats = sb("stats", [P, 3, 2, 6])
    mv = sb("mv", [P, 3, 2])
    small = sb("small", [P, 512])
    arena = sb("arena", [P, 19456])
    taken = {"arena": 0, "small": 0}

    def reg(cols):
        a = taken["arena"]
        taken["arena"] += cols
        assert taken["arena"] <= 19456, taken
        return arena[:, a:a + cols]

    def sm(cols):
        a = taken["small"]
        taken["small"] += cols
        assert taken["small"] <= 512
        return small[:, a:a + cols]

    def C(name, rows=P, cols=None):
        a, w = lay[name]
        return cst[0:rows, a:a + (cols or w)]

    def cube(ap, c):
        return ap.rearrange("p (c i) -> p c i", c=c)

    HALF_U = UNIT // 2
    wlo = cube(parts("w_lo", "ring", 0, SLOTS * UNIT), SLOTS)

    conv_out = cube(reg(12 * L), 12)
    sbT = cube(reg(8 * L), 8)
    sbv = cube(reg(3 * 512), 3)
    zs = cube(reg(NT * 512), NT)
    phase = taken["arena"]
    raw = cube(reg(12 * (L + 3)), 12)
    sq = cube(reg(8 * L), 8)
    taken["arena"] = phase
    AT, XI, XIT, TM, LM, LB, kdec, vb = [cube(reg(NM * P), NM) for _ in range(8)]
    QKT = cube(reg(8 * P), 8)
    kTm, vTm = reg(P), reg(P)
    gB, bB = AT, XI
    vnew, state = AT[:, 0:4, :], XI[:, 0:4, :]
    rhs, odec = TM[:, 0:4, :], (TM[:, 4:8, :], LB[:, 0:4, :])
    junk = LB[:, 4:8, :]
    used_up = conv_out.rearrange("p c t -> p (c t)")
    odT, osT, osb = [cube(used_up[:, a:a + 1024], 4) for a in (8 * L, 4 * L, 0)]
    osb = cube(used_up[:, 0:1024], NT)
    taken["arena"] = phase
    Z = reg(5120)
    SP = reg(5120)
    Z0, Z1, ZM = cube(Z[:, 0:2048], 8), cube(Z[:, 2048:3072], 8), cube(Z[0:META, 3072:5120], 8)
    SP0, SP1, SPM = cube(SP[:, 0:2048], 8), cube(SP[:, 2048:3072], 8), cube(SP[0:META, 3072:5120], 8)

    wr, rbias = cube(arena[:, 18496:18496 + KD * 36], KD), arena[:, 18784:18820]
    taken["arena"] = 0
    xsH, xsL = [cube(parts(n, "arena", i * D, D), KD) for i, n in enumerate(("xs_hi", "xs_lo"))]
    reg(2 * D)
    sel, selT = cube(reg(NT * P), NT), reg(NT * P)
    sg, hid, hT = cube(reg(2 * FF), 2), cube(reg(2 * FF), 2), cube(reg(2 * FF), 2)
    ysb = reg(D)
    comb = reg(NE)
    lg = cube(reg(2 * 36), 2)
    gl, exl = lg[:, :, 0:NG], lg[:, :, NG:36].rearrange("p t (g e) -> p t g e", g=NG)
    two = lambda: reg(2)
    mx, gs, gp, top1, top2, w1, w2, rank, gid, over, pos = [two() for _ in range(11)]
    gd, oh, g4 = [cube(reg(2 * NG), 2) for _ in range(3)]
    sl, sl2, oh1, oh2, e8, cmb = [cube(reg(2 * NE), 2) for _ in range(6)]
    picked = reg(2 * 32).rearrange("p (t g e) -> p t g e", t=2, g=NG)
    rk, ct = reg(3 * NG), reg(NG)
    ovf = reg(2)
    E_BUF = 2
    ehi = cube(parts("expert_hi", "arena", taken["arena"] // 8 * 8 + 8, E_BUF * UNIT), E_BUF)
    taken["arena"] = taken["arena"] // 8 * 8 + 8 + E_BUF * UNIT
    down_w = cube(reg(UNIT), 2)
    ovi = sb("ovi", [P, 2], I32)

    taken["arena"] = 0
    qk = cube(reg(NT * 2 * D), NT)
    vv = cube(reg(NT * D), NT)
    qkT = cube(reg(16 * SEQ), 16)
    sc_ = cube(reg(AT_H * 3 * P), AT_H)
    pT = cube(reg(AT_H * 3 * P), AT_H)
    rope_t = [pT[:, 4:8, 0:256].rearrange("p (a h) d -> p a (h d)", a=4)[:, a, 0:256].rearrange("p (h d) -> p h d", h=16) for a in range(4)]
    bands = reg(12 * P).rearrange("p (g b t) -> p g b t", g=4, b=3)
    causal = reg(3 * P)
    cosine, sine, ang, turn = [cube(reg(2 * HALF), 2) for _ in range(4)]
    posf = reg(2)
    posi = sb("posi", [P, 2], I32)
    mxs, sums = cube(arena[:, 18820:18836], 2), cube(arena[:, 18836:18852], 2)
    taken["arena"] = 0
    hidH, hidL = [parts(n, "arena", c, 2 * 4 * SEQ).rearrange("p (a c t) -> p a c t", a=2, c=4) for n, c in (("hidden_hi", 0), ("hidden_lo", 2048))]
    xTL = cube(parts("xT_lo", "X1", NT * D, KD * SEQ), KD)
    whi = cube(parts("w_hi", "arena", 6144, 2 * UNIT), 2)
    relu_t = cube(arena[:, 18304:18304 + 2 * 512], 2)
    xTH = cube(parts("xT_hi", "xT", 0, KD * L), KD)

    gates = X1[:, :, :].rearrange("p (t b) d -> p t b d", t=NT)
    wba = cube(sm(KD * 8), KD)
    cw = sm(12 * CONV).rearrange("p (j c) -> p j c", j=CONV)
    cwr = sb("cwr", [48, P])
    dng = sb("dng", [P, P])
    alog, dtb = sm(DN_H), sm(DN_H)
    ba = cube(sm(24), 3)
    be, ge, gt, gu = cube(sm(12), 3), cube(sm(12), 3), cube(sm(12), 3), cube(sm(12), 3)
    G, BE, DEC, ED, KF, CD, NBE, DL = [sm(NM) for _ in range(8)]
    lnv, rst = sm(4), sm(4)
    ssq, rsd = sm(8), sm(8)
    ident = C("ident")

    def rows(w, k0, nk, c0, nc_):
        return w[k0 * P:(k0 + nk) * P, c0:c0 + nc_].rearrange("(k p) n -> p k n", p=P)

    def wide(w, c0, n=512, nk=KD, k0=0):
        h = nk // 2
        return [(i * h * n, h, rows(w, k0 + i * h, h, c0, n)) for i in range(2)]

    units, freed = [], []

    def unit(loads, name, count):
        units.append(loads)
        freed.append((name, count))

    w_in = t["w_in"][0]
    for i, (col, count) in enumerate([(0, 4), (512, 8), (1024, 12), (COL_SB, 16), (COL_SB + 512, 20), (COL_SB + 1024, 23),
                                      (COL_Z, 25)] + [(COL_G + 512 * i, 27 + 2 * i) for i in range(4)]):
        unit(wide(w_in, col), "proj", count)
    unit(wide(t["w_branch_dn"][0], 0, D, 4), "branch", 4)
    unit(wide(t["w_branch_sb"][0], 0, D, 4), "branch", 8)
    unit(wide(t["w_out"][0], 0), "mixed", 2)
    unit(wide(t["w_out"][0], 512), "mixed", 4)
    U_MOE = len(units)
    wg, wu, wd = t["expert_w_gate"][0], t["expert_w_up"][0], t["expert_w_down"][0]

    def gu_slot(e):
        return (U_MOE + e) % SLOTS

    def gu_loads(g, e):
        place = ring[:, gu_slot(e), :].rearrange("p (k n) -> p k n", k=KD)
        return [(place[:, :, i * FF:(i + 1) * FF], w[bass.ds(g, 1), e].rearrange("a (k p) n -> p (a k) n", p=P)) for i, w in enumerate((wg, wu))]

    def gu_landed(eng, s_, e, over_=False):
        if over_:
            eng.wait_ge(S(f"over_landed{gu_slot(e)}"), 32 * (e // SLOTS + 1))
        else:
            eng.wait_ge(S(f"landed{gu_slot(e)}"), s_ * (32 * NE // SLOTS) + 32 * ((U_MOE + e) // SLOTS + 1))

    for g in range(NG):
        for e in range(NE):
            unit(None, "gu", NE * g + e + 1)
    U_TWO = len(units)
    for i in range(6):
        unit(wide(t["attn_w_qkv_2"][0], 512 * i), "qkv", 2 * i + 2)
    for i in range(2):
        unit(wide(t["attn_w_o_2"][0], 512 * i), "att_o", 2 * i + 2)
    MLP_ORDER = ["up0", "up1", "down0"] + [f"{n}{2 * j + a}" for j in range(3) for n, a in (("up", 2), ("down", 1), ("up", 3), ("down", 2))] + ["down7"]
    mlp_base = []

    def mlp_units(m):
        mlp_base.append(len(units))
        for name in MLP_ORDER:
            j = int(name[-1])
            if name.startswith("up"):
                unit(wide(t["mlp_w_up_2"][m], 512 * j), "up", 16 * m + 2 * j + 2)
            else:
                unit(wide(t["mlp_w_down_2"][m], 0, D, 4, 4 * j), "mlp_down", 11 * m + j + (1 if j < 7 else 4))

    mlp_units(0)
    U_POOL = len(units)
    pool_w = t["pool_w_2"][0].rearrange("g k n -> (g k) n")
    unit(wide(pool_w, 0, FF), "pooled", 4)
    mlp_units(1)

    def slot(u):
        return ring[:, u % SLOTS, :]

    def slab(u, k, n=512):
        return slot(u)[:, k * n:(k + 1) * n]

    def landed(eng, u):
        eng.wait_ge(S(f"landed{u % SLOTS}"), 32 * (u // SLOTS + 1))

    N_DN = 12
    N_FM = 20
    GATE0 = 25
    SSQ_BANK = (B[2], B[3], B[6], B[7])
    xblk = lambda i: (META + i * P, P)
    block_cm = nc.Block()
    block = block_cm.__enter__()
    M4, M8 = slice(0, 4), slice(4, 8)
    PARTS = [slice(0, 4), slice(4, 8), slice(8, 9)]
    flat = lambda a: a.rearrange("p c i -> p (c i)")

    def masks(name, n):
        return C(name).unsqueeze(1).broadcast_to([P, n, P])

    @block.sync
    def _(sp):
        def load(u):
            if u >= SLOTS:
                sp.wait_ge(S(freed[u - SLOTS][0]), freed[u - SLOTS][1])
            for a, k, src in units[u]:
                n = src.shape[2]
                sp.dma_start(slot(u)[:, a:a + k * n].rearrange("p (k n) -> p k n", k=k), src).then_inc(S(f"landed{u % SLOTS}"), 16)

        sp.dma_start(xmeta[:, :], t["meta_tokens"]).then_inc(S("meta_in"), 16)
        for i in range(NT):
            sp.dma_start(X0[:, i, :], t["x"][0, i * P:(i + 1) * P, :]).then_inc(S(f"x{i}_in"), 16)
        sp.dma_start(cst[:, :], t["consts"]).then_inc(S("cst_in"), 16)
        sp.dma_start(cwr[:, :], t["dn_conv_w"][0].rearrange("j (c p) -> (j c) p", p=P)).then_inc(S("cw_in"), 16)
        for u in range(2):
            load(u)
        sp.dma_start(wba, w_in[:, COL_BA:COL_BA + 8].rearrange("(k p) n -> p k n", p=P)).then_inc(S("wba_in"), 16)
        for u in range(2, U_MOE):
            load(u)
        def load_gu(g, e, wait, over_=False):
            sp.wait_ge(S("gu"), wait)
            for place, src in gu_loads(g, e):
                sp.dma_start(place, src).then_inc(S(f"over_landed{gu_slot(e)}" if over_ else f"landed{gu_slot(e)}"), 16)

        def load_down(g, e, wait=None):
            if wait is not None:
                sp.wait_ge(S("down"), wait)
            place = down_w[:, e % 2, :].rearrange("p (k n) -> p k n", k=2)
            sp.dma_start(place, wd[bass.ds(g, 1), e].rearrange("a (k p) n -> p (a k) n", p=P)).then_inc(S(f"down_landed{e % 2}"), 16)

        def load_group(g, nxt):
            for e in range(NE):
                if e < SLOTS:
                    load_gu(g, e + SLOTS, g * NE + (e + 1))
                elif nxt is not None:
                    load_gu(nxt, e - SLOTS, g * NE + (e + 1))
                if 2 <= e:
                    load_down(g, e, g * NE + (e - 1))
            if nxt is not None:
                for e in range(2):
                    load_down(nxt, e, g * NE + (NE - 1 + e))

        for e in range(SLOTS):
            sp.wait_ge(S(freed[U_MOE + e - SLOTS][0]), freed[U_MOE + e - SLOTS][1])
            for place, src in gu_loads(0, e):
                sp.dma_start(place, src).then_inc(S(f"landed{gu_slot(e)}"), 16)
        sp.wait_ge(S("mixed"), 4)
        for e in range(2):
            load_down(0, e)
        with sp.Fori(0, NG - 1) as g:
            load_group(g, g + 1)
        load_group(NG - 1, None)
        sp.wait_ge(S("over_made"), 1)
        flag = sp.value_load(ovi[0:1, 0:1], min_val=0, max_val=1)
        group_ = sp.value_load(ovi[0:1, 1:2], min_val=0, max_val=NG - 1)
        with sp.If(flag):
            for e in range(SLOTS):
                load_gu(group_, e, NE * (NG - 1) + SLOTS + e + 1, True)
            for e in range(2):
                load_down(group_, e, NE * NG - 1 + e)
            for e in range(NE):
                if e < SLOTS:
                    load_gu(group_, e + SLOTS, NE * NG + e + 1, True)
                if 2 <= e:
                    load_down(group_, e, NE * NG + e - 1)
            sp.wait_ge(S("down"), NE * (NG + 1))
        for u in range(U_TWO, len(units)):
            load(u)
        for i in range(NT):
            sp.wait_ge(S("xn_made"), 9 + i)
            sp.dma_start(t["out"][0, i * P:(i + 1) * P, :], X1[:, i, :]).then_inc(S("stored"), 16)
        sp.wait_ge(S("stored"), 16 * NT)

    @block.gpsimd
    def _(pool):
        def bcast(dst, src, name):
            pool.dma_start(dst, src.partition_broadcast(P)).then_inc(S(name), 16)

        bcast(params[:, 0, :], t["ln_emb_g"], "emb_in")
        bcast(params[:, 1, :], t["ln_emb_b"], "emb_in")
        nc.gpsimd.memset(raw[:, :, 0:3], 0.0).then_inc(S("raw_pad"), 1)
        bcast(alog, t["dn_a_log"][0], "dn_small_in")
        bcast(dtb, t["dn_dt_bias"][0], "dn_small_in")
        bcast(dng[:, :], t["dn_norm_g"][0], "dn_small_in")
        bcast(params[:, 2:4, :], t["b_gate"][0], "b_gate_in")
        pool.dma_start(wr[:, :, 0:NG], t["router_group_w"][0].rearrange("(k p) n -> p k n", p=P)).then_inc(S("router_in"), 16)
        for g in range(NG):
            pool.dma_start(wr[:, :, NG + NE * g:NG + NE * (g + 1)], t["router_expert_w"][0, g].rearrange("(k p) n -> p k n", p=P)).then_inc(S("router_in"), 16)
        bcast(rbias[:, 0:NG], t["router_group_b"][0], "router_in")
        bcast(rbias[:, NG:36], t["router_expert_b"][0].rearrange("g e -> (g e)"), "router_in")
        for c in range(8):
            pool.wait_ge(S("silu"), c + 1)
            nc.gpsimd.tensor_tensor(sq[:, c, :], conv_out[:, c, :], conv_out[:, c, :], ALU.mult).then_inc(S("squares"), 1)
        line = Line(pool, "pool_line")
        pool.wait_ge(S("silu"), N_DN)
        pool.wait_ge(S("normed"), 8)
        line(nc.gpsimd.memset(kTm, 0.0))
        line(nc.gpsimd.memset(vTm, 0.0))
        for h in range(DN_H):
            nc.gpsimd.tensor_copy(kTm[:, 32 * h:32 * h + META], conv_out[:, 4 + h, 0:META])
            last = nc.gpsimd.tensor_copy(vTm[:, 32 * h:32 * h + META], conv_out[:, 8 + h, 0:META])
        last.then_inc(S("meta_stack"), 1)
        pool.wait_ge(S("row_psum"), 6)
        for c in range(NM):
            nc.gpsimd.tensor_copy(XI[:, c, :], ident)
            last = nc.gpsimd.tensor_copy(XIT[:, c, :], ident)
        last.then_inc(S("inverse_start"), 1)
        for what, name in ((SP, "sp_made"), (Z, "w_made")):
            pool.wait_ge(S(name), 1 if what is SP else 2)
            a0 = cube(what[:, 0:2048], 8)[:, :, 0:P]
            a1 = cube(what[:, 2048:3072], 8)
            nc.gpsimd.tensor_tensor(a0, a0, masks("strict", 8), ALU.mult).then_inc(S("masked"), 1)
            nc.gpsimd.tensor_tensor(a1, a1, masks("strict", 8), ALU.mult).then_inc(S("masked"), 1)
        pool.wait_ge(S("embedded"), 3)
        bcast(params[:, 0, :], t["ln1_g"][0], "ln1_in")
        bcast(params[:, 1, :], t["ln1_b"][0], "ln1_in")
        pool.wait_ge(S("gate_out"), 8)
        bcast(params[:, 2, :], t["ln2_g"][0], "ln2_in")
        bcast(params[:, 3, :], t["ln2_b"][0], "ln2_in")
        for i in range(NT):
            pool.dma_start(posi[:, i:i + 1], t["positions_2"][0, i * P:(i + 1) * P].rearrange("(p a) -> p a", a=1)).then_inc(S("pos_in"), 16)
        pool.wait_ge(S("h1_made"), 2)
        bcast(params[:, 0, :], t["norm_mix_2"][0], "rms01_in")
        bcast(params[:, 1, :], t["norm_mlp_2"][0], "rms01_in")
        for u in range(2):
            for i in range(2):
                half = slice(i * HALF_U, (i + 1) * HALF_U)
                pool.wait_ge(S("split_hi"), 2 * u + i + 1)
                nc.gpsimd.tensor_tensor(wlo[:, (U_TWO + u) % SLOTS, half], slot(U_TWO + u)[:, half], f32(whi[:, u, half]), ALU.subtract).then_inc(S("qkv_lo"), 1)
        pool.wait_ge(S("h2_made"), 2)
        nc.gpsimd.tensor_copy(causal[:, 0:P], C("neg"))
        nc.gpsimd.memset(causal[:, P:2 * P], 0.0)
        nc.gpsimd.tensor_copy(causal[:, 2 * P:3 * P], C("neg")).then_inc(S("causal_made"), 1)
        pool.dma_start(bands, t["bands"]).then_inc(S("bands_in"), 16)
        bcast(params[:, 2, :], t["norm_mix_2"][1], "rms23_in")
        bcast(params[:, 3, :], t["norm_mlp_2"][1], "rms23_in")
        pool.wait_ge(S("xn_made"), 2)
        bcast(params[:, 0, :], t["pool_scale_2"][0], "scale_in")
        pool.wait_ge(S("xn_made"), 4)
        bcast(params[:, 1, :], t["norm_final_2"], "rms4_in")

    @block.tensor
    def _(pe):
        def transposes(call, tiles, made=None):
            if made:
                name, count = made if isinstance(made, tuple) else (made, 2)
                pe.wait_ge(S(name), count)
            for k in range(KD):
                if k >= 2 or call > 0:
                    pe.wait_ge(S("xT_act" if k % 2 == 0 else "xT_dve"), (KD // 2) * call + k // 2)
                for src, r, col in tiles:
                    last = tr(B[6 + k % 2][:, col:col + r], src[:, k * P:(k + 1) * P], ident[0:r, 0:r])
                last.then_inc(S("xT_psum"), 1)

        def xT_ready(call):
            pe.wait_ge(S("xT_act"), (KD // 2) * (call + 1))
            pe.wait_ge(S("xT_dve"), (KD // 2) * (call + 1))

        pe.wait_ge(S("cst_in"), 16)
        pe.wait_ge(S("embedded"), 3)
        transposes(0, [(xmeta[:, :], META, 0), (X0[:, 0, :], P, META), (X0[:, 1, :], P, META + P)])
        pe.wait_ge(S("cw_in"), 16)
        tr(B[5][:, 0:48], cwr[:, :], ident[0:48, 0:48]).then_inc(S("ba_psum"), 1)
        xT_ready(0)
        group = [0]

        def bank_free(n):
            if 4 <= n < GATE0 + 4:
                pe.wait_ge(S("proj_out"), n - 3)
            elif n >= GATE0 + 4:
                pe.wait_ge(S("gate_out"), n - 3 - GATE0)

        def features(u):
            landed(pe, u)
            for c in range(4):
                n = group[0]
                bank_free(n)
                for k in range(KD):
                    last = mm(B[n % 4][:, 0:L], slab(u, k)[:, c * P:(c + 1) * P], xT[:, k, :], start=(k == 0), stop=(k == KD - 1))
                last.then_inc(S("proj"), 1)
                group[0] += 1

        def tokens(u, tiles):
            landed(pe, u)
            for a, r in tiles:
                n = group[0]
                bank_free(n)
                for k in range(KD):
                    last = mm(B[n % 4][0:r, :], xT[:, k, a:a + r], slab(u, k), start=(k == 0), stop=(k == KD - 1))
                last.then_inc(S("proj"), 1)
                group[0] += 1

        for u in range(3):
            features(u)
        pe.wait_ge(S("wba_in"), 16)
        for i, (a, r) in enumerate([xblk(0), xblk(1), (0, META)]):
            for k in range(KD):
                last = mm(B[4][0:r, 8 * i:8 * i + 8], xT[:, k, a:a + r], wba[:, k, :], start=(k == 0), stop=(k == KD - 1))
        last.then_inc(S("ba_psum"), 1)
        pe.wait_ge(S("ba_out"), 2)
        mm(B[4][:, 32:40], C("rep", META), ba[0:META, 2, :], start=True, stop=True).then_inc(S("ba_psum"), 1)
        for u in (3, 4):
            features(u)
        tokens(5, [xblk(0), xblk(1)])
        pe.wait_ge(S("proj_out"), N_FM)
        for c in range(8):
            pe.wait_ge(S("squares"), c + 1)
            if c >= 4:
                pe.wait_ge(S("ssq_ln"), c - 3)
            mm(SSQ_BANK[c % 4][:, 0:L], C("ones"), sq[:, c, :], start=True, stop=True).then_inc(S("ssq_psum"), 1)
        pe.wait_ge(S("ssq_ln"), 5)
        tokens(5, [(0, META)])
        pe.wait_ge(S("ssq_ln"), 8)
        tokens(6, [xblk(0)])
        pe.wait_ge(S("g_made"), 1)
        pe.wait_ge(S("cw_out"), 1)
        mm(B[5][:, 0:8], C("upper"), G[:, 0:8], start=True, stop=True)
        mm(B[5][:, 8:9], C("mupper"), G[:, 8:9], start=True, stop=True)
        mm(B[5][:, 16:24], C("ones"), G[:, 0:8], start=True, stop=True)
        mm(B[5][:, 24:25], C("mones"), G[:, 8:9], start=True, stop=True).then_inc(S("dec_psum"), 1)
        pe.wait_ge(S("rows_made"), 1)
        pe.wait_ge(S("ba_out"), 3)
        for i, part in enumerate(PARTS):
            rhs_ = C("upper") if i < 2 else C("mupper")
            dst = B[4] if i == 0 else B[6] if i == 1 else B[7]
            for j, c in enumerate(range(part.start, part.stop)):
                last = mm(dst[:, j * P:(j + 1) * P], gB[:, c, :], rhs_, start=True, stop=True)
            last.then_inc(S("row_psum"), 1)
        for i, part in enumerate(PARTS):
            dst = (B[4], B[6], B[7])[i]
            pe.wait_ge(S("decay_rows"), i + 1)
            for j, c in enumerate(range(part.start, part.stop)):
                last = mm(dst[:, j * P:(j + 1) * P], bB[:, c, :], ident, start=True, stop=True)
            last.then_inc(S("row_psum"), 1)
        tokens(6, [xblk(1)])
        pe.wait_ge(S("normed"), 8)
        pe.wait_ge(S("proj_out"), 25)
        for i in range(NT):
            for h in range(DN_H):
                a = META + i * P
                last = tr(B[i][:, h * P:(h + 1) * P], conv_out[:, 4 + h, a:a + P], ident)
            last.then_inc(S("chunk_psum"), 1)
        for i in range(NT):
            for h in range(DN_H):
                a = META + i * P
                last = tr(B[2 + i][:, h * P:(h + 1) * P], conv_out[:, 8 + h, a:a + P], ident)
            last.then_inc(S("chunk_psum"), 1)
        pe.wait_ge(S("meta_stack"), 1)
        tr(B[5][:, 0:P], kTm, ident)
        tr(B[5][:, P:2 * P], vTm, ident).then_inc(S("chunk_psum"), 1)
        pe.wait_ge(S("lb_made"), 3)
        for i in range(NT):
            for h in range(DN_H):
                k_ = conv_out[:, 4 + h, META + i * P:META + (i + 1) * P]
                last = mm((B[4], B[6])[i][:, h * P:(h + 1) * P], k_, k_, start=True, stop=True)
            last.then_inc(S("chunk_psum"), 1)
        mm(B[7][:, 0:P], kTm, kTm, start=True, stop=True).then_inc(S("chunk_psum"), 1)
        for i in range(NT):
            pe.wait_ge(S("chunk_dve"), i + 1)
            for h in range(DN_H):
                a = META + i * P
                last = mm(B[i][:, h * P:(h + 1) * P], conv_out[:, 4 + h, a:a + P], conv_out[:, h, a:a + P], start=True, stop=True)
            last.then_inc(S("chunk_psum"), 1)
        pe.wait_ge(S("chunk_dve"), 8)
        pe.wait_ge(S("chunk_act"), 3)
        pe.wait_ge(S("inverse_start"), 1)
        for lv in range(LEVELS):
            for i, part in enumerate(PARTS):
                if lv:
                    pe.wait_ge(S("inv_step"), 3 * (lv - 1) + i + 1)
                for j, c in enumerate(range(part.start, part.stop)):
                    last = mm(B[i if i < 2 else 6][:, j * P:(j + 1) * P], AT[:, c, :], XI[:, c, :], start=True, stop=True)
                last.then_inc(S("inv_ax"), 1)
            for i, part in enumerate(PARTS):
                pe.wait_ge(S("inv_masked"), 3 * lv + i + 1)
                for j, c in enumerate(range(part.start, part.stop)):
                    mm((B[2], B[3], B[6][:, P:2 * P])[i][:, j * P:(j + 1) * P], XIT[:, c, :], TM[:, c, :], start=True, stop=True)
                for j, c in enumerate(range(part.start, part.stop)):
                    last = mm((B[4], B[5], B[6][:, 2 * P:3 * P])[i][:, j * P:(j + 1) * P], TM[:, c, :], XIT[:, c, :], start=True, stop=True)
                last.then_inc(S("inv_xax"), 1)
        pe.wait_ge(S("inv_step"), 3 * LEVELS)
        mm(B[0][:, 0:P], XIT[:, 8, :], vb[:, 8, :], start=True, stop=True).then_inc(S("step_psum"), 1)
        pe.wait_ge(S("v_out"), 1)
        for h in range(DN_H):
            last = mm(B[1 + h][:, 0:P], kdec[32 * h:32 * h + 32, 8, :], vnew[32 * h:32 * h + 32, 0, :], start=True, stop=True)
        last.then_inc(S("step_psum"), 1)
        for i in range(NT):
            a = META + i * P
            pe.wait_ge(S("state_first") if i == 0 else S("state_out"), 1)
            for h in range(DN_H):
                last = mm(B[0][:, h * P:(h + 1) * P], conv_out[:, 4 + h, a:a + P], state[:, h, :], start=True, stop=True)
            last.then_inc(S("step_psum"), 1)
            for h in range(DN_H):
                last = mm(B[5][:, h * P:(h + 1) * P], conv_out[:, h, a:a + P], state[:, h, :], start=True, stop=True)
            last.then_inc(S("step_psum"), 1)
            pe.wait_ge(S("rhs_made"), i + 1)
            for h in range(DN_H):
                last = mm(B[1][:, h * P:(h + 1) * P], XIT[:, 4 * i + h, :], rhs[:, h, :], start=True, stop=True)
            last.then_inc(S("step_psum"), 1)
            pe.wait_ge(S("v_out"), i + 2)
            if i < NT - 1:
                for h in range(DN_H):
                    last = mm(B[2][:, h * P:(h + 1) * P], kdec[:, 4 * i + h, :], vnew[:, h, :], start=True, stop=True)
                last.then_inc(S("step_psum"), 1)
            if i:
                pe.wait_ge(S("o_made"), i)
            for h in range(DN_H):
                last = mm(B[7][:, h * P:(h + 1) * P], QKT[:, 4 * i + h, :], vnew[:, h, :], start=True, stop=True)
            last.then_inc(S("step_psum"), 1)
        def head_qk(h):
            c, r = h // 2, 64 * (h % 2)
            return sbT[r:r + 64, c, META:L], sbT[r:r + 64, 4 + c, :]

        pe.wait_ge(S("o_decayed"), 2)
        pe.wait_ge(S("v_out"), 3)
        pe.wait_ge(S("state_out"), 1)
        pe.wait_ge(S("o_made"), 2)
        for g in range(4):
            for j in range(2):
                h = 2 * (2 * (g % 2) + j) + g // 2
                q_, k_ = head_qk(h)
                last = mm(B[g][:, j * SEQ:(j + 1) * SEQ], k_[:, META:META + P], q_, start=True, stop=True)
            last.then_inc(S("z_psum"), 1)
        for g in range(2):
            for j in range(4):
                q_, k_ = head_qk(2 * j + g)
                last = mm(B[4 + g][:, j * P:(j + 1) * P], k_[:, META + P:L], q_[:, P:SEQ], start=True, stop=True)
            last.then_inc(S("z_psum"), 1)
        for g in range(4):
            bk = B[(6, 0, 7, 1)[g]]
            if g == 1:
                pe.wait_ge(S("z_out"), 1)
            if g == 3:
                pe.wait_ge(S("z_out"), 2)
            for j in range(2):
                h = 2 * (2 * (g % 2) + j) + g // 2
                q_, k_ = head_qk(h)
                last = mm(bk[0:META, j * SEQ:(j + 1) * SEQ], k_[:, 0:META], q_, start=True, stop=True)
            last.then_inc(S("z_psum"), 1)
        pe.wait_ge(S("z_out"), 4)
        pe.wait_ge(S("zm_out"), 4)
        for u in range(7, 11):
            tokens(u, [xblk(0), xblk(1)])
        for i in range(NT):
            pe.wait_ge(S("o_normed"), i + 1)
            for k in range(4):
                last = tr(B[6 + i][:, k * P:(k + 1) * P], zs[:, i, k * P:(k + 1) * P], ident)
            last.then_inc(S("mix_psum"), 1)
        pe.wait_ge(S("z_out"), 6)
        pe.wait_ge(S("gate_out"), 8)
        pe.wait_ge(S("sp_made"), 1)
        pe.wait_ge(S("masked"), 2)
        for g in range(4):
            hs = slice(2 * g, 2 * g + 2)
            pair = cube(B[g], 2)
            mm(B[g], C("lower"), SP0[:, hs, :], start=True, stop=False)
            mm(pair[:, :, P:SEQ], C("ones"), SP1[:, hs, :], start=False, stop=True).then_inc(S("later_psum"), 1)
        for g in range(2):
            mm(B[4 + g], C("lower"), SP1[:, 4 * g:4 * g + 4, :], start=True, stop=True).then_inc(S("later_psum"), 1)
        for g in range(4):
            bk = B[(6, 7, 0, 1)[g]]
            if g == 0:
                pe.wait_ge(S("branch_in"), 2)
            if g >= 2:
                pe.wait_ge(S("later_out"), g - 1)
            hs = slice(2 * g, 2 * g + 2)
            mm(bk[0:META, :], C("lower", META, META), SPM[:, hs, :], start=True, stop=False)
            mm(bk[0:META, :], C("ones", P, META), SP0[:, hs, :], start=False, stop=False)
            mm(cube(bk[0:META, :], 2)[:, :, P:SEQ], C("ones", P, META), SP1[:, hs, :], start=False, stop=True).then_inc(S("later_psum"), 1)
        pe.wait_ge(S("masked"), 4)
        pe.wait_ge(S("w_made"), 3)
        for i in range(NT):
            for h in range(SB_H):
                hh = 4 * (h % 2) + h // 2
                vcol = slice(h * SB_D, (h + 1) * SB_D)
                o = B[2 + i][:, vcol]
                qs = slice(i * P, (i + 1) * P)
                mm(o, ZM[:, hh, qs], sbv[0:META, 2, vcol], start=True, stop=False)
                last = mm(o, Z0[:, hh, qs], sbv[:, 0, vcol], start=False, stop=(i == 0))
                if i:
                    last = mm(o, Z1[:, hh, :], sbv[:, 1, vcol], start=False, stop=True)
            last.then_inc(S("mix_psum"), 1)
        for i in range(NT):
            pe.wait_ge(S("sb_out"), i + 1)
            for k in range(4):
                last = tr(B[4 + i][:, k * P:(k + 1) * P], osb[:, i, k * P:(k + 1) * P], ident)
            last.then_inc(S("mix_psum"), 1)
        n = 0
        for u, src, ready in ((11, odT, 2), (12, osT, 4)):
            landed(pe, u)
            pe.wait_ge(S("branch_in"), ready)
            for i in range(NT):
                for half in range(2):
                    bk = B[(0, 1, 2, 3)[n % 4]]
                    if n >= 4:
                        pe.wait_ge(S("branch_out"), n - 3)
                    for k in range(4):
                        last = mm(bk, src[:, k, i * P:(i + 1) * P], slab(u, k, D)[:, half * 512:(half + 1) * 512], start=(k == 0), stop=(k == 3))
                    last.then_inc(S("branch"), 1)
                    n += 1
        pe.wait_ge(S("merged"), 2)
        transposes(1, [(gates[:, 0, 0, :], P, 0), (gates[:, 1, 0, :], P, P)])
        xT_ready(1)
        pe.wait_ge(S("branch_out"), 8)
        n = 0
        for half in range(2):
            landed(pe, 13 + half)
            for i in range(NT):
                for k in range(KD):
                    last = mm(B[n], xT[:, k, i * P:(i + 1) * P], slab(13 + half, k), start=(k == 0), stop=(k == KD - 1))
                last.then_inc(S("mixed"), 1)
                n += 1
        transposes(2, [(X1[:, 0, :], P, 0), (X1[:, 1, :], P, P)], "h1_made")
        xT_ready(2)
        pe.wait_ge(S("router_in"), 16 * (NG + 3))
        for i in range(NT):
            for k in range(KD):
                last = mm(B[0][:, 64 * i:64 * i + 36], xT[:, k, i * P:(i + 1) * P], wr[:, k, :], start=(k == 0), stop=(k == KD - 1))
        last.then_inc(S("router_psum"), 1)
        pe.wait_ge(S("router_dve"), 2)
        mm(B[1][:, 0:NG], C("strict"), oh[:, 0, :], start=True, stop=True)
        mm(B[1][:, NG:2 * NG], C("strict"), oh[:, 1, :], start=True, stop=False)
        mm(B[1][:, NG:2 * NG], C("ones"), oh[:, 0, :], start=False, stop=True)
        mm(B[1][:, 2 * NG:3 * NG], C("ones"), oh[:, 0, :], start=True, stop=False)
        mm(B[1][:, 2 * NG:3 * NG], C("ones"), oh[:, 1, :], start=False, stop=True).then_inc(S("router_psum"), 1)

        def gather(s_):
            pe.wait_ge(S("sel_made"), s_ + 1)
            if not isinstance(s_, int):
                pe.wait_ge(S("selT_out"), s_)
            for k in range(KD):
                for i in range(NT):
                    last = mm(B[5 + k // 4][:, (k % 4) * P:(k % 4 + 1) * P], X1[:, i, k * P:(k + 1) * P], sel[:, i, :], start=(i == 0), stop=(i == NT - 1))
            last.then_inc(S("gather_psum"), 1)
            for i in range(NT):
                mm(B[7][:, 0:NE], sel[:, i, :], cmb[:, i, :], start=(i == 0), stop=(i == NT - 1))
            for i in range(NT):
                last = tr(B[7][:, (i + 1) * P:(i + 2) * P], sel[:, i, :], ident)
            last.then_inc(S("sel_psum"), 1)

        def experts(s_, over_=False):
            pe.wait_ge(S("xs_out"), s_ + 1)
            for e in range(NE + 2):
                if e < NE:
                    pe.wait_ge(S("gu_lo"), s_ * 2 * NE + 2 * (e + 1))
                    pe.wait_ge(S("scat_out" if e < 2 else "hid"), s_ * 4 + 1 if e < 2 else s_ * NE + (e - 1))
                    w_hi, w_lo = ehi[:, e % E_BUF, :], wlo[:, gu_slot(e), :]
                    for k in range(KD):
                        for n, (x_, w_) in enumerate(((xsH, w_hi), (xsH, w_lo), (xsL, w_hi))):
                            last = mm(B[e % 2], x_[:, k, :], w_[:, k * 512:(k + 1) * 512], start=(k == 0 and n == 0), stop=(k == KD - 1 and n == 2))
                    last.then_inc(S("gu"), 1)
                if e >= 2:
                    d = e - 2
                    pe.wait_ge(S(f"down_landed{d % 2}"), s_ * 16 * (NE // 2) + 16 * (d // 2 + 1))
                    pe.wait_ge(S("hT_out"), s_ * NE + (d + 1))
                    for half in range(2):
                        for k in range(2):
                            a = k * D + half * 512
                            last = mm(B[2 + half], hT[:, d % 2, k * P:(k + 1) * P], down_w[:, d % 2, a:a + 512], start=(d == 0 and k == 0), stop=(d == NE - 1 and k == 1))
                    last.then_inc(S("down"), 1)
                if 1 <= e <= NE:
                    h = e - 1
                    pe.wait_ge(S("hid"), s_ * NE + (h + 1))
                    for k in range(2):
                        last = tr(B[4][:, k * P:(k + 1) * P], hid[:, h % 2, k * P:(k + 1) * P], ident)
                    last.then_inc(S("hT_psum"), 1)
                if e == NE - 1 and not over_:
                    gather(s_ + 1)
            pe.wait_ge(S("y_dve"), s_ + 1)
            pe.wait_ge(S("y_act"), s_ + 1)
            pe.wait_ge(S("selT_out"), s_ + 1)
            for q in range(4):
                if q >= 2:
                    pe.wait_ge(S("scat_out"), s_ * 4 + q)
                mm(B[q % 2], selT[:, (q // 2) * P:(q // 2 + 1) * P], ysb[:, (q % 2) * 512:(q % 2 + 1) * 512], start=True, stop=True).then_inc(S("scat"), 1)

        gather(0)
        with pe.Fori(0, NG) as s_:
            experts(s_)
        pe.wait_ge(S("over_made"), 1)
        flag = pe.value_load(ovi[0:1, 0:1], min_val=0, max_val=1)
        with pe.If(flag):
            experts(NG, True)
        def split_transposes(call, nth, made):
            pe.wait_ge(S("xn_made"), made)
            xT_ready(call - 1)
            for k in range(KD):
                if k >= 2:
                    pe.wait_ge(S("xT_split"), KD * nth + k - 1)
                for i in range(NT):
                    last = tr(B[6 + k % 2][:, i * P:(i + 1) * P], X1[:, i, k * P:(k + 1) * P], ident)
                last.then_inc(S("xT_psum"), 1)
            pe.wait_ge(S("xT_split"), KD * (nth + 1))

        def attention():
            split_transposes(3, 0, 2)
            for n in range(12):
                u, i = n // 2, n % 2
                if i == 0:
                    pe.wait_ge(S("qkv_lo" if u < 2 else "split_lo"), 2 * (u % 2 + 1) + (4 if u >= 4 else 0))
                w_hi, w_lo = whi[:, u % 2, :], wlo[:, (U_TWO + u) % SLOTS, :]
                if n >= 4:
                    pe.wait_ge(S("qkv_out"), n - 3)
                for k in range(KD):
                    for x_, w_, p_ in ((xTH, w_hi, 0), (xTH, w_lo, 1), (xTL, w_hi, 2)):
                        last = mm(B[n % 4], x_[:, k, i * P:(i + 1) * P], w_[:, k * 512:(k + 1) * 512], start=(k == 0 and p_ == 0), stop=(k == KD - 1 and p_ == 2))
                last.then_inc(S("qkv"), 1)
            for g in range(8):
                if g == 0:
                    pe.wait_ge(S("rope_made"), 2)
                if g >= 4:
                    pe.wait_ge(S("qkT_act" if g % 2 == 0 else "qkT_dve"), g // 2 - 1)
                for j in range(2):
                    for i in range(NT):
                        last = tr(B[4 + g % 4][:, (2 * j + i) * P:(2 * j + i + 1) * P], qk[:, i, (2 * g + j) * P:(2 * g + j + 1) * P], ident)
                last.then_inc(S("att_psum"), 1)
            pe.wait_ge(S("qkT_act"), 4)
            pe.wait_ge(S("qkT_dve"), 4)
            for h in range(AT_H):
                pe.wait_ge(S("qkv_out"), 12)
                if h >= 4:
                    pe.wait_ge(S("scores_out"), h - 3)
                mm(B[h % 4][:, 0:P], qkT[:, h, 0:P], qkT[:, 8 + h, 0:P], start=True, stop=True)
                mm(B[h % 4][:, P:3 * P], qkT[:, h, P:SEQ], qkT[:, 8 + h, :], start=True, stop=True).then_inc(S("att_psum"), 1)
            for h in range(AT_H):
                pe.wait_ge(S("p_made"), h + 1)
                if h >= 4:
                    pe.wait_ge(S("pT_out"), h - 3)
                for j in range(3):
                    last = tr(B[4 + h % 4][:, j * P:(j + 1) * P], sc_[:, h, j * P:(j + 1) * P], ident)
                last.then_inc(S("att_psum"), 1)
            pe.wait_ge(S("scores_out"), 8)
            for h in range(AT_H):
                pe.wait_ge(S("pT_out"), h + 1)
                o, v = slice((h % 4) * P, (h % 4 + 1) * P), slice(h * P, (h + 1) * P)
                mm(B[h // 4][:, o], pT[:, h, 0:P], vv[:, 0, v], start=True, stop=True)
                mm(B[2 + h // 4][:, o], pT[:, h, P:2 * P], vv[:, 0, v], start=True, stop=False)
                mm(B[2 + h // 4][:, o], pT[:, h, 2 * P:3 * P], vv[:, 1, v], start=False, stop=True).then_inc(S("att_psum"), 1)
            transposes(4, [(qk[:, 0, :], P, 0), (qk[:, 1, :], P, P)], "att_made")
            xT_ready(4)
            for n in range(4):
                half, i = n // 2, n % 2
                u = U_TWO + 6 + half
                if i == 0:
                    landed(pe, u)
                for k in range(KD):
                    last = mm(B[n], xT[:, k, i * P:(i + 1) * P], slab(u, k), start=(k == 0), stop=(k == KD - 1))
                last.then_inc(S("att_o"), 1)

        def mlp(m):
            base = mlp_base[m]
            split_transposes(5 + 2 * m, 1 + m, 4 * (m + 1))

            def ready(q, jj):
                pe.wait_ge(S("split_lo"), 8 + jj * 8 + 2 * (16 * m + q + 1))
                return whi[:, q % 2, :], wlo[:, (base + q) % SLOTS, :]

            def up(q, j, jj=0, wait=True):
                w_hi, w_lo = ready(q, jj)
                for pr in range(2):
                    if wait:
                        pe.wait_ge(S("relu"), jj * 4 + (16 * m + 2 * j + pr - 3))
                    for cc in range(2):
                        c = 2 * pr + cc
                        for k in range(KD):
                            for w_, x_, n in ((w_hi, xTH, 0), (w_hi, xTL, 1), (w_lo, xTH, 2)):
                                last = mm(B[4 + (2 * j + pr) % 4][:, cc * SEQ:(cc + 1) * SEQ], w_[:, k * 512 + c * P:k * 512 + (c + 1) * P], x_[:, k, 0:SEQ],
                                          start=(k == 0 and n == 0), stop=(k == KD - 1 and n == 2))
                    last.then_inc(S("up"), 1)

            def down(q, j, jj=0, first=False, final=False):
                w_hi, w_lo = ready(q, jj)
                pe.wait_ge(S("squared"), jj * 4 + (16 * m + 2 * j + 2))
                for n in range(4):
                    i, half = n // 2, n % 2
                    for c in range(4):
                        for h_, w_, p_ in ((hidH, w_hi, 0), (hidH, w_lo, 1), (hidL, w_hi, 2)):
                            last = mm(B[n], h_[:, j % 2, c, i * P:(i + 1) * P], w_[:, c * D + half * 512:c * D + (half + 1) * 512],
                                      start=(first and c == 0 and p_ == 0), stop=(final and c == 3 and p_ == 2))
                    if final or n == 3:
                        last.then_inc(S("mlp_down"), 1)

            up(0, 0, wait=False)
            up(1, 1, wait=False)
            down(2, 0, first=True)
            with pe.Fori(0, 3) as jj:
                up(3, 2, jj)
                down(4, 1, jj)
                up(5, 3, jj)
                down(6, 2, jj)
            down(15, 7, final=True)

        attention()
        pe.wait_ge(S("res"), 2)
        mlp(0)
        pe.wait_ge(S("bands_in"), 16)
        pe.wait_ge(S("xn_made"), 6)
        pe.wait_ge(S("relu"), 16)
        for c in range(KD):
            g = c // 2
            if c >= 2:
                pe.wait_ge(S("xT_act" if c % 2 == 0 else "xT_dve"), 24 + c // 2)
            cols = slice(c * P, (c + 1) * P)
            mm(B[6 + c % 2][:, 0:P], X1[:, 0, cols], bands[:, g, 0, :], start=True, stop=True)
            mm(B[6 + c % 2][:, P:SEQ], X1[:, 0, cols], bands[:, g, 2, :], start=True, stop=False)
            mm(B[6 + c % 2][:, P:SEQ], X1[:, 1, cols], bands[:, g, 1, :], start=False, stop=True).then_inc(S("xT_psum"), 1)
        xT_ready(6)
        landed(pe, U_POOL)
        for n in range(4):
            i = n // 2
            for g in (2 * (n % 2), 2 * (n % 2) + 1):
                for k in range(2):
                    last = mm(B[n][:, (g % 2) * FF:(g % 2 + 1) * FF], xT[:, 2 * g + k, i * P:(i + 1) * P], slab(U_POOL, 2 * g + k, FF), start=(k == 0), stop=(k == 1))
            last.then_inc(S("pooled"), 1)
        pe.wait_ge(S("res"), 6)
        mlp(1)

    @block.scalar
    def _(sc):
        line = Line(sc, "act_line")

        def xT_copies(call, width):
            for k in range(0, KD, 2):
                sc.wait_ge(S("xT_psum"), KD * call + k + 1)
                act(xT[:, k, 0:width], B[6][:, 0:width], ACT.Copy).then_inc(S("xT_act"), 1)

        def root(n, cols, out, scale, eps):
            line(act(lnv[:, 0:n], cols, ACT.Ln, scale=scale, bias=eps))
            return act(out, lnv[:, 0:n], ACT.Exp, scale=-0.5)

        sc.wait_ge(S("cst_in"), 16)
        for i in range(3):
            r = META if i == 0 else P
            sc.wait_ge(S("var"), i + 1)
            line(act(lnv[0:r, i:i + 1], mv[0:r, i, 1:2], ACT.Ln, bias=C("eps5", r)))
        for i in range(3):
            r = META if i == 0 else P
            act(rst[0:r, i:i + 1], lnv[0:r, i:i + 1], ACT.Exp, scale=-0.5).then_inc(S("rstd"), 1)
        xT_copies(0, L)
        sc.wait_ge(S("raw_pad"), 1)
        for c in range(N_DN):
            sc.wait_ge(S("proj"), c + 1)
            act(raw[:, c, 3:3 + L], B[c % 4][:, 0:L], ACT.Copy).then_inc(S("proj_out"), 1)
            if c >= 2:
                sc.wait_ge(S("conv"), c - 1)
                act(conv_out[:, c - 2, :], conv_out[:, c - 2, :], ACT.Silu).then_inc(S("silu"), 1)
        for c in (N_DN - 2, N_DN - 1):
            sc.wait_ge(S("conv"), c + 1)
            act(conv_out[:, c, :], conv_out[:, c, :], ACT.Silu).then_inc(S("silu"), 1)
        sc.wait_ge(S("ba_out"), 3)
        act(be, ba[:, :, 0:DN_H], ACT.Exp, scale=-1.0).then_inc(S("be_exp"), 1)
        sc.wait_ge(S("ga_abs"), 1)
        line(act(gt, gt, ACT.Exp, scale=-1.0))
        act(gt, gt, ACT.Ln, bias=C("one")).then_inc(S("ga_ln"), 1)
        sc.wait_ge(S("dn_small_in"), 48)
        act(alog, alog, ACT.Exp).then_inc(S("ga_ln"), 1)
        for c in range(8):
            sc.wait_ge(S("proj"), N_DN + c + 1)
            act(sbT[:, c, :], B[(N_DN + c) % 4][:, 0:L], ACT.Copy, scale=(SB_D ** -0.5 if c < 4 else 1.0)).then_inc(S("proj_out"), 1)
        for c in range(8):
            sc.wait_ge(S("ssq_psum"), c + 1)
            act(sq[:, c, :], SSQ_BANK[c % 4][:, 0:L], ACT.Ln, bias=C("eps6")).then_inc(S("ssq_ln"), 1)
        for c in range(8):
            sc.wait_ge(S("ssq_ln"), c + 1)
            act(sq[:, c, :], sq[:, c, :], ACT.Exp, scale=-0.5).then_inc(S("rnorm"), 1)
        sc.wait_ge(S("dec_out"), 1)
        act(ED, DEC, ACT.Exp)
        act(KF, KF, ACT.Exp)
        act(CD, DL, ACT.Exp).then_inc(S("dec_exp"), 1)
        for i, part in enumerate(PARTS):
            sc.wait_ge(S("decay_rows"), i + 1)
            act(LM[:, part, :], LM[:, part, :], ACT.Exp).then_inc(S("lm_exp"), 1)
        for n, (dst, r, f) in enumerate([(sbv[:, 0, :], P, ACT.Copy), (sbv[:, 1, :], P, ACT.Copy), (sbv[0:META, 2, :], META, ACT.Copy),
                                         (zs[:, 0, :], P, ACT.Silu), (zs[:, 1, :], P, ACT.Silu)]):
            sc.wait_ge(S("proj"), N_FM + n + 1)
            act(dst, B[(N_FM + n) % 4][0:r, :], f).then_inc(S("proj_out"), 1)
        for i in range(NT):
            sc.wait_ge(S("chunk_psum"), i + 3)
            for h in range(DN_H):
                c = 4 * i + h
                last = act(vb[:, c, :], B[2 + i][:, h * P:(h + 1) * P], ACT.Copy, scale=BE[:, c:c + 1])
            last.then_inc(S("chunk_act"), 1)
        sc.wait_ge(S("chunk_dve"), 3)
        act(vb[:, 8, :], B[5][:, P:2 * P], ACT.Copy, scale=BE[:, 8:9]).then_inc(S("chunk_act"), 1)
        sc.wait_ge(S("step_psum"), 1)
        act(vnew[:, 0, :], B[0][:, 0:P], ACT.Copy).then_inc(S("v_out"), 1)
        sc.wait_ge(S("step_psum"), 2)
        for h in range(DN_H):
            last = act(state[:, h, :], B[1 + h][:, 0:P], ACT.Copy)
        last.then_inc(S("state_first"), 1)
        for i in range(NT):
            sc.wait_ge(S("step_psum"), 5 * i + 4)
            for h in range(DN_H):
                c = 4 * i + h
                last = act(odec[i][:, h, :], B[5][:, h * P:(h + 1) * P], ACT.Copy, scale=ED[:, c:c + 1])
            last.then_inc(S("o_decayed"), 1)
            sc.wait_ge(S("step_psum"), 5 * i + 5)
            act(flat(vnew), B[1], ACT.Copy).then_inc(S("v_out"), 1)
        for i in range(NT):
            sc.wait_ge(S("o_made"), i + 1)
            for h in range(DN_H):
                line(act(junk[:, h, :], odec[i][:, h, :], ACT.Square, accum_out=ssq[:, 4 * i + h:4 * i + h + 1]))
            root(4, ssq[:, 4 * i:4 * i + 4], rsd[:, 4 * i:4 * i + 4], 1.0 / 128, C("eps6")).then_inc(S("o_rstd"), 1)
        for g in range(4):
            sc.wait_ge(S("z_psum"), g + 7)
            act(ZM[:, 2 * g:2 * g + 2, :], cube(B[(6, 0, 7, 1)[g]][0:META, :], 2), ACT.Copy).then_inc(S("zm_out"), 1)
        sc.wait_ge(S("z_out"), 4)
        sc.wait_ge(S("z_out"), 6)
        sc.wait_ge(S("zm_out"), 4)
        for f, kw in ((ACT.Abs, {}), (ACT.Exp, {"scale": -1.0}), (ACT.Ln, {"bias": None})):
            src, srm = (Z[:, 0:3072], Z[0:META, 3072:5120]) if f is ACT.Abs else (SP[:, 0:3072], SP[0:META, 3072:5120])
            kb = {"bias": C("one")} if "bias" in kw else kw
            km = {"bias": C("one", META)} if "bias" in kw else kw
            line(act(SP[:, 0:3072], src, f, **kb))
            if f is ACT.Ln:
                act(SP[0:META, 3072:5120], srm, f, **km).then_inc(S("sp_ln"), 1)
            else:
                line(act(SP[0:META, 3072:5120], srm, f, **km))
        for n in range(8):
            u, i = n // 2, n % 2
            g_ = gates[:, i, u // 2, (u % 2) * 512:(u % 2 + 1) * 512]
            sc.wait_ge(S("gate_out"), n + 1)
            act(g_, g_, ACT.Sigmoid).then_inc(S("gate_sig"), 1)
        for i in range(NT):
            sc.wait_ge(S("mix_psum"), i + 1)
            act(odT[:, :, i * P:(i + 1) * P], cube(B[6 + i], 4), ACT.Copy).then_inc(S("branch_in"), 1)
        sc.wait_ge(S("later_out"), 4)
        act(Z[:, 0:2048], Z[:, 0:2048], ACT.Exp).then_inc(S("w_made"), 1)
        sc.wait_ge(S("later_out"), 6)
        act(Z[:, 2048:3072], Z[:, 2048:3072], ACT.Exp).then_inc(S("w_made"), 1)
        sc.wait_ge(S("later_out"), 10)
        act(Z[0:META, 3072:5120], Z[0:META, 3072:5120], ACT.Exp).then_inc(S("w_made"), 1)
        for i in range(NT):
            sc.wait_ge(S("mix_psum"), i + 5)
            act(osT[:, :, i * P:(i + 1) * P], cube(B[4 + i], 4), ACT.Copy).then_inc(S("branch_in"), 1)
        xT_copies(1, SEQ)
        def deviations(n):
            sc.wait_ge(S("var"), n)
            line(act(lnv[:, 1:3].unsqueeze(2), mv[:, 1:3, 1:2], ACT.Ln, bias=C("eps5")))
            act(rst[:, 1:3], lnv[:, 1:3], ACT.Exp, scale=-0.5).then_inc(S("rstd"), 2)

        deviations(5)
        xT_copies(2, SEQ)
        sc.wait_ge(S("router_dve"), 1)
        act(gd, gd, ACT.Exp).then_inc(S("router_act"), 1)
        sc.wait_ge(S("router_dve"), 3)
        act(w2, w2, ACT.Exp).then_inc(S("router_act"), 1)

        def gathered(s_):
            sc.wait_ge(S("gather_psum"), s_ + 1)
            act(flat(xsH[:, 0:4, :]), B[5], ACT.Copy)
            act(flat(xsH[:, 4:8, :]), B[6], ACT.Copy).then_inc(S("xs_round"), 1)

        def gu_hi(s_, e, over_=False, first=False):
            gu_landed(sc, s_, e, over_)
            if not first:
                sc.wait_ge(S("gu"), s_ * NE + (e - 1))
            w_ = ring[:, gu_slot(e), :]
            for i in range(2):
                half = slice(i * HALF_U, (i + 1) * HALF_U)
                act(ehi[:, e % E_BUF, half], w_[:, half], ACT.Copy).then_inc(S("gu_hi"), 1)

        def experts(s_, over_=False, more=True):
            for e in range(NE + 1):
                if e < NE:
                    sc.wait_ge(S("gu"), s_ * NE + (e + 1))
                    if e >= 2:
                        sc.wait_ge(S("hid"), s_ * NE + (e - 1))
                    act(sg[:, e % 2, :], B[e % 2][:, 0:FF], ACT.Silu).then_inc(S("sg_made"), 1)
                    if e < NE - 2:
                        gu_hi(s_, e + 2, over_)
                    elif more:
                        gu_hi(s_ + 1, e + 2 - NE)
                if e == NE and not over_:
                    gathered(s_ + 1)
                if e >= 1:
                    h = e - 1
                    sc.wait_ge(S("hT_psum"), s_ * NE + (h + 1))
                    if h >= 2:
                        sc.wait_ge(S("down"), s_ * NE + (h - 1))
                    act(hT[:, h % 2, :], B[4][:, 0:FF], ACT.Copy).then_inc(S("hT_out"), 1)
            sc.wait_ge(S("down"), s_ * NE + NE)
            act(ysb[:, 512:1024], B[3], ACT.Copy).then_inc(S("y_act"), 1)

        for e in range(2):
            gu_hi(0, e, first=True)
        gathered(0)
        with sc.Fori(0, NG - 1) as s_:
            experts(s_)
        experts(NG - 1, more=False)
        sc.wait_ge(S("over_made"), 1)
        flag = sc.value_load(ovi[0:1, 0:1], min_val=0, max_val=1)
        with sc.If(flag):
            for e in range(2):
                gu_hi(NG, e, True)
            experts(NG, True, more=False)

        def hi_halves(u, n):
            for i in range(2):
                half = slice(i * HALF_U, (i + 1) * HALF_U)
                act(whi[:, n % 2, half], slot(u)[:, half], ACT.Copy).then_inc(S("split_hi"), 1)

        def qkv_hi(u):
            landed(sc, U_TWO + u)
            if u >= 2:
                sc.wait_ge(S("qkv"), 2 * (u - 1))
            hi_halves(U_TWO + u, u)

        def xT_round(call):
            for k in range(0, KD, 2):
                sc.wait_ge(S("xT_psum"), KD * call + k + 1)
                act(xTH[:, k, 0:SEQ], B[6][:, 0:SEQ], ACT.Copy).then_inc(S("xT_act"), 1)

        qkv_hi(0)
        deviations(7)
        qkv_hi(1)

        def mean_square(r, ready, count):
            for i in range(NT):
                sc.wait_ge(S(ready), count + i + 1)
                line(act(X1[:, i, :], X0[:, i, :], ACT.Square, accum_out=ssq[:, i:i + 1]))
            root(NT, ssq[:, 0:NT], rsd[:, 0:NT], 1.0 / D, C("eps6")).then_inc(S("rms"), 1)

        sc.wait_ge(S("turned"), 1)
        act(sine, sine, ACT.Sin)
        act(cosine, cosine, ACT.Sin).then_inc(S("sines"), 1)
        mean_square(0, "h2_made", 0)
        xT_round(3)
        for n in range(12):
            u, i = n // 2, n % 2
            sc.wait_ge(S("qkv"), n + 1)
            dst = qk[:, i, u * 512:(u + 1) * 512] if u < 4 else vv[:, i, (u - 4) * 512:(u - 3) * 512]
            act(dst, B[n % 4], ACT.Copy).then_inc(S("qkv_out"), 1)
            if i == 1 and u < 4:
                qkv_hi(u + 2)
        for g in range(0, 8, 2):
            sc.wait_ge(S("att_psum"), g + 1)
            act(flat(qkT[:, 2 * g:2 * g + 2, :]), B[4 + g % 4], ACT.Copy).then_inc(S("qkT_act"), 1)
        for h in range(AT_H):
            sc.wait_ge(S("max_made"), h // 4 + 1)
            act(sc_[:, h, 0:P], sc_[:, h, 0:P], ACT.Exp, bias=mxs[:, 0, h:h + 1], accum_out=sums[:, 0, h:h + 1])
            act(sc_[:, h, P:3 * P], sc_[:, h, P:3 * P], ACT.Exp, bias=mxs[:, 1, h:h + 1], accum_out=sums[:, 1, h:h + 1]).then_inc(S("p_made"), 1)
        xT_copies(4, SEQ)

        def split_hi(m, q, jj=0, first=None):
            u = mlp_base[m] + q
            sc.wait_ge(S(f"landed{u % SLOTS}"), jj * 32 + 32 * (u // SLOTS + 1))
            if first is None:
                name, count = freed[u - 2]
                sc.wait_ge(S(name), jj * (4 if name == "up" else 2) + count)
            elif q == 0:
                sc.wait_ge(S(first[0]), first[1])
            hi_halves(u, q)

        def mlp(m):
            xT_round(5 + 2 * m)

            def relu(j, jj=0):
                for pr in range(2):
                    n = 16 * m + 2 * j + pr
                    sc.wait_ge(S("up"), jj * 4 + (n + 1))
                    if n >= 2:
                        sc.wait_ge(S("squared"), jj * 4 + (n - 1))
                    act(relu_t[:, pr, :], B[4 + (2 * j + pr) % 4], ACT.Relu).then_inc(S("relu"), 1)

            relu(0)
            split_hi(m, 2)
            relu(1)
            split_hi(m, 3)
            with sc.Fori(0, 3) as jj:
                split_hi(m, 4, jj)
                relu(2, jj)
                split_hi(m, 5, jj)
                split_hi(m, 6, jj)
                relu(3, jj)
                split_hi(m, 7, jj)

        for q in range(2):
            split_hi(0, q, first=("att_psum", 32))
        mean_square(1, "res", 0)
        mlp(0)
        mean_square(2, "res", 2)
        for k in range(0, KD, 2):
            sc.wait_ge(S("xT_psum"), KD * 6 + k + 1)
            act(xT[:, k, 0:SEQ], B[6][:, 0:SEQ], ACT.Copy).then_inc(S("xT_act"), 1)
        for q in range(2):
            split_hi(1, q, first=("mlp_down", 11))
        mean_square(3, "res", 4)
        mlp(1)
        mean_square(4, "res", 6)

    @block.vector
    def _(dve):
        line = Line(dve, "dve_line")

        def xT_copies(call, width):
            for k in range(1, KD, 2):
                dve.wait_ge(S("xT_psum"), KD * call + k + 1)
                nc.vector.tensor_copy(xT[:, k, 0:width], B[7][:, 0:width]).then_inc(S("xT_dve"), 1)

        def moments(i, x, r):
            for j in range(2):
                line(nc.vector.bn_stats(stats[0:r, i, j, :], x[:, j * 512:(j + 1) * 512]))
            nc.vector.bn_aggr(mv[0:r, i, :], stats[0:r, i, :, :].rearrange("p a b -> p (a b)")).then_inc(S("var"), 1)

        def centered(x, out, i, r, g, var):
            dve.wait_ge(S("var"), var)
            line(stt(out, x, mv[0:r, i, 0:1], params[0:r, g, :], ALU.subtract, ALU.mult))

        def scaled(out, i, r, b):
            return stt(out, out, rst[0:r, i:i + 1], params[0:r, b, :], ALU.mult, ALU.add)

        tiles = [(xmeta[:, :], META, "meta_in"), (X0[:, 0, :], P, "x0_in"), (X0[:, 1, :], P, "x1_in")]
        for i, (x, r, sem) in enumerate(tiles):
            dve.wait_ge(S(sem), 16)
            moments(i, x, r)
        dve.wait_ge(S("emb_in"), 32)
        for i, (x, r, sem) in enumerate(tiles):
            centered(x, x, i, r, 0, i + 1)
        for i, (x, r, sem) in enumerate(tiles):
            dve.wait_ge(S("rstd"), i + 1)
            scaled(x, i, r, 1).then_inc(S("embedded"), 1)
        xT_copies(0, L)
        dve.wait_ge(S("ba_psum"), 1)
        nc.vector.tensor_copy(cw.rearrange("p j c -> p (j c)"), B[5][:, 0:48]).then_inc(S("cw_out"), 1)
        dve.wait_ge(S("cw_out"), 1)
        for c in range(N_DN):
            dve.wait_ge(S("proj_out"), c + 1)
            line(ts(conv_out[:, c, :], raw[:, c, 0:L], cw[:, 0, c:c + 1], None, ALU.mult))
            for j in range(1, CONV):
                ins = stt(conv_out[:, c, :], raw[:, c, j:j + L], cw[:, j, c:c + 1], conv_out[:, c, :], ALU.mult, ALU.add)
                if j < CONV - 1:
                    line(ins)
            ins.then_inc(S("conv"), 1)
        dve.wait_ge(S("ba_psum"), 2)
        nc.vector.tensor_copy(ba[:, 0:2, :], cube(B[4][:, 0:16], 2)).then_inc(S("ba_out"), 1)
        nc.vector.tensor_copy(ba[0:META, 2, :], B[4][0:META, 16:24]).then_inc(S("ba_out"), 1)
        dve.wait_ge(S("ba_psum"), 3)
        nc.vector.tensor_copy(ba[:, 2, :], B[4][:, 32:40]).then_inc(S("ba_out"), 1)
        dve.wait_ge(S("ba_out"), 3)
        dve.wait_ge(S("dn_small_in"), 48)
        line(tt(gu, ba[:, :, DN_H:2 * DN_H], dtb.unsqueeze(1).broadcast_to([P, 3, DN_H]), ALU.add))
        stt(gt, gu, -1.0, gu, ALU.mult, ALU.max).then_inc(S("ga_abs"), 1)
        dve.wait_ge(S("be_exp"), 1)
        line(ts(be, be, 1.0, None, ALU.add))
        line(nc.vector.reciprocal(be, be))
        dve.wait_ge(S("ga_ln"), 2)
        line(stt(gu, gu, 0.0, gt, ALU.max, ALU.add))
        line(stt(ge, gu, -1.0, alog.unsqueeze(1).broadcast_to([P, 3, DN_H]), ALU.mult, ALU.mult))
        for src, dst in ((ge, G), (be, BE)):
            nc.vector.tensor_copy(dst[:, 0:8], src[:, 0:2, :].rearrange("p t h -> p (t h)"))
            line(tt(gt[:, 0, :], src[:, 2, :], C("hmask"), ALU.mult))
            line(nc.vector.reduce_sum(dst[:, 8:9], gt[:, 0, :], AX.X))
        dve.nop().then_inc(S("g_made"), 1)
        for dst, src in ((gB, G), (bB, BE)):
            for c in range(NM):
                last = ts(dst[:, c, :], C("ones"), src[:, c:c + 1], None, ALU.mult)
        last.then_inc(S("rows_made"), 1)
        for c in range(8):
            dve.wait_ge(S("rnorm"), c + 1)
            stt(conv_out[:, c, :], conv_out[:, c, :], (128 ** -0.5 if c < 4 else 1.0), sq[:, c, :], ALU.mult, ALU.mult).then_inc(S("normed"), 1)
        dve.wait_ge(S("dec_psum"), 1)
        nc.vector.tensor_copy(DEC, B[5][:, 0:NM])
        line(nc.vector.tensor_copy(DL, B[5][:, 16:16 + NM]))
        tt(KF, DL, DEC, ALU.subtract).then_inc(S("dec_out"), 1)
        rowbank = (B[4], B[6], B[7])
        for i, part in enumerate(PARTS):
            dve.wait_ge(S("row_psum"), i + 1)
            for j, c in enumerate(range(part.start, part.stop)):
                last = ts(LM[:, c, :], rowbank[i][:, j * P:(j + 1) * P], DEC[:, c:c + 1], 0.0, ALU.subtract, ALU.min)
            last.then_inc(S("decay_rows"), 1)
        dve.wait_ge(S("dec_exp"), 1)
        line(stt(NBE, BE, -1.0, ED, ALU.mult, ALU.mult))
        for i, part in enumerate(PARTS):
            n = part.stop - part.start
            dve.wait_ge(S("lm_exp"), i + 1)
            line(tt(LM[:, part, :], LM[:, part, :], masks("upper" if i < 2 else "mupper", n), ALU.mult))
            dve.wait_ge(S("row_psum"), i + 4)
            tt(flat(LB[:, part, :]), flat(LM[:, part, :]), rowbank[i][:, 0:n * P], ALU.mult).then_inc(S("lb_made"), 1)
        for i in range(NT):
            dve.wait_ge(S("chunk_psum"), i + 1)
            for h in range(DN_H):
                c = 4 * i + h
                last = ts(kdec[:, c, :], B[i][:, h * P:(h + 1) * P], KF[:, c:c + 1], None, ALU.mult)
            last.then_inc(S("chunk_dve"), 1)
        dve.wait_ge(S("chunk_psum"), 5)
        ts(kdec[:, 8, :], B[5][:, 0:P], KF[:, 8:9], None, ALU.mult).then_inc(S("chunk_dve"), 1)
        dve.wait_ge(S("lb_made"), 3)
        for i, part in enumerate(PARTS):
            dve.wait_ge(S("chunk_psum"), i + 6)
            n = part.stop - part.start
            tt(flat(AT[:, part, :]), rowbank[i][:, 0:n * P], flat(LB[:, part, :]), ALU.mult).then_inc(S("chunk_dve"), 1)
        for i in range(NT):
            dve.wait_ge(S("chunk_psum"), i + 9)
            tt(flat(QKT[:, PARTS[i], :]), B[i], flat(LM[:, PARTS[i], :]), ALU.mult).then_inc(S("chunk_dve"), 1)
        dve.wait_ge(S("proj_out"), 25)
        dve.wait_ge(S("dn_small_in"), 48)
        for i in range(NT):
            last = tt(cube(zs[:, i, :], 4), cube(zs[:, i, :], 4), dng[:, :].unsqueeze(1).broadcast_to([P, 4, P]), ALU.mult)
        line(last)
        dve.wait_ge(S("inverse_start"), 1)
        for lv in range(LEVELS):
            for i, part in enumerate(PARTS):
                n = part.stop - part.start
                dve.wait_ge(S("inv_ax"), 3 * lv + i + 1)
                tt(TM[:, part, :], cube(B[i if i < 2 else 6][:, 0:n * P], n), masks(f"level{lv}", n), ALU.mult).then_inc(S("inv_masked"), 1)
            for i, part in enumerate(PARTS):
                n = part.stop - part.start
                dve.wait_ge(S("inv_xax"), 3 * lv + i + 1)
                if lv:
                    dve.wait_ge(S("inv_step"), 3 * (lv - 1) + i + 1)
                tt(flat(XI[:, part, :]), flat(XI[:, part, :]), (B[2], B[3], B[6][:, P:2 * P])[i][:, 0:n * P], ALU.subtract)
                tt(flat(XIT[:, part, :]), flat(XIT[:, part, :]), (B[4], B[5], B[6][:, 2 * P:3 * P])[i][:, 0:n * P], ALU.subtract).then_inc(S("inv_step"), 1)
        dve.wait_ge(S("chunk_act"), 2)
        dve.wait_ge(S("state_first"), 1)
        for i in range(NT):
            dve.wait_ge(S("step_psum"), 5 * i + 3)
            for h in range(DN_H):
                c = 4 * i + h
                last = stt(rhs[:, h, :], B[0][:, h * P:(h + 1) * P], NBE[:, c:c + 1], vb[:, c, :], ALU.mult, ALU.add)
            last.then_inc(S("rhs_made"), 1)
            if i < NT - 1:
                dve.wait_ge(S("step_psum"), 5 * i + 6)
                for h in range(DN_H):
                    c = 4 * i + h
                    last = stt(state[:, h, :], state[:, h, :], CD[:, c:c + 1], B[2][:, h * P:(h + 1) * P], ALU.mult, ALU.add)
                last.then_inc(S("state_out"), 1)
            dve.wait_ge(S("step_psum"), 4 * i + 7)
            dve.wait_ge(S("o_decayed"), i + 1)
            tt(flat(odec[i]), flat(odec[i]), B[7], ALU.add).then_inc(S("o_made"), 1)
        for i in range(NT):
            dve.wait_ge(S("o_rstd"), i + 1)
            for h in range(DN_H):
                zh = zs[:, i, h * P:(h + 1) * P]
                last = stt(zh, odec[i][:, h, :], rsd[:, 4 * i + h:4 * i + h + 1], zh, ALU.mult, ALU.mult)
            last.then_inc(S("o_normed"), 1)
        for g in range(4):
            hs = slice(2 * g, 2 * g + 2)
            dve.wait_ge(S("z_psum"), g + 1)
            nc.vector.tensor_copy(Z0[:, hs, P:SEQ], cube(B[g], 2)[:, :, P:SEQ])
            tt(Z0[:, hs, 0:P], cube(B[g], 2)[:, :, 0:P], masks("strict", 2), ALU.mult).then_inc(S("z_out"), 1)
        for g in range(2):
            dve.wait_ge(S("z_psum"), g + 5)
            tt(Z1[:, 4 * g:4 * g + 4, :], cube(B[4 + g], 4), masks("strict", 4), ALU.mult).then_inc(S("z_out"), 1)

        def gate(n):
            u, i = n // 2, n % 2
            cols = slice((u % 2) * 512, (u % 2 + 1) * 512)
            dve.wait_ge(S("proj"), GATE0 + n + 1)
            tt(gates[:, i, u // 2, cols], B[(GATE0 + n) % 4], params[:, 2 + u // 2, cols], ALU.add).then_inc(S("gate_out"), 1)

        dve.wait_ge(S("b_gate_in"), 16)
        for n in range(2):
            gate(n)
        dve.wait_ge(S("sp_ln"), 1)
        dve.wait_ge(S("z_out"), 6)
        stt(SP[0:META, 3072:5120], Z[0:META, 3072:5120], 0.0, SP[0:META, 3072:5120], ALU.max, ALU.add)
        stt(SP[:, 0:3072], Z[:, 0:3072], 0.0, SP[:, 0:3072], ALU.max, ALU.add).then_inc(S("sp_made"), 1)
        for n in range(2, 8):
            gate(n)
        for g in range(4):
            hs = slice(2 * g, 2 * g + 2)
            dve.wait_ge(S("later_psum"), g + 1)
            tt(Z0[:, hs, :], Z0[:, hs, :], cube(B[g], 2), ALU.subtract).then_inc(S("later_out"), 1)
        for g in range(2):
            dve.wait_ge(S("later_psum"), g + 5)
            hs = slice(4 * g, 4 * g + 4)
            tt(Z1[:, hs, :], Z1[:, hs, :], cube(B[4 + g], 4), ALU.subtract).then_inc(S("later_out"), 1)
        for g in range(4):
            hs = slice(2 * g, 2 * g + 2)
            dve.wait_ge(S("later_psum"), g + 7)
            tt(ZM[:, hs, :], ZM[:, hs, :], cube(B[(6, 7, 0, 1)[g]][0:META, :], 2), ALU.subtract).then_inc(S("later_out"), 1)
        for i in range(NT):
            dve.wait_ge(S("mix_psum"), i + 3)
            nc.vector.tensor_copy(osb[:, i, :], B[2 + i]).then_inc(S("sb_out"), 1)
        dve.wait_ge(S("gate_sig"), 8)
        for n in range(8):
            br, i, half = n // 4, (n // 2) % 2, n % 2
            g_ = gates[:, i, br, half * 512:(half + 1) * 512]
            dve.wait_ge(S("branch"), n + 1)
            tt(g_, g_, B[n % 4], ALU.mult).then_inc(S("branch_out"), 1)
        for i in range(NT):
            dve.wait_ge(S("branch_out"), 6 + 2 * i)
            tt(gates[:, i, 0, :], gates[:, i, 0, :], gates[:, i, 1, :], ALU.add).then_inc(S("merged"), 1)
        xT_copies(1, SEQ)
        for n in range(4):
            half, i = n // 2, n % 2
            x = X0[:, i, half * 512:(half + 1) * 512]
            dve.wait_ge(S("mixed"), n + 1)
            stt(x, x, ALPHA, B[n], ALU.mult, ALU.add).then_inc(S("mixed_out"), 1)
        b3 = lambda a, n: a.unsqueeze(2).broadcast_to([P, 2, n])
        b2 = lambda name, n: C(name).unsqueeze(1).broadcast_to([P, 2, n])
        red = nc.vector.tensor_reduce
        n_rstd = [3]

        def norm_pair(src, dst, g, b, ready, out_sem):
            for i in range(NT):
                moments(1 + i, src[:, i, :], P)
            dve.wait_ge(S(ready), 32)
            for i in range(NT):
                centered(src[:, i, :], dst[:, i, :], 1 + i, P, g, n_rstd[0] + i + 1)
            for i in range(NT):
                n_rstd[0] += 1
                dve.wait_ge(S("rstd"), n_rstd[0])
                scaled(dst[:, i, :], 1 + i, P, b).then_inc(S(out_sem), 1)

        dve.wait_ge(S("mixed_out"), 4)
        norm_pair(X0, X1, 0, 1, "ln1_in", "h1_made")
        xT_copies(2, SEQ)
        dve.wait_ge(S("h1_made"), 2)
        for i in range(NT):
            ts(X0[:, i, :], X1[:, i, :], ALPHA, None, ALU.mult)
        dve.wait_ge(S("router_in"), 16 * (NG + 3))
        dve.wait_ge(S("router_psum"), 1)
        line(tt(lg, B[0][:, 0:128].rearrange("p (t n) -> p t n", t=2)[:, :, 0:36], rbias.unsqueeze(1).broadcast_to([P, 2, 36]), ALU.add))
        line(red(mx, gl, AX.X, ALU.max))
        line(tt(gd, gl, b3(mx, NG), ALU.subtract))
        line(ts(g4, gd, 0.0, None, ALU.is_equal))
        dve.nop().then_inc(S("router_dve"), 1)
        line(tt(g4, g4, b2("desc4", NG), ALU.mult))
        line(red(gs, g4, AX.X, ALU.max))
        tt(oh, g4, b3(gs, NG), ALU.is_equal).then_inc(S("router_dve"), 1)
        dve.wait_ge(S("router_dve"), 2)
        line(tt(g4, oh, b2("idx4", NG), ALU.mult))
        line(red(gid, g4, AX.X, ALU.add))
        dve.wait_ge(S("router_act"), 1)
        line(red(gs, gd, AX.X, ALU.add))
        line(nc.vector.reciprocal(gp, gs))
        for i in range(NT):
            last = tt(picked[:, i], exl[:, i], oh[:, i, :].unsqueeze(2).broadcast_to([P, NG, NE]), ALU.mult)
        line(last)
        line(red(sl, picked.rearrange("p t g e -> p t e g"), AX.X, ALU.add))

        def largest(vals, top, one_hot):
            line(red(top, vals, AX.X, ALU.max))
            line(tt(e8, vals, b3(top, NE), ALU.is_equal))
            line(tt(e8, e8, b2("desc8", NE), ALU.mult))
            line(red(gs, e8, AX.X, ALU.max))
            line(tt(one_hot, e8, b3(gs, NE), ALU.is_equal))

        largest(sl, top1, oh1)
        line(stt(sl2, oh1, NEG, sl, ALU.mult, ALU.add))
        largest(sl2, top2, oh2)
        tt(w2, top2, top1, ALU.subtract).then_inc(S("router_dve"), 1)
        dve.wait_ge(S("router_act"), 2)
        line(ts(w1, w2, 1.0, None, ALU.add))
        line(nc.vector.reciprocal(w1, w1))
        line(tt(w1, w1, gp, ALU.mult))
        line(tt(w2, w2, w1, ALU.mult))
        line(tt(oh1, oh1, b3(w1, NE), ALU.mult))
        line(tt(oh2, oh2, b3(w2, NE), ALU.mult))
        line(tt(cmb, oh1, oh2, ALU.add))
        dve.wait_ge(S("router_psum"), 2)
        nc.vector.tensor_copy(rk, B[1][:, 0:3 * NG]).then_inc(S("scat_out"), 1)
        dve.wait_ge(S("scat_out"), 1)
        line(tt(g4, oh, cube(rk[:, 0:2 * NG], 2), ALU.mult))
        line(red(rank, g4, AX.X, ALU.add))
        line(ts(over, rank, float(P), None, ALU.is_ge))
        line(stt(pos, gid, float(P), rank, ALU.mult, ALU.add))
        line(ts(gid, gid, -float(P), 3.0 * P, ALU.mult, ALU.add))
        line(tt(gid, gid, over, ALU.mult))
        line(tt(pos, pos, gid, ALU.add))
        line(ts(ct, rk[:, 2 * NG:3 * NG], float(P), None, ALU.is_gt))
        line(red(ovf[:, 0:1], ct, AX.X, ALU.add))
        line(tt(ct, ct, C("idx4"), ALU.mult))
        line(red(ovf[:, 1:2], ct, AX.X, ALU.add))
        nc.vector.tensor_copy(ovi[:, :], ovf).then_inc(S("over_made"), 1)

        def select(s_):
            for i in range(NT):
                last = ts(sel[:, i, :], C("iota"), pos[:, i:i + 1], None, ALU.is_equal)
            last.then_inc(S("sel_made"), 1)
            dve.wait_ge(S("sel_made"), s_ + 1)
            ts(pos, pos, -float(P), None, ALU.add).then_inc(S("pos_made"), 1)

        def weights(s_):
            dve.wait_ge(S("sel_psum"), s_ + 1)
            nc.vector.tensor_copy(comb, B[7][:, 0:NE]).then_inc(S("comb_out"), 1)

        def selection(s_):
            nc.vector.tensor_copy(selT, B[7][:, P:3 * P]).then_inc(S("selT_out"), 1)

        def gu_low(s_, e):
            u = gu_slot(e)
            for i in range(2):
                half = slice(i * HALF_U, (i + 1) * HALF_U)
                dve.wait_ge(S("gu_hi"), s_ * 2 * NE + (2 * e + i + 1))
                tt(wlo[:, u, half], ring[:, u, half], f32(ehi[:, e % E_BUF, half]), ALU.subtract).then_inc(S("gu_lo"), 1)

        def xs_low(s_):
            dve.wait_ge(S("xs_round"), s_ + 1)
            tt(flat(xsL[:, 0:4, :]), B[5], f32(flat(xsH[:, 0:4, :])), ALU.subtract)
            tt(flat(xsL[:, 4:8, :]), B[6], f32(flat(xsH[:, 4:8, :])), ALU.subtract).then_inc(S("xs_out"), 1)

        def experts(s_, over_=False, more=True):
            dve.wait_ge(S("comb_out"), s_ + 1)
            for e in range(NE):
                dve.wait_ge(S("sg_made"), s_ * NE + (e + 1))
                if e >= 2:
                    dve.wait_ge(S("hT_psum"), s_ * NE + (e - 1))
                stt(hid[:, e % 2, :], sg[:, e % 2, :], comb[:, e:e + 1], B[e % 2][:, FF:2 * FF], ALU.mult, ALU.mult).then_inc(S("hid"), 1)
                if e < NE - 2:
                    gu_low(s_, e + 2)
                elif more:
                    gu_low(s_ + 1, e + 2 - NE)
                if e == 4 and not over_:
                    dve.wait_ge(S("sel_psum"), s_ + 1)
                    dve.wait_ge(S("pos_made"), s_ + 1)
                    select(s_ + 1)
            if not over_:
                dve.wait_ge(S("hid"), s_ * NE + NE)
                weights(s_ + 1)
                xs_low(s_ + 1)
            dve.wait_ge(S("down"), s_ * NE + NE)
            nc.vector.tensor_copy(ysb[:, 0:512], B[2]).then_inc(S("y_dve"), 1)
            for q in range(4):
                x_ = X0[:, q // 2, (q % 2) * 512:(q % 2 + 1) * 512]
                dve.wait_ge(S("scat"), s_ * 4 + (q + 1))
                tt(x_, x_, B[q % 2], ALU.add).then_inc(S("scat_out"), 1)
            if not over_:
                selection(s_ + 1)

        select(0)
        for e in range(2):
            gu_low(0, e)
        weights(0)
        selection(0)
        xs_low(0)
        with dve.Fori(0, NG - 1) as s_:
            experts(s_)
        experts(NG - 1, more=False)
        dve.wait_ge(S("over_made"), 1)
        flag = dve.value_load(ovi[0:1, 0:1], min_val=0, max_val=1)
        with dve.If(flag):
            for e in range(2):
                gu_low(NG, e)
            experts(NG, True, more=False)
            dve.wait_ge(S("scat_out"), 4 * (NG + 1) + 1)
        dve.wait_ge(S("scat_out"), 4 * NG + 1)
        norm_pair(X0, X0, 2, 3, "ln2_in", "h2_made")
        def rms_norm(r, param):
            for i in range(NT):
                dve.wait_ge(S("rms"), r + 1)
                if i == 0:
                    dve.wait_ge(S(("rms01_in", "rms01_in", "rms23_in", "rms23_in", "rms4_in")[r]), 32 if r < 4 else 16)
                stt(X1[:, i, :], X0[:, i, :], rsd[:, i:i + 1], params[:, param, :], ALU.mult, ALU.mult).then_inc(S("xn_made"), 1)

        dve.wait_ge(S("pos_in"), 32)
        line(nc.vector.tensor_copy(posf, posi[:, :]))
        for i in range(NT):
            last = ts(ang[:, i, :], C("freq"), posf[:, i:i + 1], None, ALU.mult)
        line(last)
        for out, quarter in ((sine, 0.0), (cosine, 0.25)):
            line(ts(turn, ang, 1.0 / (2 * math.pi), quarter, ALU.mult, ALU.add))
            line(ts(turn, turn, ROUND, -ROUND, ALU.add, ALU.add))
            line(stt(out, turn, -TWO_PI[0], ang, ALU.mult, ALU.add))
            line(stt(out, turn, -TWO_PI[1], out, ALU.mult, ALU.add))
            line(stt(out, turn, -TWO_PI[2], out, ALU.mult, ALU.add))
            if quarter:
                line(ts(out, out, math.pi / 2, None, ALU.add))
            line(ts(out, out, 3.1415925, -3.1415925, ALU.min, ALU.max))
        dve.nop().then_inc(S("turned"), 1)
        def xT_parts(call):
            for k in range(KD):
                if k % 2:
                    dve.wait_ge(S("xT_psum"), KD * call + k + 1)
                    nc.vector.tensor_copy(xTH[:, k, 0:SEQ], B[7][:, 0:SEQ]).then_inc(S("xT_dve"), 1)
                dve.wait_ge(S("xT_dve" if k % 2 else "xT_act"), (KD // 2) * call + k // 2 + 1)
                tt(xTL[:, k, :], B[6 + k % 2][:, 0:SEQ], f32(xTH[:, k, 0:SEQ]), ALU.subtract).then_inc(S("xT_split"), 1)

        def lo_halves(u, n, hi_count):
            for i in range(2):
                half = slice(i * HALF_U, (i + 1) * HALF_U)
                dve.wait_ge(S("split_hi"), hi_count + (i + 1))
                tt(wlo[:, u % SLOTS, half], slot(u)[:, half], f32(whi[:, n % 2, half]), ALU.subtract).then_inc(S("split_lo"), 1)

        rms_norm(0, 0)
        xT_parts(3)
        for u in range(2, 6):
            lo_halves(U_TWO + u, u, 2 * u)
        dve.wait_ge(S("sines"), 1)
        for i in range(NT):
            dve.wait_ge(S("qkv_out"), 7 + i)
            heads = qk[:, i, :].rearrange("p (h d) -> p h d", d=AT_D)
            x1, x2 = heads[:, :, 0:HALF], heads[:, :, HALF:ROT]
            cb, sb_ = [a[:, i, :].unsqueeze(1).broadcast_to([P, 16, HALF]) for a in (cosine, sine)]
            a, b, c, d = rope_t
            for o_, p_, q_ in ((a, x1, cb), (b, x2, sb_), (c, x2, cb), (d, x1, sb_)):
                last = tt(o_, p_, q_, ALU.mult)
            line(last)
            line(tt(x1, a, b, ALU.subtract))
            tt(x2, c, d, ALU.add).then_inc(S("rope_made"), 1)
            dve.wait_ge(S("rope_made"), i + 1)
        for g in range(1, 8, 2):
            dve.wait_ge(S("att_psum"), g + 1)
            nc.vector.tensor_copy(flat(qkT[:, 2 * g:2 * g + 2, :]), B[4 + g % 4]).then_inc(S("qkT_dve"), 1)
        dve.wait_ge(S("causal_made"), 1)
        for h in range(AT_H):
            dve.wait_ge(S("att_psum"), h + 9)
            stt(sc_[:, h, :], B[h % 4][:, 0:3 * P], AT_D ** -0.5, causal, ALU.mult, ALU.add).then_inc(S("scores_out"), 1)
            if h % 4 == 3:
                hs = slice(h - 3, h + 1)
                dve.wait_ge(S("scores_out"), h + 1)
                red(mxs[:, 0, hs], sc_[:, hs, 0:P], AX.X, ALU.max)
                line(red(mxs[:, 1, hs], sc_[:, hs, P:3 * P], AX.X, ALU.max))
                ts(mxs[:, :, hs], mxs[:, :, hs], -1.0, None, ALU.mult).then_inc(S("max_made"), 1)
        for h in range(AT_H):
            dve.wait_ge(S("att_psum"), h + 17)
            nc.vector.tensor_copy(pT[:, h, :], B[4 + h % 4][:, 0:3 * P]).then_inc(S("pT_out"), 1)
        dve.wait_ge(S("p_made"), 8)
        line(nc.vector.reciprocal(sums, sums))
        for i in range(NT):
            for hh in range(2):
                dve.wait_ge(S("att_psum"), 24 + (4 if hh == 0 and i == 0 else 8))
                rec = sums[:, i, 4 * hh:4 * hh + 4].unsqueeze(2).broadcast_to([P, 4, P])
                last = tt(cube(qk[:, i, hh * 512:(hh + 1) * 512], 4), cube(B[2 * i + hh], 4), rec, ALU.mult)
            last.then_inc(S("att_made"), 1)
        def split_lo(m, q, jj=0):
            lo_halves(mlp_base[m] + q, q, jj * 8 + (12 + 2 * (16 * m + q)))

        xT_copies(4, SEQ)
        for q in range(2):
            split_lo(0, q)
        for n in range(4):
            half, i = n // 2, n % 2
            x = X0[:, i, half * 512:(half + 1) * 512]
            dve.wait_ge(S("att_o"), n + 1)
            ins = tt(x, x, B[n], ALU.add)
            if half:
                ins.then_inc(S("res"), 1)

        def mlp(m):
            xT_parts(5 + 2 * m)

            def square(j, jj=0, wait=True):
                for pr in range(2):
                    hs = slice(2 * pr, 2 * pr + 2)
                    r_ = cube(relu_t[:, pr, :], 2)
                    dve.wait_ge(S("relu"), jj * 4 + (16 * m + 2 * j + pr + 1))
                    steps = jj * 8 + 2 * (16 * m + 2 * j + pr)
                    tt(r_, r_, r_, ALU.mult).then_inc(S("square_steps"), 1)
                    dve.wait_ge(S("square_steps"), steps + 1)
                    if wait and pr == 0:
                        dve.wait_ge(S("mlp_down"), jj * 2 + (11 * m + j - 1))
                    nc.vector.tensor_copy(hidH[:, j % 2, hs, :], r_).then_inc(S("square_steps"), 1)
                    dve.wait_ge(S("square_steps"), steps + 2)
                    tt(hidL[:, j % 2, hs, :], r_, f32(hidH[:, j % 2, hs, :]), ALU.subtract).then_inc(S("squared"), 1)

            square(0, wait=False)
            split_lo(m, 2)
            square(1, wait=False)
            split_lo(m, 3)
            with dve.Fori(0, 3) as jj:
                split_lo(m, 4, jj)
                square(2, jj)
                split_lo(m, 5, jj)
                split_lo(m, 6, jj)
                square(3, jj)
                split_lo(m, 7, jj)
            for n in range(4):
                dve.wait_ge(S("mlp_down"), 11 * m + 8 + n)
                x = X0[:, n // 2, (n % 2) * 512:(n % 2 + 1) * 512]
                ins = tt(x, x, B[n], ALU.add)
                if n % 2:
                    ins.then_inc(S("res"), 1)

        rms_norm(1, 1)
        mlp(0)
        rms_norm(2, 2)
        xT_copies(6, SEQ)
        dve.wait_ge(S("scale_in"), 16)
        for n in range(4):
            i, cols = n // 2, slice((n % 2) * 512, (n % 2 + 1) * 512)
            dve.wait_ge(S("pooled"), n + 1)
            line(tt(X1[:, i, cols], B[n], params[:, 0, cols], ALU.mult))
            ins = tt(X0[:, i, cols], X0[:, i, cols], X1[:, i, cols], ALU.add)
            if n % 2:
                ins.then_inc(S("res"), 1)
        for q in range(2):
            split_lo(1, q)
        rms_norm(3, 3)
        mlp(1)
        rms_norm(4, 1)

    block_cm.__exit__(None, None, None)


_INS = ['x', 'meta_tokens', 'ln_emb_g', 'ln_emb_b', 'w_in', 'b_gate', 'dn_conv_w', 'dn_a_log', 'dn_dt_bias', 'dn_norm_g',
        'w_branch_dn', 'w_branch_sb', 'w_out', 'ln1_g', 'ln1_b', 'router_group_w', 'router_group_b', 'router_expert_w',
        'router_expert_b', 'expert_w_gate', 'expert_w_up', 'expert_w_down', 'ln2_g', 'ln2_b', 'positions_2', 'norm_mix_2',
        'norm_mlp_2', 'attn_w_qkv_2', 'attn_w_o_2', 'pool_w_2', 'pool_scale_2', 'mlp_w_up_2', 'mlp_w_down_2', 'norm_final_2']


def kernel(**inputs):
    import concourse.bacc as bacc
    from concourse.bass_utils import run_bass_kernel_spmd

    nc = bacc.Bacc("TRN2", target_bir_lowering=False, num_devices=1)
    arrays, args = {}, {}
    consts, bands = shape_constants()
    for name, a in [(n, inputs[n]) for n in _INS] + [("consts", consts), ("bands", bands)]:
        a = np.ascontiguousarray(a)
        arrays[f"in_{name}"] = a
        args[name] = nc.dram_tensor(f"in_{name}", a.shape, mybir.dt.from_np(a.dtype), kind="ExternalInput").ap()
    args["out"] = nc.dram_tensor("out_y", (1, SEQ, D), F32, kind="ExternalOutput").ap()
    build(nc, args)
    result = run_bass_kernel_spmd(nc, [arrays], core_ids=[0])
    return result.results[0]["out_y"]
```
